# Optimizing a Trainium2 kernel written in Bass

```python
import jax, jax.numpy as jnp
from jax import lax
import numpy as np

D_MODEL = 1024
BATCH = 1
SEQ = 256
DEPTH = 1
DEC_BATCH = 1
DEC_SEQ = 2048
PAST_LEN = 256

GRID_W = 64
N_HEADS_A = 8
HEAD_DIM = 64
W_A = N_HEADS_A * HEAD_DIM
W_B = 512
CONV_K = 31
CONV_PAD = CONV_K // 2
WIN_R_MAX = 8
WIN_C = 16
EPS = 1e-6
PROJ_SPLITS = (W_A, 2 * W_A, 3 * W_A, 4 * W_A, 4 * W_A + 2 * W_B, 4 * W_A + 3 * W_B)
D_IN = 4 * W_A + 3 * W_B + 2 * D_MODEL

kernel_name = "gated_natten_conformer_prefix_diffusion"

def rmsnorm(x, g):
    xf = x.astype(jnp.float32)
    y = xf * lax.rsqrt(jnp.mean(xf * xf, axis=-1, keepdims=True) + EPS)
    return (y * g.astype(jnp.float32)).astype(x.dtype)

def layernorm(x, g, b):
    xf = x.astype(jnp.float32)
    mu = jnp.mean(xf, axis=-1, keepdims=True)
    var = jnp.mean(jnp.square(xf - mu), axis=-1, keepdims=True)
    y = (xf - mu) * lax.rsqrt(var + EPS)
    return (y * g.astype(jnp.float32) + b.astype(jnp.float32)).astype(x.dtype)

def context_attention(q, k, v):
    s = jnp.einsum('bqhd,bkhd->bhqk', q, k).astype(jnp.float32) * (HEAD_DIM ** -0.5)
    p = jax.nn.softmax(s, axis=-1).astype(v.dtype)
    o = jnp.einsum('bhqk,bkhd->bqhd', p, v)
    return o.reshape(q.shape[0], q.shape[1], W_A)

def neighbourhood_attention(q, k, v, ck, cv, table):
    B, L, H, Dh = q.shape
    rows = L // GRID_W
    wr = min(WIN_R_MAX, rows)
    r = jnp.arange(rows)
    r0 = jnp.clip(r - wr // 2, 0, rows - wr)
    band = r0[:, None] + jnp.arange(wr)[None, :]
    cq = jnp.arange(GRID_W)
    c0 = jnp.clip(cq - WIN_C // 2, 0, GRID_W - WIN_C)
    col_ok = (cq[None, :] >= c0[:, None]) & (cq[None, :] < c0[:, None] + WIN_C)
    dr = band - r[:, None] + (WIN_R_MAX - 1)
    dc = jnp.clip(cq[None, :] - cq[:, None] + (WIN_C - 1), 0, 2 * WIN_C - 2)
    bias = table[:, dr[:, None, :, None], dc[None, :, None, :]]
    qg = q.reshape(B, rows, GRID_W, H, Dh)
    kb = k.reshape(B, rows, GRID_W, H, Dh)[:, band]
    vb = v.reshape(B, rows, GRID_W, H, Dh)[:, band]
    scale = Dh ** -0.5
    s_win = jnp.einsum('brchd,brkwhd->bhrckw', qg, kb).astype(jnp.float32) * scale
    s_win = s_win + bias.astype(jnp.float32)[None]
    s_win = jnp.where(col_ok[:, None, :], s_win, -jnp.inf)
    s_win = s_win.reshape(B, H, rows, GRID_W, wr * GRID_W)
    s_ctx = jnp.einsum('brchd,bshd->bhrcs', qg, ck).astype(jnp.float32) * scale
    p = jax.nn.softmax(jnp.concatenate([s_win, s_ctx], axis=-1), axis=-1).astype(v.dtype)
    p_win = p[..., :wr * GRID_W].reshape(B, H, rows, GRID_W, wr, GRID_W)
    p_ctx = p[..., wr * GRID_W:]
    o = jnp.einsum('bhrckw,brkwhd->brchd', p_win, vb) + jnp.einsum('bhrcs,bshd->brchd', p_ctx, cv)
    return o.reshape(B, L, H * Dh)

def conv_branch(glu, dw_w, dw_b, ln_g, ln_b):
    a, b = jnp.split(glu, 2, axis=-1)
    u = a * jax.nn.sigmoid(b)
    u = lax.conv_general_dilated(u, dw_w[:, None, :], window_strides=(1,),
                                 padding=[(CONV_PAD, CONV_PAD)],
                                 dimension_numbers=('NWC', 'WIO', 'NWC'),
                                 feature_group_count=W_B) + dw_b
    return jax.nn.silu(layernorm(u, ln_g, ln_b))

def mixer_layer(x, mod, rms_g, w_in, b_in, dw_w, dw_b, ln_g, ln_b, w_proj_a, w_proj_b, w_out, attend):
    shift, scale, gate = jnp.split(mod, 3, axis=-1)
    h = rmsnorm(x, rms_g) * (1 + scale) + shift
    q, k, v, z_a, glu, z_b, gates = jnp.split(h @ w_in + b_in, PROJ_SPLITS, axis=-1)
    B, L, _ = x.shape
    q = q.reshape(B, L, N_HEADS_A, HEAD_DIM)
    k = k.reshape(B, L, N_HEADS_A, HEAD_DIM)
    v = v.reshape(B, L, N_HEADS_A, HEAD_DIM)
    y_a = attend(q, k, v) * jax.nn.silu(z_a)
    y_b = conv_branch(glu, dw_w, dw_b, ln_g, ln_b) * jax.nn.silu(z_b)
    g_a, g_b = jnp.split(jax.nn.sigmoid(gates), 2, axis=-1)
    m = g_a * (y_a @ w_proj_a) + g_b * (y_b @ w_proj_b)
    return x + gate * (m @ w_out), k, v

def setup_inputs(seed: int = 0) -> dict:
    key = jax.random.key(seed)
    ks = jax.random.split(key, 20)
    n = jax.random.normal
    f32 = jnp.float32
    return {
        "x_prompt": n(ks[0], (BATCH, SEQ, D_MODEL), f32),
        "x_sample": n(ks[1], (DEC_BATCH, DEC_SEQ, D_MODEL), f32),
        "cache_k": n(ks[2], (DEC_BATCH, DEPTH, PAST_LEN, N_HEADS_A, HEAD_DIM), f32),
        "cache_v": n(ks[3], (DEC_BATCH, DEPTH, PAST_LEN, N_HEADS_A, HEAD_DIM), f32),
        "c": n(ks[4], (DEC_BATCH, D_MODEL), f32),
        "c_ctx": n(ks[5], (D_MODEL,), f32),
        "rms_g": 1.0 + 0.1 * n(ks[6], (DEPTH, D_MODEL), f32),
        "w_ada": 0.5 * D_MODEL ** -0.5 * n(ks[7], (DEPTH, D_MODEL, 3 * D_MODEL), f32),
        "b_ada": 0.01 * n(ks[8], (DEPTH, 3 * D_MODEL), f32),
        "w_in": D_MODEL ** -0.5 * n(ks[9], (DEPTH, D_MODEL, D_IN), f32),
        "b_in": 0.01 * n(ks[10], (DEPTH, D_IN), f32),
        "rel_bias": 0.1 * n(ks[11], (DEPTH, N_HEADS_A, 2 * WIN_R_MAX - 1, 2 * WIN_C - 1), f32),
        "dw_w": CONV_K ** -0.5 * n(ks[12], (DEPTH, CONV_K, W_B), f32),
        "dw_b": 0.01 * n(ks[13], (DEPTH, W_B), f32),
        "ln_g": 1.0 + 0.1 * n(ks[14], (DEPTH, W_B), f32),
        "ln_b": 0.01 * n(ks[15], (DEPTH, W_B), f32),
        "w_proj_a": W_A ** -0.5 * n(ks[16], (DEPTH, W_A, D_MODEL), f32),
        "w_proj_b": W_B ** -0.5 * n(ks[17], (DEPTH, W_B, D_MODEL), f32),
        "w_out": D_MODEL ** -0.5 * n(ks[18], (DEPTH, D_MODEL, D_MODEL), f32),
        "final_g": 1.0 + 0.1 * n(ks[19], (D_MODEL,), f32),
    }

def reference(x_prompt, x_sample, cache_k, cache_v, c, c_ctx, rms_g, w_ada, b_ada, w_in, b_in,
              rel_bias, dw_w, dw_b, ln_g, ln_b, w_proj_a, w_proj_b, w_out, final_g):
    x = x_prompt
    ks, vs = [], []
    for l in range(DEPTH):
        mod_ctx = jax.nn.silu(c_ctx) @ w_ada[l] + b_ada[l]
        x, k, v = mixer_layer(x, mod_ctx, rms_g[l], w_in[l], b_in[l], dw_w[l], dw_b[l], ln_g[l], ln_b[l],
                              w_proj_a[l], w_proj_b[l], w_out[l], context_attention)
        ks.append(k)
        vs.append(v)
    y_prompt = rmsnorm(x, final_g)
    state_k = jnp.stack(ks, axis=1)
    state_v = jnp.stack(vs, axis=1)

    z = x_sample
    for l in range(DEPTH):
        mod_lat = (jax.nn.silu(c) @ w_ada[l] + b_ada[l])[:, None, :]
        attend = lambda q, k, v, l=l: neighbourhood_attention(q, k, v, cache_k[:, l], cache_v[:, l], rel_bias[l])
        z, _, _ = mixer_layer(z, mod_lat, rms_g[l], w_in[l], b_in[l], dw_w[l], dw_b[l], ln_g[l], ln_b[l],
                              w_proj_a[l], w_proj_b[l], w_out[l], attend)
    y_sample = rmsnorm(z, final_g)
    return (y_prompt, y_sample, state_k, state_v)


_drawn_inputs = setup_inputs


def setup_inputs(seed=0):
    import zlib

    import numpy as np

    out = dict(_drawn_inputs(seed))
    spreads = {}
    factors = {'cache_k': 8.0,
     'cache_v': 7.398,
     'b_ada': 4.474,
     'b_in': 6.309,
     'rel_bias': 64.0,
     'dw_b': 8.0,
     'ln_g': 7.644,
     'ln_b': 64.0}
    for name, (base, spread) in spreads.items():
        noise = np.random.default_rng([zlib.crc32(name.encode()), seed]).standard_normal(out[name].shape)
        drawn = base * np.exp(spread * noise) if base else spread * noise
        out[name] = __import__('jax').numpy.asarray(drawn.astype(out[name].dtype))
    for name, factor in factors.items():
        out[name] = (out[name] * factor).astype(out[name].dtype)
    return out
```

```python
from contextlib import ExitStack

import numpy as np

import concourse.bass as bass
from concourse import mybir

F32 = mybir.dt.float32
F32R = mybir.dt.float32r
ALU = mybir.AluOpType
ACT = mybir.ActivationFunctionType
AX_X = mybir.AxisListType.X
ds = bass.ds

P = 128
D = 1024
KC = D // P
LAT, CTX = 2048, 256
TOK = LAT + CTX
HEADS, DH = 8, 64
WA = WB = 512
TAPS, PAD = 31, 15
GRID, ROWS = 64, 32
WIN_R, WIN_C = 8, 16
EPS = 1e-6
Q0, K0, V0, ZA0 = 0, WA, 2 * WA, 3 * WA
GA0 = 4 * WA
GB0 = GA0 + WB
ZB0 = 4 * WA + 2 * WB
G0 = 4 * WA + 3 * WB
D_IN = G0 + 2 * D

GROUP_A = [(0, 512, 0), (512, 512, 512), (1024, CTX, LAT)]
GROUP_B = [(0, 512, 1024), (512, 512, 1536)]
HT_W = 1280
IS_CTX = LAT

R_BIN, R_DWB, R_LNG, R_LNB, R_RMS, R_BADA, R_C = 0, 44, 48, 52, 56, 64, 88
R_END = R_C + 2 * KC

SECTIONS = [
    ("glu", GA0, GB0, P, 4),
    ("value", V0, V0 + P, 2 * P, 2),
    ("qk", Q0, K0, P, 4),
    ("z", ZA0, ZB0, P, 4),
    ("gates", G0, G0 + D, P, 8),
]
TURNS = sum(s[4] for s in SECTIONS)
CREDIT = 16


def rms_scale(pool, src, out, eps_tmp, minus_half, done, n):
    pool.tensor_scalar(eps_tmp, src, 1.0 / D, EPS, ALU.mult, ALU.add).then_inc(done, 1)
    pool.wait_ge(done, n + 1)
    pool.tensor_tensor(out, eps_tmp, minus_half, ALU.pow).then_inc(done, 1)


def wait_reg(eng, sem, value):
    eng.wait_ge(sem, value)
    eng.nop(nofuse=True)


def modulation(nc, io, cst, hT_hi, hT_lo):
    with ExitStack() as ctx:
        sb = lambda n, s, d=F32: ctx.enter_context(nc.sbuf_tensor(n, s, d))
        sem = lambda n: ctx.enter_context(nc.semaphore(n))
        rows = sb("param_rows", [P, P])
        taps = sb("tap_rows", [P, P])
        silu_c = sb("silu_c", [P, 2 * KC])
        wada = sb("wada", [P, 3, KC, 256])
        xn = sb("xn_a", [P, 10, D])
        square = sb("square", [P, D])
        ssum = sb("ssum", [P, 10])
        tmp = sb("rms_tmp", [P, 10])
        rstd = sb("rstd", [P, 10])
        half = sb("minus_half", [P, 10])
        scale1 = sb("scale1", [P, KC, 2])
        hf = sb("h_f32", [P, 3, 512])
        psT = ctx.enter_context(nc.psum_tensor("psT", [P, 2, 512], F32))
        psM = ctx.enter_context(nc.psum_tensor("psM", [P, 2, 512], F32))
        psX = ctx.enter_context(nc.psum_tensor("psX", [P, 3, 512], F32))
        ident_in = sem("ident_in")
        rows_in, x_in, ada_in = sem("rows_in"), [sem(f"x_in{i}") for i in range(5)], [sem(f"ada_in{i}") for i in range(3)]
        turned, cols_out, silu_done = sem("turned"), sem("cols_out"), sem("silu_done")
        ada_mm, ada_out, sq_done, rms_done, xn_done = sem("ada_mm"), sem("ada_out"), sem("sq_done"), sem("rms_done"), sem("xn_done")
        half_set, mod_done, tr_done, hf_done, hi_done, lo_dve, lo_pool = (
            sem("half_set"), sem("mod_done"), sem("tr_done"), sem("hf_done"), sem("hi_done"), sem("lo_dve"), sem("lo_pool"))
        units = [(c, k) for c in range(3) for k in range(KC)]
        block = ctx.enter_context(nc.Block())

        @block.sync
        def _(sp):
            sp.dma_start(cst.ident[:], io.ident).then_inc(ident_in, 16)
            for r, a, n in ((R_BIN, io.b_in, 44), (R_DWB, io.dw_b, 4), (R_LNG, io.ln_g, 4), (R_LNB, io.ln_b, 4),
                            (R_RMS, io.rms_g, 8), (R_BADA, io.b_ada, 24), (R_C, io.c_ctx, 8), (R_C + KC, io.c, 8)):
                sp.dma_start(rows[r:r + n, :], a.rearrange("(r p) -> r p", p=P)).then_inc(rows_in, 16)
            sp.dma_start(taps[0:4 * TAPS, :], io.dw_w.rearrange("k (b p) -> (k b) p", p=P)).then_inc(rows_in, 16)
            for j in range(12):
                if j >= 3:
                    sp.wait_ge(ada_mm, 2 * (j - 2))
                sp.dma_start(wada[:, j % 3], io.w_ada[:, 256 * j:256 * j + 256]
                             .rearrange("(c p) n -> p c n", p=P)).then_inc(ada_in[j % 3], 16)

        @block.gpsimd
        def _(pool):
            pool.memset(half[:], -0.5).then_inc(half_set, 1)
            pool.wait_ge(half_set, 1)
            pool.wait_ge(sq_done, 10)
            rms_scale(pool, ssum[:], rstd[:], tmp[:], half[:], rms_done, 0)
            for n, (c, k) in enumerate(units):
                if n % 2:
                    pool.wait_ge(hi_done, n + 1)
                    w, at = GROUP_A[c][1], GROUP_A[c][0]
                    pool.tensor_tensor(hT_lo[:, k, at:at + w], hf[:, n % 3, 0:w],
                                       hT_hi[:, k, at:at + w].bitcast(F32), ALU.subtract).then_inc(lo_pool, 1)

        @block.scalar
        def _(act):
            for t in range(10):
                src = io.x_sample[P * t:P * t + P] if t < 8 else io.x_prompt[P * (t - 8):P * (t - 7)]
                act.dma_start(xn[:, t], src).then_inc(x_in[t // 2], 16)
            act.wait_ge(turned, 1)
            act.activation(silu_c[:], psT[:, 0, R_C:R_END], ACT.Silu).then_inc(silu_done, 1)
            for t in range(10):
                act.wait_ge(x_in[t // 2], 32)
                if t:
                    act.wait_ge(sq_done, t)
                act.activation(square[:], xn[:, t], ACT.Square, accum_out=ssum[:, t:t + 1]).then_inc(sq_done, 1)
            for n, (c, k) in enumerate(units):
                w, g = GROUP_A[c][1], 0 if c == 2 else 1
                if n == 0:
                    act.wait_ge(mod_done, 2)
                act.wait_ge(tr_done, n + 1)
                if n >= 3:
                    act.wait_ge(lo_pool if n % 2 == 0 else lo_dve, (n - 3) // 2 + 1)
                act.activation(hf[:, n % 3, 0:w], psX[:, n % 3, 0:w], ACT.Identity,
                               bias=cst.shift[:, k, g:g + 1], scale=cst.scale[:, k, g:g + 1]).then_inc(hf_done, 1)

        @block.vector
        def _(dve):
            dve.wait_ge(turned, 1)
            dve.wait_ge(silu_done, 1)
            dve.tensor_copy(cst.cols[:, 0:R_C], psT[:, 0, 0:R_C]).then_inc(cols_out, 1)
            dve.wait_ge(turned, 2)
            dve.tensor_copy(cst.taps[:], psT[:, 1, 0:4 * TAPS]).then_inc(cols_out, 1)
            dve.wait_ge(cols_out, 2)
            dve.tensor_scalar(cst.qbias[:], cst.cols[:, 0:4], DH ** -0.5, None, ALU.mult)
            for b in range(24):
                dst = (cst.shift, scale1, cst.gate)[b // 8]
                dve.wait_ge(ada_mm, b + 1)
                dve.tensor_scalar(dst[:, b % 8, :], psM[:, b % 2, 0:2], cst.cols[:, R_BADA + b:R_BADA + b + 1],
                                  None, ALU.add).then_inc(ada_out, 1)
                if b == 15:
                    dve.wait_ge(ada_out, 16)
                    for g in range(2):
                        dve.scalar_tensor_tensor(cst.scale[:, :, g], scale1[:, :, g], 1.0,
                                                 cst.cols[:, R_RMS:R_RMS + KC], ALU.add, ALU.mult).then_inc(mod_done, 1)
            dve.wait_ge(rms_done, 2)
            for t in range(10):
                dve.tensor_scalar(xn[:, t], xn[:, t], rstd[:, t:t + 1], None, ALU.mult).then_inc(xn_done, 1)
            for n, (c, k) in enumerate(units):
                w, at = GROUP_A[c][1], GROUP_A[c][0]
                dve.wait_ge(hf_done, n + 1)
                dve.tensor_copy(hT_hi[:, k, at:at + w], hf[:, n % 3, 0:w]).then_inc(hi_done, 1)
                if n % 2 == 0:
                    dve.wait_ge(hi_done, n + 1)
                    dve.tensor_tensor(hT_lo[:, k, at:at + w], hf[:, n % 3, 0:w],
                                      hT_hi[:, k, at:at + w].bitcast(F32), ALU.subtract).then_inc(lo_dve, 1)

        @block.tensor
        def _(pe):
            pe.wait_ge(ident_in, 16)
            pe.wait_ge(rows_in, 16 * 9)
            pe.transpose(psT[:, 0, 0:R_END], rows[0:R_END, :], cst.ident[0:R_END, 0:R_END]).then_inc(turned, 1)
            pe.transpose(psT[:, 1, 0:4 * TAPS], taps[0:4 * TAPS, :], cst.ident[0:4 * TAPS, 0:4 * TAPS]).then_inc(turned, 1)
            pe.wait_ge(silu_done, 1)
            sc = silu_c[:].rearrange("p (g k) -> p k g", g=2)
            for b in range(24):
                j = b // 2
                if b % 2 == 0:
                    pe.wait_ge(ada_in[j % 3], 16 * (j // 3 + 1))
                if b >= 2:
                    pe.wait_ge(ada_out, b - 1)
                for k in range(KC):
                    mm = pe.matmul(psM[:, b % 2, 0:2], wada[:, j % 3, k, P * (b % 2):P * (b % 2) + P], sc[:, k, :],
                                   start=(k == 0), stop=(k == KC - 1))
                mm.then_inc(ada_mm, 1)
            pe.wait_ge(xn_done, 10)
            for n, (c, k) in enumerate(units):
                if n >= 3:
                    pe.wait_ge(hf_done, n - 2)
                tiles = range(4 * c, 4 * c + GROUP_A[c][1] // P)
                for m, t in enumerate(tiles):
                    tr = pe.transpose(psX[:, n % 3, P * m:P * m + P], xn[:, t, P * k:P * k + P], cst.ident[:])
                tr.then_inc(tr_done, 1)


def turn_group_b(nc, cst, xn, hT_hi, hT_lo):
    with ExitStack() as ctx:
        sem = lambda n: ctx.enter_context(nc.semaphore(n))
        hf = ctx.enter_context(nc.sbuf_tensor("hb_f32", [P, 3, 512], F32))
        psX = ctx.enter_context(nc.psum_tensor("psXb", [P, 3, 512], F32))
        tr_done, hf_done, hi_done, lo_dve, lo_pool = (
            sem("b_tr_done"), sem("b_hf_done"), sem("b_hi_done"), sem("b_lo_dve"), sem("b_lo_pool"))
        units = [(c, k) for c in range(2) for k in range(KC)]
        block = ctx.enter_context(nc.Block())

        @block.tensor
        def _(pe):
            for n, (c, k) in enumerate(units):
                if n >= 3:
                    pe.wait_ge(hf_done, n - 2)
                for m in range(4):
                    tr = pe.transpose(psX[:, n % 3, P * m:P * m + P], xn[:, 4 * c + m, P * k:P * k + P], cst.ident[:])
                tr.then_inc(tr_done, 1)

        @block.scalar
        def _(act):
            for n, (c, k) in enumerate(units):
                act.wait_ge(tr_done, n + 1)
                if n >= 3:
                    act.wait_ge(lo_pool if n % 2 == 0 else lo_dve, (n - 3) // 2 + 1)
                act.activation(hf[:, n % 3], psX[:, n % 3], ACT.Identity, bias=cst.shift[:, k, 1:2],
                               scale=cst.scale[:, k, 1:2]).then_inc(hf_done, 1)

        @block.vector
        def _(dve):
            for n, (c, k) in enumerate(units):
                at = 512 * c
                dve.wait_ge(hf_done, n + 1)
                dve.tensor_copy(hT_hi[:, k, at:at + 512], hf[:, n % 3]).then_inc(hi_done, 1)
                if n % 2 == 0:
                    dve.wait_ge(hi_done, n + 1)
                    dve.tensor_tensor(hT_lo[:, k, at:at + 512], hf[:, n % 3],
                                      hT_hi[:, k, at:at + 512].bitcast(F32), ALU.subtract).then_inc(lo_dve, 1)

        @block.gpsimd
        def _(pool):
            for n, (c, k) in enumerate(units):
                if n % 2:
                    at = 512 * c
                    pool.wait_ge(hi_done, n + 1)
                    pool.tensor_tensor(hT_lo[:, k, at:at + 512], hf[:, n % 3],
                                       hT_hi[:, k, at:at + 512].bitcast(F32), ALU.subtract).then_inc(lo_pool, 1)


def project(nc, io, cst, hT_hi, hT_lo, group, g, xn=None):
    chunks = group
    nch = len(chunks)
    nU = 2 * nch
    ntile = sum(w for _, w, _ in chunks) // P
    half_tiles = ntile // 2
    first = g == 0
    with ExitStack() as ctx:
        sb = lambda n, s, d=F32: ctx.enter_context(nc.sbuf_tensor(f"{n}{g}", s, d))
        sem = lambda n: ctx.enter_context(nc.semaphore(f"{n}{g}"))
        wst = sb("w_stage", [P, 2, KC, P])
        w_hi, w_lo = sb("w_hi", [P, 4, KC, P], F32R), sb("w_lo", [P, 4, KC, P], F32R)
        ostg = sb("out_stage", [P, 4, P * ntile])
        vbias = sb("v_bias", [P, WA])
        ps = ctx.enter_context(nc.psum_tensor(f"psP{g}", [P, nU, 512], F32))
        if first:
            square = sb("square_b", [P, D])
            ssum, tmp, rstd, half = (sb(n, [P, 8]) for n in ("ssum_b", "tmp_b", "rstd_b", "half_b"))
        else:
            UW = PAD + LAT + PAD + CTX + PAD
            OW = LAT + PAD + CTX
            u_in = sb("conv_in", [P, 2, UW])
            acc = sb("conv_acc", [P, 2, OW])
        w_in_sem = [sem("w_in_even"), sem("w_in_odd")]
        vb_in = sem("v_bias_in")
        hi_done, lo_done = sem("w_hi_done"), sem("w_lo_done")
        mm, ev_act, ev_dve = sem("unit_mm"), sem("evac_act"), sem("evac_dve")
        out_d = [sem(f"out_dma{s}_") for s in range(4)]
        x_in, sq_done, rms_done, half_set, xn_done = sem("xb_in"), sem("sqb"), sem("rmsb"), sem("halfb"), sem("xnb")
        u_sem, pad_set, tap_done, conv_out = [sem("u_in0_"), sem("u_in1_")], sem("pad_set"), sem("tap_done"), [sem("cv0_"), sem("cv1_")]

        at = []
        n_mm = 0
        n_act = n_dve = CREDIT
        n_out = [0, 0, 0, 0]
        turn = 0
        for kind, *_, turns in SECTIONS:
            at.append((turn, n_mm, n_act, n_dve, list(n_out)))
            turn += turns
            if kind == "value":
                n_mm += ntile * turns
                n_dve += ntile * turns
            else:
                n_mm += nU * turns
            if kind == "glu":
                n_act += nch * turns
                n_dve += nch * turns
            elif kind != "value":
                n_act += nU * turns
            for s in range(4):
                if kind == "value":
                    n_out[s] += 16 * (3 if first and s % 2 else 1) * turns // 2
                elif kind != "glu" or s % 2 == 0:
                    n_out[s] += 16 * (2 if first else 1) * turns // 2
        end_out = n_out
        block = ctx.enter_context(nc.Block())

        def conv_load(eng, b):
            rows = io.proj[GA0 + P * b:GA0 + P * b + P]
            eng.dma_start(u_in[:, b % 2, PAD:PAD + LAT], rows[:, 0:LAT]).then_inc(u_sem[b % 2], 16)
            eng.dma_start(u_in[:, b % 2, 2 * PAD + LAT:2 * PAD + TOK], rows[:, LAT:TOK]).then_inc(u_sem[b % 2], 16)

        @block.sync
        def _(sp):
            def conv_store(b):
                rows = io.conv[P * b:P * b + P]
                sp.dma_start(rows[:, 0:LAT], acc[:, b % 2, 0:LAT]).then_inc(conv_out[b % 2], 16)
                sp.dma_start(rows[:, LAT:TOK], acc[:, b % 2, LAT + PAD:OW]).then_inc(conv_out[b % 2], 16)

            sp.dma_start(vbias[:], io.b_in[V0:V0 + WA].partition_broadcast(P)).then_inc(vb_in, 16)
            for (kind, c0, c1, step, turns), (t0, *_) in zip(SECTIONS, at):
                def load(i, guarded):
                    for b, col in ((0, c0), (1, c1)):
                        if guarded:
                            sp.wait_ge(lo_done, 2 * (t0 + i - 1) + b + 1)
                        sp.dma_start(wst[:, b], io.w_in[:, ds(col + step * i, P)].rearrange("(c p) n -> p c n", p=P)
                                     ).then_inc(w_in_sem[b], 16)
                start = 0
                if t0 == 0:
                    load(0, False)
                    start = 1
                with sp.Fori(start, turns) as i:
                    load(i, True)
                if first:
                    if kind == "qk":
                        sp.dma_start(xn[:], io.x_sample[LAT // 2:LAT].rearrange("(t p) d -> p t d", p=P)
                                     ).then_inc(x_in, 16)
                    continue
                for b in {"qk": (0,), "z": (1,), "gates": (2, 3)}.get(kind, ()):
                    sp.wait_ge(tap_done, TAPS * (b + 1))
                    conv_store(b)
                    if b < 2:
                        conv_load(sp, b + 2)
            if not first:
                for s in conv_out:
                    sp.wait_ge(s, 64)

        @block.gpsimd
        def _(pool):
            def split(turn_no, h, units_done):
                for b in range(2):
                    s = 2 * h + b
                    wait_reg(pool, w_in_sem[b], 16 * (turn_no + 1))
                    if units_done is not None and b == 0:
                        wait_reg(pool, mm, units_done)
                    pool.tensor_copy(w_hi[:, s], wst[:, b]).then_inc(hi_done, 1)
                    wait_reg(pool, hi_done, 2 * turn_no + b + 1)
                    pool.tensor_tensor(w_lo[:, s], wst[:, b], w_hi[:, s].bitcast(F32), ALU.subtract).then_inc(lo_done, 1)
            if first:
                pool.memset(half[:], -0.5).then_inc(half_set, 1)
            for (kind, *_, turns), (t0, m0, *_) in zip(SECTIONS, at):
                start = 0
                if t0 == 0:
                    split(0, 0, None)
                    split(1, 1, None)
                    start = 1
                if kind == "value":
                    split(t0, 0, m0 - nU)
                    split(t0 + 1, 1, m0)
                    continue
                if first and kind == "gates":
                    pool.wait_ge(half_set, 1)
                    pool.wait_ge(sq_done, 8)
                    rms_scale(pool, ssum[:], rstd[:], tmp[:], half[:], rms_done, 0)
                if turns // 2 > start:
                    with pool.Fori(start, turns // 2) as j:
                        split(t0 + 2 * j, 0, m0 + nU * (2 * j - 1))
                        split(t0 + 2 * j + 1, 1, m0 + nU * 2 * j)

        @block.tensor
        def _(pe):
            def triple(out, w_hi_c, w_lo_c, h_hi_c, h_lo_c, k):
                pe.matmul(out, w_hi_c, h_hi_c, start=(k == 0), stop=False)
                pe.matmul(out, w_hi_c, h_lo_c, start=False, stop=False)
                return pe.matmul(out, w_lo_c, h_hi_c, start=False, stop=(k == KC - 1))

            for (kind, *_, turns), (t0, m0, a0, d0, _) in zip(SECTIONS, at):
                pe.wait_ge(ev_act, a0)
                pe.wait_ge(ev_dve, d0)

                def turn(i, h):
                    if kind == "value":
                        pe.wait_ge(lo_done, 2 * (t0 + i + 1))
                        for t in range(ntile):
                            n = ntile * i + t
                            if n >= nU:
                                pe.wait_ge(ev_dve, d0 + n - nU + 1)
                            for k in range(KC):
                                tok = slice(P * t, P * t + P)
                                wv = [w[:, 2 * h:2 * h + 2, k, :] for w in (w_hi, w_lo)]
                                pe.matmul(ps[:, n % nU, 0:256], hT_hi[:, k, tok], wv[0], start=(k == 0), stop=False)
                                pe.matmul(ps[:, n % nU, 0:256], hT_hi[:, k, tok], wv[1], start=False, stop=False)
                                last = pe.matmul(ps[:, n % nU, 0:256], hT_lo[:, k, tok], wv[0], start=False,
                                                 stop=(k == KC - 1))
                            last.then_inc(mm, 1)
                        return
                    for b in range(2):
                        s = 2 * h + b
                        pe.wait_ge(lo_done, 2 * (t0 + i) + b + 1)
                        for c, (col, w, _) in enumerate(chunks):
                            u = nch * b + c
                            if kind == "glu":
                                pe.wait_ge(ev_dve if b == 0 else ev_act, (d0 if b == 0 else a0) + nch * i + c + 1 - nch)
                            else:
                                pe.wait_ge(ev_act, a0 + nU * i + u + 1 - nU)
                            for k in range(KC):
                                last = triple(ps[:, u, 0:w], w_hi[:, s, k], w_lo[:, s, k],
                                              hT_hi[:, k, col:col + w], hT_lo[:, k, col:col + w], k)
                            last.then_inc(mm, 1)

                if kind == "value":
                    turn(0, 0)
                    turn(1, 1)
                else:
                    with pe.Fori(0, turns // 2) as j:
                        turn(2 * j, 0)
                        turn(2 * j + 1, 1)

        @block.scalar
        def _(act):
            def store_rows(s, row):
                w = chunks[0][1] + chunks[1][1]
                act.dma_start(io.proj[ds(row, P), chunks[0][2]:chunks[0][2] + w], ostg[:, s, 0:w]).then_inc(out_d[s], 16)
                if first:
                    act.dma_start(io.proj[ds(row, P), LAT:TOK], ostg[:, s, w:w + CTX]).then_inc(out_d[s], 16)

            per = 16 * (2 if first else 1)
            act.sem_inc(ev_act, CREDIT)
            for (kind, c0, c1, step, turns), (t0, m0, a0, d0, o0) in zip(SECTIONS, at):
                if kind == "value":
                    for i in range(turns):
                        for b in range(2):
                            s, last = 2 * i + b, ntile * i + half_tiles * (b + 1)
                            act.wait_ge(ev_dve, d0 + last)
                            vcol = slice(256 * i, 256 * i + 256)
                            src = ostg[:, s].rearrange("p (t n) -> p t n", n=256)
                            tok0 = chunks[0][2] + P * half_tiles * b
                            n = 3 if first and b else half_tiles
                            act.dma_start(io.v[tok0:tok0 + P * n, vcol].rearrange("(t p) n -> p t n", p=P),
                                          src[:, 0:n]).then_inc(out_d[s], 16)
                            if first and b:
                                act.dma_start(io.v[LAT:TOK, vcol].rearrange("(t p) n -> p t n", p=P),
                                              src[:, 3:5]).then_inc(out_d[s], 16)
                                act.dma_start(io.state_v[:, vcol].rearrange("(t p) n -> p t n", p=P),
                                              src[:, 3:5]).then_inc(out_d[s], 16)
                        if not first and i == 0:
                            act.wait_ge(pad_set, 2)
                            act.wait_ge(out_d[0], at[1][4][0] + 16)
                            act.wait_ge(out_d[2], at[1][4][2])
                            conv_load(act, 0)
                            conv_load(act, 1)
                    continue
                with act.Fori(0, turns // 2) as j:
                    for h in range(2):
                        i = 2 * j + h
                        if kind == "glu":
                            s = 2 * h + 1
                            act.wait_ge(ev_dve, d0 + nch * i - nch)
                            for c, (col, w, _) in enumerate(chunks):
                                wait_reg(act, mm, m0 + nU * i + nch + c + 1)
                                act.activation(ostg[:, s, col:col + w], ps[:, nch + c, 0:w], ACT.Sigmoid,
                                               bias=cst.cols[:, ds(GB0 // P + i, 1)]).then_inc(ev_act, 1)
                            act.wait_ge(ev_dve, d0 + nch * (i + 1))
                            store_rows(2 * h, GA0 + P * i)
                            continue
                        for b in range(2):
                            s = 2 * h + b
                            act.wait_ge(out_d[s], o0[s] + per * j)
                            for c, (col, w, _) in enumerate(chunks):
                                u = nch * b + c
                                wait_reg(act, mm, m0 + nU * i + u + 1)
                                func, scale = ACT.Identity, 1.0
                                bias = cst.cols[:, ds((c0, c1)[b] // P + i, 1)]
                                if kind == "z":
                                    func = ACT.Silu
                                elif kind == "gates":
                                    func = ACT.Sigmoid
                                elif b == 0:
                                    scale, bias = DH ** -0.5, cst.qbias[:, ds(i, 1)]
                                act.activation(ostg[:, s, col:col + w], ps[:, u, 0:w], func, bias=bias,
                                               scale=scale).then_inc(ev_act, 1)
                            act.wait_ge(ev_act, a0 + nU * i + nch * (b + 1))
                            store_rows(s, (c0, c1)[b] + P * i)
            for s in range(4):
                act.wait_ge(out_d[s], end_out[s])

        @block.vector
        def _(dve):
            dve.sem_inc(ev_dve, CREDIT)
            if not first:
                dve.memset(u_in[:, 0], 0.0).then_inc(pad_set, 1)
                dve.memset(u_in[:, 1], 0.0).then_inc(pad_set, 1)
            for (kind, c0, c1, step, turns), (t0, m0, a0, d0, o0) in zip(SECTIONS, at):
                if kind == "glu":
                    with dve.Fori(0, turns // 2) as j:
                        for h in range(2):
                            i = 2 * j + h
                            s = 2 * h
                            dve.wait_ge(out_d[s], (32 if first else 16) * j)
                            for c, (col, w, _) in enumerate(chunks):
                                dve.wait_ge(mm, m0 + nU * i + c + 1)
                                dve.wait_ge(ev_act, a0 + nch * i + c + 1)
                                dve.scalar_tensor_tensor(ostg[:, s, col:col + w], ps[:, c, 0:w],
                                                         cst.cols[:, ds(GA0 // P + i, 1)], ostg[:, s + 1, col:col + w],
                                                         ALU.add, ALU.mult).then_inc(ev_dve, 1)
                if kind == "value":
                    dve.wait_ge(vb_in, 16)
                    for i in range(turns):
                        for t in range(ntile):
                            s = 2 * i + t // half_tiles
                            if t % half_tiles == 0:
                                dve.wait_ge(out_d[s], o0[s])
                            n = ntile * i + t
                            dve.wait_ge(mm, m0 + n + 1)
                            dst = ostg[:, s].rearrange("p (t n) -> p t n", n=256)[:, t % half_tiles]
                            dve.tensor_tensor(dst, ps[:, n % nU, 0:256], vbias[:, 256 * i:256 * i + 256],
                                              ALU.add).then_inc(ev_dve, 1)
            if first:
                for t in range(8):
                    dve.wait_ge(x_in, 16)
                    dve.tensor_tensor_reduce(square[:], xn[:, t], xn[:, t], 1.0, 0.0, ALU.mult, ALU.add,
                                             ssum[:, t:t + 1]).then_inc(sq_done, 1)
                    dve.wait_ge(sq_done, t + 1)
                dve.wait_ge(rms_done, 2)
                for t in range(8):
                    dve.tensor_scalar(xn[:, t], xn[:, t], rstd[:, t:t + 1], None, ALU.mult).then_inc(xn_done, 1)
                return
            for b in range(4):
                dve.wait_ge(u_sem[b % 2], 32 * (b // 2 + 1))
                if b >= 2:
                    dve.wait_ge(conv_out[b % 2], 32)
                for k in range(TAPS):
                    src, dst = u_in[:, b % 2, k:k + OW], acc[:, b % 2]
                    tap = cst.taps[:, 4 * k + b:4 * k + b + 1]
                    n = TAPS * b + k
                    if k == 0:
                        op = dve.tensor_scalar(dst, src, tap, cst.cols[:, R_DWB + b:R_DWB + b + 1], ALU.mult, ALU.add)
                    else:
                        dve.wait_ge(tap_done, n)
                        op = dve.scalar_tensor_tensor(dst, src, tap, dst, ALU.mult, ALU.add)
                    op.then_inc(tap_done, 1)



QR, QC = 8, 16
BANDS = [(0, 12, 0), (4, 16, 1), (12, 16, 1), (20, 12, 2)]
SETS = [(0, 24, 0), (8, 32, 1), (24, 32, 1), (40, 24, 2)]
ROW_TYPES = [(4, 12), (0, 16), (0, 12)]
COL_TYPES = [(8, 24), (0, 32), (0, 24)]
BW_R, BW_C = 16, 47
BT = 24 * BW_C
ST = (QR - 1) * BW_C + BW_R * BW_C
MASKED = -1e30
LT = 16
TPH = LT + CTX // P
TPP = 2 * TPH
RED = 2 * LT + CTX // P
KW = TOK + CTX
T_OFF, _o = {}, 0
for _r in range(3):
    for _c in range(3):
        T_OFF[_r, _c] = _o
        _o += ROW_TYPES[_r][1] * COL_TYPES[_c][1]
T_W = _o


def window_masks():
    q = np.arange(P)
    rm, cm = np.zeros((3, P, 16), np.float32), np.zeros((3, P, 32), np.float32)
    for (kr0, nr, rt), a in zip(BANDS, range(4)):
        r = QR * a + q // QC
        lo = np.clip(r - WIN_R // 2, 0, ROWS - WIN_R)[:, None]
        kr = kr0 + np.arange(nr)[None]
        rm[rt, :, :nr] = np.where((kr >= lo) & (kr < lo + WIN_R), 0, MASKED)
    for (kc0, w, ct), b in zip(SETS, range(4)):
        c = QC * b + q % QC
        lo = np.clip(c - WIN_C // 2, 0, GRID - WIN_C)[:, None]
        kc = kc0 + np.arange(w)[None]
        cm[ct, :, :w] = np.where((kc >= lo) & (kc < lo + WIN_C), 0, MASKED)
    return rm, cm


def attend(nc, io, cst):
    with ExitStack() as ctx:
        sb = lambda n, s, d=F32: ctx.enter_context(nc.sbuf_tensor(n, s, d))
        ps = lambda n, s: ctx.enter_context(nc.psum_tensor(n, s, F32))
        sem = lambda n: ctx.enter_context(nc.semaphore(n))
        q_raw, k_raw, ck_raw = sb("q_raw", [P, TOK]), sb("k_raw", [P, KW]), sb("ck_raw", [P, 2, P])
        q_sp, k_hi, k_lo = sb("q_split", [P, 2, TOK], F32R), sb("k_hi", [P, 2, KW], F32R), sb("k_lo", [P, 2, KW], F32R)
        v_win, v_ctx = sb("v_win", [P, 2, 4, 8, DH]), sb("v_ctx", [P, 2, 4, DH])
        table_pad = sb("table_pad", [HEADS, BT])
        window, win_c, tables = sb("bias_window", [P, BW_R * BW_C]), sb("bias_cols", [P, 3, 512]), sb("bias", [P, 2, T_W])
        rmask, cmask = sb("row_mask", [P, 3, 16]), sb("col_mask", [P, 3, 32])
        s_sb, p_sb, pT = sb("scores", [P, 2, 512]), sb("probs", [P, 2, 768]), sb("probs_t", [P, 2, 6, P])
        stat = sb("stat", [P, 4, 8])
        o_sb, z_sb, y_sb, sk_sb = sb("o_pair", [P, TPH, P]), sb("z_pair", [P, TOK]), sb("y_pair", [P, TOK]), sb("sk", [P, 2, DH])
        ps_win, ps_ctx = [ps("ps_win0", [P, 512]), ps("ps_win1", [P, 512])], [ps("ps_ctx0", [P, 512]), ps("ps_ctx1", [P, 512])]
        ps_tw, ps_tc, ps_o, ps_y = ps("ps_tw", [P, 4, P]), ps("ps_tc", [P, 4, P]), ps("ps_o", [P, 512]), ps("ps_y", [P, 512])
        qk_in, v_in, win_in, mask_in, z_in = sem("qk_in"), [sem("v_in0"), sem("v_in1")], sem("win_in"), sem("mask_in"), sem("z_in")
        tab_zero, tab_in, tab_out = sem("tab_zero"), sem("tab_in"), sem("tab_out")
        ck_turned, ck_done, sk_done, sk_out = sem("ck_turned"), sem("ck_done"), sem("sk_done"), sem("sk_out")
        hi_done, lo_done, col_done, tab_done = sem("qk_hi"), sem("qk_lo"), sem("cols_done"), sem("tables_done")
        s_mm, red, negmax, exp_done = sem("scores_mm"), sem("maxima"), sem("negmax"), sem("exp_done")
        tr_done, pt_win, pt_ctx, pv_done = sem("probs_turned"), sem("pt_win"), sem("pt_ctx"), sem("pv_done")
        lsum, o_done, y_turned, y_done, y_out = sem("lsum"), sem("o_done"), sem("y_turned"), sem("y_done"), sem("y_out")

        TILES = [(u, i) for u in range(2) for i in range(TPH)]
        red_before = [min(i, LT) * 2 + max(i - LT, 0) for i in range(TPH + 1)]
        PREP_AT = 5

        def keys_of(buf, u, i):
            if i >= LT:
                return None, buf[:, u, LAT:TOK]
            kr0, nr, _ = BANDS[i // 4]
            kc0, w, _ = SETS[i % 4]
            grid = buf[:, u, 0:LAT].rearrange("p (r c) -> p r c", c=GRID)
            return grid[:, kr0:kr0 + nr, kc0:kc0 + w], buf[:, u, TOK:KW]

        def n_keys(i):
            return 0 if i >= LT else BANDS[i // 4][1] * SETS[i % 4][1]

        block = ctx.enter_context(nc.Block())

        @block.sync
        def _(sp):
            sp.dma_start(rmask[:], io.row_mask.rearrange("t p r -> p t r")).then_inc(mask_in, 16)
            sp.dma_start(cmask[:], io.col_mask.rearrange("t p r -> p t r")).then_inc(mask_in, 16)
            sp.wait_ge(tab_zero, 1)
            pad3 = table_pad[:].rearrange("h (r c) -> h r c", c=BW_C)
            sp.dma_start(pad3[:, 4:19, 8:39], io.rel_bias).then_inc(tab_in, 16)

            def load_qk(n, free):
                if free:
                    sp.wait_ge(lo_done, 2 * n)
                    sp.wait_ge(sk_done, n)
                for half in range(2):
                    part = slice(DH * half, DH * half + DH)
                    sp.dma_start(q_raw[part], io.proj[ds(Q0 + n * DH, DH)]).then_inc(qk_in, 16)
                    sp.dma_start(k_raw[part, 0:TOK], io.proj[ds(K0 + n * DH, DH)]).then_inc(qk_in, 16)
                    sp.dma_start(ck_raw[:, :, part], io.cache_k[:, ds(n * DH, DH)].rearrange("(t p) d -> p t d", p=P)
                                 ).then_inc(qk_in, 16)

            def load_v(n, u, pv_before):
                if pv_before is not None:
                    sp.wait_ge(pv_done, pv_before)
                for b, (kc0, w, _) in enumerate(SETS):
                    for r in range(4):
                        src = io.v[0:LAT].rearrange("(rb r c) d -> r c rb d", r=4, c=GRID)[r, kc0:kc0 + w, :, ds(n * DH, DH)]
                        sp.dma_start(v_win[w * r:w * r + w, u, b], src).then_inc(v_in[u], 16)
                sp.dma_start(v_ctx[:, u, 0:2], io.cache_v[:, ds(n * DH, DH)].rearrange("(t p) d -> p t d", p=P)
                             ).then_inc(v_in[u], 16)
                sp.dma_start(v_ctx[:, u, 2:4], io.v[LAT:TOK, ds(n * DH, DH)].rearrange("(t p) d -> p t d", p=P)
                             ).then_inc(v_in[u], 16)

            def load_window(n, free):
                if free:
                    sp.wait_ge(col_done, 3 * n)
                for r in range(QR):
                    at = (QR - 1 - r) * BW_C
                    sp.dma_start(window[QC * r:QC * r + QC], io.table[ds(n, 1), :, at:at + BW_R * BW_C]
                                 .rearrange("h q x -> (h q) x")).then_inc(win_in, 16)

            load_qk(0, False)
            sp.wait_ge(tab_in, 16)
            for c in range(QC):
                sp.dma_start(io.table[:, c], table_pad[:, QC - 1 - c:QC - 1 - c + ST]).then_inc(tab_out, 16)
            load_v(0, 0, None)
            sp.wait_ge(tab_out, 16 * QC)
            load_window(0, False)

            def body(hp, last):
                load_qk(2 * hp + 1, True)
                load_v(2 * hp + 1, 1, hp * TPP)
                load_window(2 * hp + 1, True)
                sp.wait_ge(y_done, hp * TPH)
                sp.dma_start(z_sb[:], io.proj[ds(ZA0 + hp * P, P)]).then_inc(z_in, 16)
                sp.wait_ge(sk_done, 2 * hp + 1)
                sp.dma_start(io.state_k[:, ds(2 * hp * DH, DH)].rearrange("(t p) d -> p t d", p=P), sk_sb[:]).then_inc(sk_out, 16)
                if not last:
                    load_qk(2 * hp + 2, True)
                    load_v(2 * hp + 2, 0, hp * TPP + TPH)
                    load_window(2 * hp + 2, True)
                else:
                    pass
                sp.wait_ge(sk_done, 2 * hp + 2)
                sp.dma_start(io.state_k[:, ds((2 * hp + 1) * DH, DH)].rearrange("(t p) d -> p t d", p=P), sk_sb[:]).then_inc(sk_out, 16)
                sp.wait_ge(y_done, hp * TPH + TPH)
                sp.dma_start(io.ya[ds(hp * P, P)], y_sb[:]).then_inc(y_out, 16)

            with sp.Fori(0, HEADS // 2 - 1) as hp:
                body(hp, False)
            body(HEADS // 2 - 1, True)
            sp.wait_ge(y_out, 16 * HEADS // 2)
            sp.wait_ge(sk_out, 16 * HEADS)

        @block.tensor
        def _(pe):
            def turn_keys(n, y_before):
                pe.wait_ge(qk_in, 96 * n + 96)
                pe.wait_ge(y_done, y_before)
                pe.wait_ge(ck_done, n)
                pe.wait_ge(sk_done, n)
                for t in range(2):
                    pe.transpose(ps_y[:, P * t:P * t + P], ck_raw[:, t], cst.ident[:])
                for t in range(2):
                    tr = pe.transpose(ps_y[:, 256 + DH * t:256 + DH * t + DH], k_raw[0:DH, LAT + P * t:LAT + P * t + P],
                                      cst.ident[0:DH, 0:DH])
                tr.then_inc(ck_turned, 1)

            def scores(u, i, base, m):
                if i == 0:
                    pe.wait_ge(lo_done, 2 * (base // TPP * 2 + u + 1) if isinstance(base, int) else lo_of[0] + 2 * u + 2)
                if m >= 2:
                    pe.wait_ge(exp_done, base + m - 1)
                else:
                    pe.wait_ge(exp_done, base)
                q = q_sp[:, u, P * i:P * i + P]
                (w_hi, c_hi), (w_lo, c_lo) = keys_of(k_hi, u, i), keys_of(k_lo, u, i)
                nk = n_keys(i)
                if nk:
                    pe.matmul(ps_win[m % 2][:, 0:nk], q, w_hi, start=True, stop=False)
                    pe.matmul(ps_win[m % 2][:, 0:nk], q, w_lo, start=False, stop=True)
                pe.matmul(ps_ctx[m % 2][:, 0:CTX], q, c_hi, start=True, stop=False)
                pe.matmul(ps_ctx[m % 2][:, 0:CTX], q, c_lo, start=False, stop=True).then_inc(s_mm, 1)

            def turn_probs(u, i, base, m):
                pe.wait_ge(exp_done, base + m + 1)
                pe.wait_ge(pt_win, base + m)
                pe.wait_ge(pt_ctx, base + m)
                if i < LT:
                    w4, nb = 4 * SETS[i % 4][1], BANDS[i // 4][1] // 4
                    for j in range(nb):
                        pe.transpose(ps_tw[0:w4, j], p_sb[:, m % 2, w4 * j:w4 * j + w4], cst.ident[:])
                for j in range(2):
                    tr = pe.transpose(ps_tc[:, j], p_sb[:, m % 2, 512 + P * j:512 + P * j + P], cst.ident[:])
                tr.then_inc(tr_done, 1)

            def weigh_values(u, i, base, m, v_count):
                if i == 0:
                    pe.wait_ge(v_in[u], v_count)
                pe.wait_ge(pt_win, base + m + 1)
                pe.wait_ge(pt_ctx, base + m + 1)
                pe.wait_ge(o_done, base + m)
                nb = 0
                if i < LT:
                    w4, nb, rb0 = 4 * SETS[i % 4][1], BANDS[i // 4][1] // 4, BANDS[i // 4][0] // 4
                    for j in range(nb):
                        pe.matmul(ps_o[:, 0:DH], pT[0:w4, m % 2, j], v_win[0:w4, u, i % 4, rb0 + j],
                                  start=(j == 0), stop=False)
                for j in range(2):
                    mm = pe.matmul(ps_o[:, 0:DH], pT[:, m % 2, 4 + j], v_ctx[:, u, (2 if i >= LT else 0) + j],
                                   start=(nb == 0 and j == 0), stop=(j == 1))
                mm.then_inc(pv_done, 1)

            def turn_out(i, base, y_base, keys):
                pe.wait_ge(sk_done, keys)
                pe.wait_ge(o_done, base + TPH + i + 1)
                pe.wait_ge(y_done, y_base + i)
                pe.transpose(ps_y[:, 0:P], o_sb[:, i], cst.ident[:]).then_inc(y_turned, 1)

            lo_of = [None]
            turn_keys(0, 0)

            def body(hp, last):
                base = hp * TPP
                lo_of[0] = hp * 4
                for m in (0, 1):
                    scores(*TILES[m], base, m)
                for m, (u, i) in enumerate(TILES):
                    turn_probs(u, i, base, m)
                    if m + 2 < TPP:
                        scores(*TILES[m + 2], base, m + 2)
                    if m >= 1:
                        weigh_values(*TILES[m - 1], base, m - 1, 288 * (hp + 1))
                    if i == PREP_AT and not (last and u == 1):
                        turn_keys(2 * hp + u + 1, hp * TPH + (max(0, i - 3) if u else 0))
                    if u == 1 and i >= 3:
                        turn_out(i - 3, base, hp * TPH, 2 * hp + (2 if last or i < PREP_AT else 3))
                weigh_values(*TILES[-1], base, TPP - 1, 288 * (hp + 1))
                for i in range(TPH - 3, TPH):
                    turn_out(i, base, hp * TPH, 2 * hp + (2 if last else 3))

            with pe.Fori(0, HEADS // 2 - 1) as hp:
                body(hp, False)
            body(HEADS // 2 - 1, True)

        @block.vector
        def _(dve):
            dve.memset(table_pad[:], 0.0).then_inc(tab_zero, 1)

            def split_high(n, u):
                wait_reg(dve, qk_in, 96 * n + 96)
                wait_reg(dve, ck_done, n + 1)
                dve.tensor_copy(q_sp[:, u].rearrange("p (a b r c) -> p a b r c", a=4, b=4, r=QR) if False else q_sp[:, u, LAT:TOK],
                                q_raw[:, LAT:TOK])
                for a in range(4):
                    src = q_raw[:, 512 * a:512 * a + 512].rearrange("p (r b c) -> p b r c", r=QR, b=4)
                    dst = q_sp[:, u, 512 * a:512 * a + 512].rearrange("p (b r c) -> p b r c", b=4, r=QR)
                    dve.tensor_copy(dst, src)
                dve.tensor_copy(k_hi[:, u], k_raw[:]).then_inc(hi_done, 1)

            def soften(u, i, base, m, rbase, ready):
                nk, st = n_keys(i), stat[:, m % 4]
                if i == 0:
                    wait_reg(dve, tab_done, ready)
                wait_reg(dve, s_mm, base + m + 1)
                if m >= 2:
                    wait_reg(dve, exp_done, base + m - 1)
                r0 = rbase + u * RED + red_before[i]
                if nk:
                    off = T_OFF[BANDS[i // 4][2], SETS[i % 4][2]]
                    dve.tensor_tensor_reduce(s_sb[:, m % 2, 0:nk], ps_win[m % 2][:, 0:nk], tables[:, u, off:off + nk],
                                             1.0, -3e38, ALU.add, ALU.max, st[:, 0:1]).then_inc(red, 1)
                dve.reduce_max(st[:, 1:2], ps_ctx[m % 2][:, 0:CTX], AX_X).then_inc(red, 1)
                wait_reg(dve, red, rbase + u * RED + red_before[i + 1])
                if nk:
                    dve.tensor_scalar(st[:, 2:3], st[:, 0:1], st[:, 1:2], -1.0, ALU.max, ALU.mult).then_inc(negmax, 1)
                else:
                    dve.tensor_scalar(st[:, 2:3], st[:, 1:2], -1.0, None, ALU.mult).then_inc(negmax, 1)

            def copy_window(u, i, base, m):
                wait_reg(dve, tr_done, base + m + 1)
                if m >= 2:
                    wait_reg(dve, pv_done, base + m - 1)
                w4, nb = (4 * SETS[i % 4][1], BANDS[i // 4][1] // 4) if i < LT else (P, 0)
                if nb:
                    dve.tensor_copy(pT[0:w4, m % 2, 0:nb], ps_tw[0:w4, 0:nb]).then_inc(pt_win, 1)
                else:
                    dve.sem_inc(pt_win, 1)

            def finish_out(u, i, base, m):
                st = stat[:, m % 4]
                wait_reg(dve, exp_done, base + m + 1)
                if i < LT:
                    dve.tensor_tensor(st[:, 5:6], st[:, 3:4], st[:, 4:5], ALU.add).then_inc(lsum, 1)
                else:
                    dve.tensor_copy(st[:, 5:6], st[:, 4:5]).then_inc(lsum, 1)
                wait_reg(dve, lsum, 2 * (base + m) + 1)
                dve.reciprocal(st[:, 6:7], st[:, 5:6]).then_inc(lsum, 1)
                wait_reg(dve, lsum, 2 * (base + m) + 2)
                wait_reg(dve, pv_done, base + m + 1)
                dve.tensor_scalar(o_sb[:, i, DH * u:DH * u + DH], ps_o[:, 0:DH], st[:, 6:7], None, ALU.mult).then_inc(o_done, 1)

            def gate_out(i, y_base, z_ready):
                wait_reg(dve, y_turned, y_base + i + 1)
                if i == 0:
                    wait_reg(dve, z_in, z_ready)
                    wait_reg(dve, y_out, z_ready - 16)
                if i >= LT:
                    at = slice(LAT + P * (i - LT), LAT + P * (i - LT) + P)
                    dve.tensor_tensor(y_sb[:, at], ps_y[:, 0:P], z_sb[:, at], ALU.mult).then_inc(y_done, 1)
                    return
                a, b = i // 4, i % 4
                y, z = (x[:, 512 * a:512 * a + 512].rearrange("p (r b c) -> p b r c", r=QR, b=4)[:, b] for x in (y_sb, z_sb))
                dve.tensor_tensor(y, ps_y[:, 0:P].rearrange("p (r c) -> p r c", c=QC), z, ALU.mult).then_inc(y_done, 1)

            split_high(0, 0)

            def body(hp, last):
                base, rbase = hp * TPP, hp * 2 * RED
                wait_reg(dve, y_turned, hp * TPH)
                for m in (0, 1):
                    soften(*TILES[m], base, m, rbase, 2 * hp + 1)
                for m, (u, i) in enumerate(TILES):
                    copy_window(u, i, base, m)
                    if m + 2 < TPP:
                        u2, i2 = TILES[m + 2]
                        soften(u2, i2, base, m + 2, rbase, 2 * hp + u2 + 1)
                    if m >= 1:
                        finish_out(*TILES[m - 1], base, m - 1)
                    if i == PREP_AT + 2 and not (last and u == 1):
                        split_high(2 * hp + u + 1, 1 - u)
                    if u == 1 and i >= 3:
                        gate_out(i - 3, hp * TPH, 16 * (hp + 1))
                finish_out(*TILES[-1], base, TPP - 1)
                for i in range(TPH - 3, TPH):
                    gate_out(i, hp * TPH, 16 * (hp + 1))

            with dve.Fori(0, HEADS // 2 - 1) as hp:
                body(hp, False)
            body(HEADS // 2 - 1, True)

        @block.scalar
        def _(act):
            def copy_keys(n):
                wait_reg(act, ck_turned, n + 1)
                act.activation(k_raw[:, TOK:KW], ps_y[:, 0:CTX], ACT.Copy).then_inc(ck_done, 1)
                wait_reg(act, sk_out, 16 * n)
                act.activation(sk_sb[:], ps_y[:, 256:256 + P].rearrange("p (t d) -> p t d", t=2), ACT.Copy).then_inc(sk_done, 1)

            def exponents(u, i, base, m):
                nk, st = n_keys(i), stat[:, m % 4]
                wait_reg(act, negmax, base + m + 1)
                if m >= 2:
                    wait_reg(act, tr_done, base + m - 1)
                    wait_reg(act, lsum, 2 * (base + m) - 6 if m >= 4 else base * 2)
                if nk:
                    act.activation(p_sb[:, m % 2, 0:nk], s_sb[:, m % 2, 0:nk], ACT.Exp, bias=st[:, 2:3],
                                   accum_out=st[:, 3:4])
                act.activation(p_sb[:, m % 2, 512:768], ps_ctx[m % 2][:, 0:CTX], ACT.Exp, bias=st[:, 2:3],
                               accum_out=st[:, 4:5]).then_inc(exp_done, 1)

            def copy_context(u, i, base, m):
                wait_reg(act, tr_done, base + m + 1)
                if m >= 2:
                    wait_reg(act, pv_done, base + m - 1)
                act.activation(pT[:, m % 2, 4:6], ps_tc[:, 0:2], ACT.Copy).then_inc(pt_ctx, 1)

            copy_keys(0)

            def body(hp, last):
                base = hp * TPP
                for m in (0, 1):
                    exponents(*TILES[m], base, m)
                for m, (u, i) in enumerate(TILES):
                    copy_context(u, i, base, m)
                    if m + 2 < TPP:
                        exponents(*TILES[m + 2], base, m + 2)
                    if i == PREP_AT and not (last and u == 1):
                        copy_keys(2 * hp + u + 1)

            with act.Fori(0, HEADS // 2 - 1) as hp:
                body(hp, False)
            body(HEADS // 2 - 1, True)

        @block.gpsimd
        def _(pool):
            def prepare(n, u, s_before):
                wait_reg(pool, hi_done, n + 1)
                wait_reg(pool, tab_done, n)
                low = slice(DH, P)
                for a in range(4):
                    src = q_raw[low, 512 * a:512 * a + 512].rearrange("p (r b c) -> p b r c", r=QR, b=4)
                    dst = q_sp[low, u, 512 * a:512 * a + 512].rearrange("p (b r c) -> p b r c", b=4, r=QR)
                    for b in range(4):
                        pool.tensor_tensor(dst[:, b], src[:, b], dst[:, b].bitcast(F32), ALU.subtract)
                pool.tensor_tensor(q_sp[low, u, LAT:TOK], q_raw[low, LAT:TOK], q_sp[low, u, LAT:TOK].bitcast(F32),
                                   ALU.subtract).then_inc(lo_done, 1)
                wait_reg(pool, lo_done, 2 * n + 1)
                pool.tensor_tensor(k_lo[:, u], k_raw[:], k_hi[:, u].bitcast(F32), ALU.subtract).then_inc(lo_done, 1)
                wait_reg(pool, win_in, 128 * n + 128)
                wait_reg(pool, negmax, s_before)
                win = window[:].rearrange("p (r c) -> p r c", c=BW_C)
                for ct, (c0, w) in enumerate(COL_TYPES):
                    pool.tensor_tensor(win_c[:, ct, 0:16 * w].rearrange("p (r c) -> p r c", c=w), win[:, :, c0:c0 + w],
                                       cmask[:, ct, 0:w].unsqueeze(1).to_broadcast([P, 16, w]), ALU.add).then_inc(col_done, 1)
                wait_reg(pool, col_done, 3 * n + 3)
                for (rt, ct), off in T_OFF.items():
                    (r0, nr), w = ROW_TYPES[rt], COL_TYPES[ct][1]
                    op = pool.tensor_tensor(tables[:, u, off:off + nr * w].rearrange("p (r c) -> p r c", c=w),
                                            win_c[:, ct, w * r0:w * (r0 + nr)].rearrange("p (r c) -> p r c", c=w),
                                            rmask[:, rt, 0:nr].unsqueeze(2).to_broadcast([P, nr, w]), ALU.add)
                op.then_inc(tab_done, 1)

            pool.wait_ge(mask_in, 32)
            prepare(0, 0, 0)
            with pool.Fori(0, HEADS // 2 - 1) as hp:
                prepare(2 * hp + 1, 1, hp * TPP)
                prepare(2 * hp + 2, 0, hp * TPP + TPH)
            prepare(HEADS - 1, 1, (HEADS // 2 - 1) * TPP)


CH = 256
NCH = TOK // CH


def split_weights(nc, sp_loads, stage, w_hi, w_lo, w_in, w_hi_done, w_lo_done, n):
    def load(sp):
        for k in range(n):
            if k >= 2:
                sp.wait_ge(w_lo_done, k - 1)
            sp.dma_start(stage[:, k % 2], sp_loads[k]).then_inc(w_in[k % 2], 16)

    def split(dve):
        for k in range(n):
            dve.wait_ge(w_in[k % 2], 16 * (k // 2 + 1))
            dve.tensor_copy(w_hi[:, k], stage[:, k % 2]).then_inc(w_hi_done, 1)
            dve.wait_ge(w_hi_done, k + 1)
            dve.tensor_tensor(w_lo[:, k], stage[:, k % 2], w_hi[:, k].bitcast(F32), ALU.subtract).then_inc(w_lo_done, 1)
    return load, split


def merge(nc, io, cst):
    with ExitStack() as ctx:
        sb = lambda n, s, d=F32: ctx.enter_context(nc.sbuf_tensor(n, s, d))
        sem = lambda n: ctx.enter_context(nc.semaphore(n))
        stage, w_hi, w_lo = sb("wp_stage", [P, 2, D]), sb("wp_hi", [P, 8, D], F32R), sb("wp_lo", [P, 8, D], F32R)
        ya, cv, zb = (sb(n, [P, 2, 4, CH]) for n in ("ya_in", "cv_in", "zb_in"))
        gates = sb("gates_in", [P, 2, 2 * KC, CH])
        y_hi, y_lo = sb("y_hi", [P, 2, 8, CH], F32R), sb("y_lo", [P, 2, 8, CH], F32R)
        act_sb, yb = sb("ln_silu", [P, 4, CH]), sb("yb", [P, 4, CH])
        normed = sb("normed", [P, 2, WB])
        bn, mv, var_eps, rstd, shift, half = (sb(n, [P, 2, w]) for n, w in (
            ("bn", 6), ("mv", 2), ("var_eps", 1), ("ln_rstd", 1), ("ln_shift", 1), ("ln_half", 1)))
        gated, m_sb = sb("gated", [P, 2, 2, CH]), sb("m_out", [P, 2, KC, CH])
        ps_o = ctx.enter_context(nc.psum_tensor("ps_proj", [P, 4, 2, CH], F32))
        ps_n = ctx.enter_context(nc.psum_tensor("ps_norm", [P, 2, WB], F32))
        ps_b = ctx.enter_context(nc.psum_tensor("ps_back", [P, 4, CH], F32))
        w_in, w_hid, w_lod = [sem("wp_in0"), sem("wp_in1")], sem("wp_hid"), sem("wp_lod")
        s_in, g_in = [sem("s_in0"), sem("s_in1")], [sem("g_in0"), sem("g_in1")]
        t_in, bn_done, mv_done, rs_done, sh_done, n_done = (sem(n) for n in ("t_in", "bn_done", "mv_done", "rs_done", "sh_done", "n_done"))
        t_back, silu_done, yb_done, hi_done, lo_done, half_set = (sem(n) for n in ("t_back", "silu_m", "yb_done", "y_hid", "y_lod", "half_m"))
        mm, gated_done, m_done, m_out = sem("proj_mm"), sem("gated_done"), sem("m_done"), [sem("m_out0"), sem("m_out1")]
        loads = [w[P * k:P * k + P] for w in (io.w_proj_a, io.w_proj_b) for k in range(4)]
        load_w, split_w = split_weights(nc, loads, stage, w_hi, w_lo, w_in, w_hid, w_lod, 8)
        GD0 = 4
        block = ctx.enter_context(nc.Block())

        def chunks(eng, body):
            with eng.Fori(0, NCH // 2) as t:
                body(2 * t, t, 0, False)
                body(2 * t + 1, t, 1, False)
            body(NCH - 1, NCH // 2, 0, True)

        @block.sync
        def _(sp):
            def small(j, par):
                for src, dst in ((io.ya, ya), (io.conv, cv), (io.proj[ZB0:ZB0 + WB], zb)):
                    sp.dma_start(dst[:, par], src[:, ds(CH * j, CH)].rearrange("(b p) t -> p b t", p=P)).then_inc(s_in[par], 16)

            def big(j, par):
                sp.dma_start(gates[:, par], io.proj[G0:D_IN, ds(CH * j, CH)].rearrange("(b p) t -> p b t", p=P)
                             ).then_inc(g_in[par], 16)

            small(0, 0)
            load_w(sp)
            small(1, 1)
            big(0, 0)

            def body(j, par):
                wait_reg(sp, gated_done, GD0 + 8 * j)
                big(j + 1, 1 - par)
                wait_reg(sp, lo_done, 2 * j + 2)
                small(j + 2, par)

            with sp.Fori(0, NCH // 2 - 1) as t:
                body(2 * t, 0)
                body(2 * t + 1, 1)
            body(NCH - 3, 0)
            sp.wait_ge(gated_done, GD0 + 8 * (NCH - 2))
            big(NCH - 1, 0)

        @block.gpsimd
        def _(pool):
            pool.memset(half[:], -0.5).then_inc(half_set, 1)
            pool.wait_ge(half_set, 1)

            def norm_and_split(j, jh, par):
                wait_reg(pool, mv_done, 2 * j + 2)
                pool.tensor_scalar(var_eps[:], mv[:, :, 1:2], EPS, None, ALU.add).then_inc(rs_done, 1)
                wait_reg(pool, rs_done, 2 * j + 1)
                pool.tensor_tensor(rstd[:], var_eps[:], half[:], ALU.pow).then_inc(rs_done, 1)
                wait_reg(pool, hi_done, 2 * j + 1)
                pool.tensor_tensor(y_lo[:, par, 0:4], ya[:, par], y_hi[:, par, 0:4].bitcast(F32), ALU.subtract).then_inc(lo_done, 1)
                wait_reg(pool, hi_done, 2 * j + 2)
                pool.tensor_tensor(y_lo[:, par, 4:8], yb[:], y_hi[:, par, 4:8].bitcast(F32), ALU.subtract).then_inc(lo_done, 1)

            norm_and_split(0, 0, 0)
            chunks(pool, lambda j, jh, par, last: None if last else norm_and_split(j + 1, jh, 1 - par))

        @block.tensor
        def _(pe):
            def turn_in(j, jh, par):
                pe.wait_ge(s_in[par], 48 * (jh + 1))
                pe.wait_ge(n_done, 2 * j)
                for t in range(2):
                    for b in range(4):
                        tr = pe.transpose(ps_n[:, t, P * b:P * b + P], cv[:, par, b, P * t:P * t + P], cst.ident[:])
                tr.then_inc(t_in, 1)

            def turn_back(j):
                pe.wait_ge(n_done, 2 * j + 2)
                pe.wait_ge(silu_done, 4 * j)
                for b in range(4):
                    for t in range(2):
                        tr = pe.transpose(ps_b[:, b, P * t:P * t + P], normed[:, t, P * b:P * b + P], cst.ident[:])
                tr.then_inc(t_back, 1)

            def next_half(jh, par):
                return jh + par

            turn_in(0, 0, 0)
            turn_back(0)

            def body(j, jh, par, last):
                pe.wait_ge(w_lod, 8)
                pe.wait_ge(lo_done, 2 * j + 2)
                for o in range(8):
                    pe.wait_ge(gated_done, GD0 + 8 * j + o + 1 - 4)
                    for half_no in range(2):
                        out = ps_o[:, o % 4, half_no]
                        for k in range(4):
                            kk, col = 4 * half_no + k, slice(P * o, P * o + P)
                            pe.matmul(out, w_hi[:, kk, col], y_hi[:, par, kk], start=(k == 0), stop=False)
                            pe.matmul(out, w_hi[:, kk, col], y_lo[:, par, kk], start=False, stop=False)
                            last_mm = pe.matmul(out, w_lo[:, kk, col], y_hi[:, par, kk], start=False, stop=(k == 3))
                    last_mm.then_inc(mm, 1)
                    if not last and o == 1:
                        turn_in(j + 1, next_half(jh, par), 1 - par)
                    if not last and o == 4:
                        turn_back(j + 1)

            chunks(pe, body)

        @block.scalar
        def _(act):
            def norm(j):
                wait_reg(act, sh_done, j + 1)
                wait_reg(act, t_back, j)
                for t in range(2):
                    act.activation(normed[:, t], ps_n[:, t], ACT.Identity, bias=shift[:, t], scale=rstd[:, t]).then_inc(n_done, 1)

            def silu(j):
                wait_reg(act, t_back, j + 1)
                wait_reg(act, yb_done, j)
                for b in range(4):
                    act.activation(act_sb[:, b], ps_b[:, b], ACT.Silu, bias=cst.cols[:, R_LNB + b:R_LNB + b + 1],
                                   scale=cst.cols[:, R_LNG + b:R_LNG + b + 1]).then_inc(silu_done, 1)

            norm(0)
            silu(0)

            def body(j, jh, par, last):
                if not last:
                    norm(j + 1)
                    silu(j + 1)
                wait_reg(act, m_done, 8 * j + 8)
                act.dma_start(io.m[:, ds(CH * j, CH)].rearrange("(b p) t -> p b t", p=P), m_sb[:, par]).then_inc(m_out[par], 16)

            chunks(act, body)
            act.wait_ge(m_out[0], 16 * (NCH // 2 + 1))
            act.wait_ge(m_out[1], 16 * (NCH // 2))

        @block.vector
        def _(dve):
            def stats(j):
                wait_reg(dve, t_in, j + 1)
                for t in range(2):
                    dve.bn_stats(bn[:, t], ps_n[:, t]).then_inc(bn_done, 1)
                wait_reg(dve, bn_done, 2 * j + 2)
                for t in range(2):
                    dve.bn_aggr(mv[:, t], bn[:, t]).then_inc(mv_done, 1)
                wait_reg(dve, rs_done, 2 * j + 2)
                dve.scalar_tensor_tensor(shift[:], mv[:, :, 0:1], -1.0, rstd[:], ALU.mult, ALU.mult).then_inc(sh_done, 1)

            def high(j, jh, par, part):
                if part == 0:
                    wait_reg(dve, s_in[par], 48 * (jh + 1))
                    dve.tensor_copy(y_hi[:, par, 0:4], ya[:, par]).then_inc(hi_done, 1)
                else:
                    wait_reg(dve, silu_done, 4 * j + 4)
                    wait_reg(dve, lo_done, 2 * j)
                    dve.tensor_tensor(yb[:], act_sb[:], zb[:, par], ALU.mult).then_inc(yb_done, 1)
                    wait_reg(dve, yb_done, j + 1)
                    dve.tensor_copy(y_hi[:, par, 4:8], yb[:]).then_inc(hi_done, 1)

            dve.sem_inc(gated_done, GD0)
            stats(0)
            high(0, 0, 0, 0)
            high(0, 0, 0, 1)
            split_w(dve)

            def body(j, jh, par, last):
                wait_reg(dve, g_in[par], 16 * (jh + 1))
                wait_reg(dve, m_out[par], 16 * jh)
                for o in range(8):
                    n = 8 * j + o
                    wait_reg(dve, mm, n + 1)
                    dve.tensor_tensor(gated[:, o % 2], ps_o[:, o % 4], gates[:, par, o:o + KC + 1:KC], ALU.mult).then_inc(gated_done, 1)
                    wait_reg(dve, gated_done, GD0 + n + 1)
                    dve.tensor_tensor(m_sb[:, par, o], gated[:, o % 2, 0], gated[:, o % 2, 1], ALU.add).then_inc(m_done, 1)
                    if not last and o == 1:
                        stats(j + 1)
                    if not last and o == 2:
                        high(j + 1, jh + par, 1 - par, 0)
                    if not last and o == 5:
                        high(j + 1, jh + par, 1 - par, 1)

            chunks(dve, body)


def finish(nc, io, cst):
    with ExitStack() as ctx:
        sb = lambda n, s, d=F32: ctx.enter_context(nc.sbuf_tensor(n, s, d))
        sem = lambda n: ctx.enter_context(nc.semaphore(n))
        stage, w_hi, w_lo = sb("wo_stage", [P, 2, D]), sb("wo_hi", [P, KC, D], F32R), sb("wo_lo", [P, KC, D], F32R)
        m_in, x_in = sb("m_in", [P, 2, KC, CH]), sb("x_in", [P, 2, 2, D])
        m_hi, m_lo = sb("m_hi", [P, 2, KC, CH], F32R), sb("m_lo", [P, 2, KC, CH], F32R)
        ones, diag = sb("ones", [P, P]), sb("diag", [P, 2, P])
        gate_bc, fg = sb("gate_rows", [P, 2, D]), sb("final_g", [P, D])
        z, square = sb("z_res", [P, 2, D]), sb("z_square", [P, D])
        ssum, tmp, rstd, half = (sb(n, [P, 2, 1]) for n in ("z_ssum", "z_tmp", "z_rstd", "z_half"))
        psF = ctx.enter_context(nc.psum_tensor("psF", [P, 2, 2, 2, 512], F32))
        w_in, w_hid, w_lod = [sem("wo_in0"), sem("wo_in1")], sem("wo_hid"), sem("wo_lod")
        m_ins, x_ins, fg_in = [sem("m_in0"), sem("m_in1")], [sem("x_in0_"), sem("x_in1_")], sem("fg_in")
        ones_set, diag_done, gate_mm, gate_out, half_set = (sem(n) for n in ("ones_set", "diag_done", "gate_mm", "gate_out", "half_f"))
        hi_done, lo_done, mm, scaled, z_done, sq_done, rs_done, y_done = (
            sem(n) for n in ("m_hid", "m_lod", "out_mm", "gated_f", "z_done", "z_sq", "z_rs", "y_fin"))
        y_out = [sem("y_out0"), sem("y_out1")]
        load_w, split_w = split_weights(nc, [io.w_out[P * k:P * k + P] for k in range(KC)], stage, w_hi, w_lo, w_in, w_hid, w_lod, KC)
        SC0 = 8
        block = ctx.enter_context(nc.Block())

        def chunks(eng, body):
            with eng.Fori(0, NCH // 2) as t:
                body(2 * t, t, 0, False)
                body(2 * t + 1, t, 1, False)
            body(NCH - 1, NCH // 2, 0, True)

        @block.sync
        def _(sp):
            def load(j, par, last):
                sp.dma_start(m_in[:, par], io.m[:, ds(CH * j, CH)].rearrange("(b p) t -> p b t", p=P)).then_inc(m_ins[par], 16)
                x = io.x_prompt if last else io.x_sample[ds(CH * j, CH)]
                sp.dma_start(x_in[:, par], x.rearrange("(t p) d -> p t d", p=P)).then_inc(x_ins[par], 16)
            load(0, 0, False)
            load_w(sp)
            load(1, 1, False)
            sp.dma_start(fg[:], io.final_g.partition_broadcast(P)).then_inc(fg_in, 16)

            def again(j, last):
                wait_reg(sp, lo_done, j - 1)
                wait_reg(sp, z_done, 4 * (j - 1))
            with sp.Fori(1, NCH // 2) as t:
                again(2 * t, False)
                load(2 * t, 0, False)
                again(2 * t + 1, False)
                load(2 * t + 1, 1, False)
            again(NCH - 1, True)
            load(NCH - 1, 0, True)

        @block.gpsimd
        def _(pool):
            pool.memset(half[:], -0.5).then_inc(half_set, 1)
            pool.wait_ge(half_set, 1)

            def low(j, par):
                wait_reg(pool, hi_done, j + 1)
                pool.tensor_tensor(m_lo[:, par], m_in[:, par], m_hi[:, par].bitcast(F32), ALU.subtract).then_inc(lo_done, 1)
            low(0, 0)

            def body(j, jh, par, last):
                if not last:
                    low(j + 1, 1 - par)
                for t in range(2):
                    n = 2 * j + t
                    wait_reg(pool, sq_done, n + 1)
                    pool.tensor_scalar(tmp[:, t], ssum[:, t], 1.0 / D, EPS, ALU.mult, ALU.add).then_inc(rs_done, 1)
                    wait_reg(pool, rs_done, 2 * n + 1)
                    pool.tensor_tensor(rstd[:, t], tmp[:, t], half[:, t], ALU.pow).then_inc(rs_done, 1)
            chunks(pool, body)

        @block.tensor
        def _(pe):
            pe.wait_ge(ones_set, 1)
            for n in range(2 * KC):
                g, k = n // KC, n % KC
                pe.wait_ge(diag_done, n + 1)
                pe.matmul(psF[:, 0, g, k // 4, P * (k % 4):P * (k % 4) + P], ones[:], diag[:, n % 2], start=True,
                          stop=True).then_inc(gate_mm, 1)
            pe.wait_ge(gate_out, 2)
            pe.wait_ge(w_lod, KC)

            def body(j, jh, par, last):
                pe.wait_ge(lo_done, j + 1)
                for t in range(2):
                    for h in range(2):
                        out = psF[:, par, t, h]
                        pe.wait_ge(scaled, SC0 + 4 * j + 2 * t + h + 1 - 8)
                        for k in range(KC):
                            tok, col = slice(P * t, P * t + P), slice(512 * h, 512 * h + 512)
                            pe.matmul(out, m_hi[:, par, k, tok], w_hi[:, k, col], start=(k == 0), stop=False)
                            pe.matmul(out, m_hi[:, par, k, tok], w_lo[:, k, col], start=False, stop=False)
                            mmi = pe.matmul(out, m_lo[:, par, k, tok], w_hi[:, k, col], start=False, stop=(k == KC - 1))
                        mmi.then_inc(mm, 1)
            chunks(pe, body)

        @block.scalar
        def _(act):
            def body(j, jh, par, last):
                for t in range(2):
                    n = 2 * j + t
                    wait_reg(act, z_done, 2 * n + 2)
                    act.activation(square[:], z[:, t], ACT.Square, accum_out=ssum[:, t]).then_inc(sq_done, 1)
                    wait_reg(act, sq_done, n + 1)
                for t in range(2):
                    wait_reg(act, y_done, 2 * j + t + 1)
                    y = (io.y_prompt if last else io.y_sample[ds(CH * j, CH)])[P * t:P * t + P]
                    act.dma_start(y, z[:, t]).then_inc(y_out[t], 16)
            chunks(act, body)
            for s in y_out:
                act.wait_ge(s, 16 * NCH)

        @block.vector
        def _(dve):
            dve.sem_inc(scaled, SC0)
            dve.memset(ones[:], 1.0).then_inc(ones_set, 1)

            def high(j, jh, par):
                wait_reg(dve, m_ins[par], 16 * (jh + 1))
                wait_reg(dve, mm, 4 * (j - 1) if isinstance(j, int) and j > 0 else (4 * j - 4 if not isinstance(j, int) else 0))
                dve.tensor_copy(m_hi[:, par], m_in[:, par]).then_inc(hi_done, 1)

            for n in range(2 * KC):
                g, k = n // KC, n % KC
                if n >= 2:
                    dve.wait_ge(gate_mm, n - 1)
                dve.tensor_scalar(diag[:, n % 2], cst.ident[:], cst.gate[:, k, g:g + 1], None, ALU.mult).then_inc(diag_done, 1)
            dve.wait_ge(gate_mm, 2 * KC)
            for g in range(2):
                dve.tensor_copy(gate_bc[:, g], psF[:, 0, g].rearrange("p h n -> p (h n)")).then_inc(gate_out, 1)
            high(0, 0, 0)
            split_w(dve)
            dve.wait_ge(fg_in, 16)
            dve.wait_ge(gate_out, 2)

            def body(j, jh, par, last):
                if not last:
                    high(j + 1, jh + par, 1 - par)
                g = 0 if last else 1
                wait_reg(dve, x_ins[par], 16 * (jh + 1))
                for t in range(2):
                    wait_reg(dve, y_out[t], 16 * j)
                    for h in range(2):
                        n = 4 * j + 2 * t + h
                        col = slice(512 * h, 512 * h + 512)
                        wait_reg(dve, mm, n + 1)
                        dve.tensor_tensor(z[:, t, col], psF[:, par, t, h], gate_bc[:, g, col], ALU.mult).then_inc(scaled, 1)
                        wait_reg(dve, scaled, SC0 + n + 1)
                        dve.tensor_tensor(z[:, t, col], z[:, t, col], x_in[:, par, t, col], ALU.add).then_inc(z_done, 1)
                    wait_reg(dve, rs_done, 4 * j + 2 * t + 2)
                    dve.scalar_tensor_tensor(z[:, t], z[:, t], rstd[:, t], fg[:], ALU.mult, ALU.mult).then_inc(y_done, 1)
            chunks(dve, body)


IN_NAMES = ["x_prompt", "x_sample", "cache_k", "cache_v", "c", "c_ctx", "rms_g", "w_ada", "b_ada", "w_in", "b_in",
            "rel_bias", "dw_w", "dw_b", "ln_g", "ln_b", "w_proj_a", "w_proj_b", "w_out", "final_g"]
OUTS = [("y_prompt", (CTX, D)), ("y_sample", (LAT, D)), ("state_k", (CTX, WA)), ("state_v", (CTX, WA))]


class Store:
    pass


def build(nc, io):
    io.proj = nc.dram_tensor("proj", (D_IN, TOK), F32, kind="Internal").ap()
    io.v = nc.dram_tensor("v_tokens", (TOK, WA), F32, kind="Internal").ap()
    io.conv = nc.dram_tensor("conv", (WB, TOK), F32, kind="Internal").ap()
    io.ya = nc.dram_tensor("ya", (WA, TOK), F32, kind="Internal").ap()
    io.m = nc.dram_tensor("merged", (D, TOK), F32, kind="Internal").ap()
    io.table = nc.dram_tensor("shifted_bias", (HEADS, QC, ST), F32, kind="Internal").ap()
    cst = Store()
    with ExitStack() as ctx:
        sb = lambda n, s, d=F32: ctx.enter_context(nc.sbuf_tensor(n, s, d))
        cst.ident = sb("ident", [P, P])
        cst.cols = sb("param_cols", [P, R_C])
        cst.taps = sb("taps", [P, 4 * TAPS])
        cst.qbias = sb("q_bias", [P, 4])
        cst.shift, cst.scale, cst.gate = (sb(n, [P, KC, 2]) for n in ("shift", "scale", "gate"))
        with ExitStack() as c2:
            hT_hi = c2.enter_context(nc.sbuf_tensor("hT_hi", [P, KC, HT_W], F32R))
            hT_lo = c2.enter_context(nc.sbuf_tensor("hT_lo", [P, KC, HT_W], F32R))
            modulation(nc, io, cst, hT_hi, hT_lo)
            with nc.sbuf_tensor("xn_b", [P, 8, D], F32) as xn:
                project(nc, io, cst, hT_hi, hT_lo, GROUP_A, 0, xn)
                turn_group_b(nc, cst, xn, hT_hi, hT_lo)
            project(nc, io, cst, hT_hi, hT_lo, GROUP_B, 1)
        attend(nc, io, cst)
        merge(nc, io, cst)
        finish(nc, io, cst)


def kernel(**inputs):
    import concourse.bacc as bacc
    from concourse.bass_utils import run_bass_kernel_spmd

    nc = bacc.Bacc("TRN2", target_bir_lowering=False, num_devices=1)
    arrays, io = {}, Store()
    flat = {"x_prompt": (CTX, D), "x_sample": (LAT, D), "cache_k": (CTX, WA), "cache_v": (CTX, WA), "c": (D,),
            "rms_g": (D,), "w_ada": (D, 3 * D), "b_ada": (3 * D,), "w_in": (D, D_IN), "b_in": (D_IN,),
            "rel_bias": (HEADS, 2 * WIN_R - 1, 2 * WIN_C - 1), "dw_w": (TAPS, WB), "dw_b": (WB,), "ln_g": (WB,),
            "ln_b": (WB,), "w_proj_a": (WA, D), "w_proj_b": (WB, D), "w_out": (D, D)}
    row_mask, col_mask = window_masks()
    consts = {"ident": np.eye(P, dtype=np.float32), "row_mask": row_mask, "col_mask": col_mask}
    given = {n: inputs[n] for n in IN_NAMES}
    given.update(consts)

    aps = {}
    for name, a in given.items():
        a = np.ascontiguousarray(a).reshape(flat.get(name, np.shape(a)))
        arrays[f"in_{name}"] = a
        aps[name] = nc.dram_tensor(f"in_{name}", a.shape, mybir.dt.from_np(a.dtype), kind="ExternalInput").ap()
    for name, shape in OUTS:
        aps[name] = nc.dram_tensor(f"out_{name}", shape, F32, kind="ExternalOutput").ap()
    io.__dict__.update(aps)
    build(nc, io)
    r = run_bass_kernel_spmd(nc, [arrays], core_ids=[0]).results[0]
    y_p, y_s, sk, sv = (r[f"out_{name}"] for name, _ in OUTS)
    return (y_p.reshape(1, CTX, D), y_s.reshape(1, LAT, D), sk.reshape(1, 1, CTX, HEADS, DH),
            sv.reshape(1, 1, CTX, HEADS, DH))
```

```python
from contextlib import ExitStack

import numpy as np

import concourse.bass as bass
from concourse import mybir

F32 = mybir.dt.float32
F32R = mybir.dt.float32r
ALU = mybir.AluOpType
ACT = mybir.ActivationFunctionType
AX_X = mybir.AxisListType.X
ds = bass.ds

P = 128
D = 1024
KC = D // P
LAT, CTX = 2048, 256
TOK = LAT + CTX
HEADS, DH = 8, 64
WA = WB = 512
TAPS, PAD = 31, 15
GRID, ROWS = 64, 32
WIN_R, WIN_C = 8, 16
EPS = 1e-6
Q0, K0, V0, ZA0 = 0, WA, 2 * WA, 3 * WA
GA0 = 4 * WA
GB0 = GA0 + WB
ZB0 = 4 * WA + 2 * WB
G0 = 4 * WA + 3 * WB
D_IN = G0 + 2 * D

GROUP_A = [(0, 512, 0), (512, 512, 512), (1024, CTX, LAT)]
GROUP_B = [(0, 512, 1024), (512, 512, 1536)]
HT_W = 1280

R_BIN, R_DWB, R_LNG, R_LNB, R_RMS, R_BADA, R_C = 0, 44, 48, 52, 56, 64, 88
R_END = R_C + 2 * KC

SECTIONS = [
    ("glu", GA0, GB0, P, 4),
    ("value", V0, V0 + P, 2 * P, 2),
    ("qk", Q0, K0, P, 4),
    ("z", ZA0, ZB0, P, 4),
    ("gates", G0, G0 + D, P, 8),
]
TURNS = sum(s[4] for s in SECTIONS)
CREDIT = 16


START, DMA_START = 1, 16


def rms_scale(pool, src, out, eps_tmp, minus_half, done, n):
    pool.tensor_scalar(eps_tmp, src, 1.0 / D, EPS, ALU.mult, ALU.add).then_inc(done, 1)
    pool.wait_ge(done, n + 1)
    pool.tensor_tensor(out, eps_tmp, minus_half, ALU.pow).then_inc(done, 1)


def wait_reg(eng, sem, value):
    eng.wait_ge(sem, value)
    eng.nop(nofuse=True)


GATE_OUT_AT = [12, 20]


def modulation(nc, io, cst, hT_hi, hT_lo):
    with ExitStack() as ctx:
        sb = lambda n, s, d=F32: ctx.enter_context(nc.sbuf_tensor(n, s, d))
        sem = lambda n: ctx.enter_context(nc.semaphore(n))
        rows = sb("param_rows", [P, P])
        taps = sb("tap_rows", [P, P])
        silu_c = sb("silu_c", [P, 2 * KC])
        wada = sb("wada", [P, 3, KC, 512])
        ada_row = sb("ada_row", [2, 4 * 512])
        gate_bias = sb("gate_bias", [2, D])
        table_pad = sb("table_pad", [HEADS, BT])
        xn = sb("xn_a", [P, 10, D])
        square = sb("square", [P, D])
        ssum = sb("ssum", [P, 10])
        tmp = sb("rms_tmp", [P, 10])
        rstd = sb("rstd", [P, 10])
        half = sb("minus_half", [P, 10])
        scale1 = sb("scale1", [P, KC, 2])
        hf = sb("h_f32", [P, 3, 512])
        psT = ctx.enter_context(nc.psum_tensor("psT", [P, 2, 512], F32))
        psM = ctx.enter_context(nc.psum_tensor("psM", [P, 2, 512], F32))
        psX = ctx.enter_context(nc.psum_tensor("psX", [P, 3, 512], F32))
        psC = ctx.enter_context(nc.psum_tensor("psC", [P, 2 * KC, 2], F32))
        ada_turned, gb_in, gate_done = sem("ada_turned"), sem("gate_bias_in"), sem("gate_done")
        tab_zero, tab_in, tab_out = sem("tab_zero"), sem("tab_in"), sem("tab_out")
        ident_in = sem("ident_in")
        rows_in, x_in, ada_in = sem("rows_in"), [sem(f"x_in{i}") for i in range(5)], [sem(f"ada_in{i}") for i in range(3)]
        turned, cols_out, silu_done = sem("turned"), sem("cols_out"), sem("silu_done")
        ada_mm, ada_out, sq_done, rms_done, xn_done = sem("ada_mm"), sem("ada_out"), sem("sq_done"), sem("rms_done"), sem("xn_done")
        half_set, mod_done, tr_done, hf_done, hi_done, lo_dve, lo_pool = (
            sem("half_set"), sem("mod_done"), sem("tr_done"), sem("hf_done"), sem("hi_done"), sem("lo_dve"), sem("lo_pool"))
        units = [(c, k) for c in range(3) for k in range(KC)]
        block = ctx.enter_context(nc.Block())

        @block.sync
        def _(sp):
            sp.dma_start(cst.ident[:], io.ident).then_inc(ident_in, 16)
            for r, a, n in ((R_BIN, io.b_in, 44), (R_DWB, io.dw_b, 4), (R_LNG, io.ln_g, 4), (R_LNB, io.ln_b, 4),
                            (R_RMS, io.rms_g, 8), (R_BADA, io.b_ada, 24), (R_C, io.c_ctx, 8), (R_C + KC, io.c, 8)):
                sp.dma_start(rows[r:r + n, :], a.rearrange("(r p) -> r p", p=P)).then_inc(rows_in, 16)
            sp.dma_start(taps[0:4 * TAPS, :], io.dw_w.rearrange("k (b p) -> (k b) p", p=P)).then_inc(rows_in, 16)
            for j in range(6):
                if j >= 3:
                    sp.wait_ge(ada_mm, j - 2)
                sp.dma_start(wada[:, j % 3], io.w_ada[:, 512 * j:512 * j + 512]
                             .rearrange("(c p) n -> p c n", p=P)).then_inc(ada_in[j % 3], 16)
                if j == 2:
                    sp.dma_start(gate_bias[:], io.b_ada[2 * D:3 * D].partition_broadcast(2)).then_inc(gb_in, 16)
                    sp.wait_ge(tab_zero, 1)
                    pad3 = table_pad[:].rearrange("h (r c) -> h r c", c=BW_C)
                    sp.dma_start(pad3[:, 4:19, 8:39], io.rel_bias).then_inc(tab_in, 16)
            sp.wait_ge(tab_in, 16)
            for c in range(QC):
                sp.dma_start(io.table[:, c], table_pad[:, QC - 1 - c:QC - 1 - c + ST]).then_inc(tab_out, 16)
            sp.wait_ge(tab_out, 16 * QC)

        @block.gpsimd
        def _(pool):
            pool.memset(half[:], -0.5).then_inc(half_set, 1)
            pool.wait_ge(half_set, 1)
            pool.wait_ge(sq_done, 10)
            rms_scale(pool, ssum[:], rstd[:], tmp[:], half[:], rms_done, 0)
            for n, (c, k) in enumerate(units):
                if n % 2:
                    pool.wait_ge(hi_done, n + 1)
                    w, at = GROUP_A[c][1], GROUP_A[c][0]
                    pool.tensor_tensor(hT_lo[:, k, at:at + w], hf[:, n % 3, 0:w],
                                       hT_hi[:, k, at:at + w].bitcast(F32), ALU.subtract).then_inc(lo_pool, 1)

        @block.scalar
        def _(act):
            for t in range(10):
                src = io.x_sample[P * t:P * t + P] if t < 8 else io.x_prompt[P * (t - 8):P * (t - 7)]
                act.dma_start(xn[:, t], src).then_inc(x_in[t // 2], 16)
            act.wait_ge(turned, 1)
            act.activation(silu_c[:], psT[:, 0, R_C:R_END], ACT.Silu).then_inc(silu_done, 1)
            for t in range(10):
                act.wait_ge(x_in[t // 2], 32)
                if t:
                    act.wait_ge(sq_done, t)
                act.activation(square[:], xn[:, t], ACT.Square, accum_out=ssum[:, t:t + 1]).then_inc(sq_done, 1)
            for n, (c, k) in enumerate(units):
                w, g = GROUP_A[c][1], 0 if c == 2 else 1
                if n == 0:
                    act.wait_ge(mod_done, 4)
                act.wait_ge(tr_done, n + 1)
                if n >= 3:
                    act.wait_ge(lo_pool if n % 2 == 0 else lo_dve, (n - 3) // 2 + 1)
                act.activation(hf[:, n % 3, 0:w], psX[:, n % 3, 0:w], ACT.Identity,
                               bias=cst.shift[:, k, g:g + 1], scale=cst.scale[:, k, g:g + 1]).then_inc(hf_done, 1)

        @block.vector
        def _(dve):
            dve.memset(table_pad[:], 0.0).then_inc(tab_zero, 1)
            dve.wait_ge(turned, 1)
            dve.wait_ge(silu_done, 1)
            dve.tensor_copy(cst.cols[:, 0:R_C], psT[:, 0, 0:R_C]).then_inc(cols_out, 1)
            dve.wait_ge(turned, 2)
            dve.tensor_copy(cst.taps[:], psT[:, 1, 0:4 * TAPS]).then_inc(cols_out, 1)
            dve.wait_ge(cols_out, 2)
            dve.tensor_scalar(cst.qbias[:], cst.cols[:, 0:4], DH ** -0.5, None, ALU.mult)

            def ada_out_of(j):
                dve.wait_ge(ada_mm, j + 1)
                dve.tensor_copy(ada_row[:, 512 * j:512 * j + 512], psM[0:2, j % 2]).then_inc(ada_out, 1)

            ada_out_of(0)
            ada_out_of(1)
            dve.wait_ge(rms_done, 2)
            for t in range(10):
                dve.tensor_scalar(xn[:, t], xn[:, t], rstd[:, t:t + 1], None, ALU.mult).then_inc(xn_done, 1)
            ada_out_of(2)
            ada_out_of(3)
            dve.wait_ge(ada_turned, 1)
            for dst, b in ((cst.shift, 0), (scale1, KC)):
                bias = cst.cols[:, R_BADA + b:R_BADA + b + KC].unsqueeze(2).to_broadcast([P, KC, 2])
                dve.tensor_tensor(dst[:], psC[:, b:b + KC], bias, ALU.add).then_inc(mod_done, 1)
            dve.wait_ge(mod_done, 2)
            for g in range(2):
                dve.scalar_tensor_tensor(cst.scale[:, :, g], scale1[:, :, g], 1.0,
                                         cst.cols[:, R_RMS:R_RMS + KC], ALU.add, ALU.mult).then_inc(mod_done, 1)
            for n, (c, k) in enumerate(units):
                if n in GATE_OUT_AT:
                    h = GATE_OUT_AT.index(n)
                    at = slice(512 * h, 512 * h + 512)
                    dve.wait_ge(gb_in, 16)
                    dve.wait_ge(ada_mm, 5 + h)
                    dve.tensor_tensor(cst.gate[:, at], psM[0:2, h], gate_bias[:, at], ALU.add).then_inc(gate_done, 1)
                w, at = GROUP_A[c][1], GROUP_A[c][0]
                dve.wait_ge(hf_done, n + 1)
                dve.tensor_copy(hT_hi[:, k, at:at + w], hf[:, n % 3, 0:w]).then_inc(hi_done, 1)
                if n % 2 == 0:
                    dve.wait_ge(hi_done, n + 1)
                    dve.tensor_tensor(hT_lo[:, k, at:at + w], hf[:, n % 3, 0:w],
                                      hT_hi[:, k, at:at + w].bitcast(F32), ALU.subtract).then_inc(lo_dve, 1)

        @block.tensor
        def _(pe):
            pe.wait_ge(ident_in, 16)
            pe.wait_ge(rows_in, 16 * 9)
            pe.transpose(psT[:, 0, 0:R_END], rows[0:R_END, :], cst.ident[0:R_END, 0:R_END]).then_inc(turned, 1)
            pe.transpose(psT[:, 1, 0:4 * TAPS], taps[0:4 * TAPS, :], cst.ident[0:4 * TAPS, 0:4 * TAPS]).then_inc(turned, 1)
            pe.wait_ge(silu_done, 1)
            sc = silu_c[:].rearrange("p (g k) -> p k g", g=2)

            def ada_product(j, k):
                if k == 0:
                    pe.wait_ge(ada_in[j % 3], 16 * (j // 3 + 1))
                    if j >= 2:
                        pe.wait_ge(ada_out, j - 1)
                mm = pe.matmul(psM[0:2, j % 2], sc[:, k, :], wada[:, j % 3, k], start=(k == 0), stop=(k == KC - 1))
                if k == KC - 1:
                    mm.then_inc(ada_mm, 1)

            for j in range(5):
                if j < 4:
                    for k in range(KC):
                        ada_product(j, k)
                if j >= 1:
                    pe.wait_ge(ada_out, j)
                    for m in range(4 * j - 4, 4 * j):
                        tr = pe.transpose(psC[:, m], ada_row[:, P * m:P * m + P], cst.ident[0:2, 0:2])
            tr.then_inc(ada_turned, 1)
            pe.wait_ge(xn_done, 10)
            for n, (c, k) in enumerate(units):
                if n >= 3:
                    pe.wait_ge(hf_done, n - 2)
                if 2 <= n < 2 + 2 * KC:
                    ada_product(4 + (n - 2) // KC, (n - 2) % KC)
                tiles = range(4 * c, 4 * c + GROUP_A[c][1] // P)
                for m, t in enumerate(tiles):
                    tr = pe.transpose(psX[:, n % 3, P * m:P * m + P], xn[:, t, P * k:P * k + P], cst.ident[:])
                tr.then_inc(tr_done, 1)


def turn_group_b(nc, cst, xn, hT_hi, hT_lo):
    with ExitStack() as ctx:
        sem = lambda n: ctx.enter_context(nc.semaphore(n))
        hf = ctx.enter_context(nc.sbuf_tensor("hb_f32", [P, 3, 512], F32))
        psX = ctx.enter_context(nc.psum_tensor("psXb", [P, 3, 512], F32))
        tr_done, hf_done, hi_done, lo_dve, lo_pool = (
            sem("b_tr_done"), sem("b_hf_done"), sem("b_hi_done"), sem("b_lo_dve"), sem("b_lo_pool"))
        units = [(c, k) for c in range(2) for k in range(KC)]
        block = ctx.enter_context(nc.Block())

        @block.tensor
        def _(pe):
            for n, (c, k) in enumerate(units):
                if n >= 3:
                    pe.wait_ge(hf_done, n - 2)
                for m in range(4):
                    tr = pe.transpose(psX[:, n % 3, P * m:P * m + P], xn[:, 4 * c + m, P * k:P * k + P], cst.ident[:])
                tr.then_inc(tr_done, 1)

        @block.scalar
        def _(act):
            for n, (c, k) in enumerate(units):
                act.wait_ge(tr_done, n + 1)
                if n >= 3:
                    act.wait_ge(lo_pool if n % 2 == 0 else lo_dve, (n - 3) // 2 + 1)
                act.activation(hf[:, n % 3], psX[:, n % 3], ACT.Identity, bias=cst.shift[:, k, 1:2],
                               scale=cst.scale[:, k, 1:2]).then_inc(hf_done, 1)

        @block.vector
        def _(dve):
            for n, (c, k) in enumerate(units):
                at = 512 * c
                dve.wait_ge(hf_done, n + 1)
                dve.tensor_copy(hT_hi[:, k, at:at + 512], hf[:, n % 3]).then_inc(hi_done, 1)
                if n % 2 == 0:
                    dve.wait_ge(hi_done, n + 1)
                    dve.tensor_tensor(hT_lo[:, k, at:at + 512], hf[:, n % 3],
                                      hT_hi[:, k, at:at + 512].bitcast(F32), ALU.subtract).then_inc(lo_dve, 1)

        @block.gpsimd
        def _(pool):
            for n, (c, k) in enumerate(units):
                if n % 2:
                    at = 512 * c
                    pool.wait_ge(hi_done, n + 1)
                    pool.tensor_tensor(hT_lo[:, k, at:at + 512], hf[:, n % 3],
                                       hT_hi[:, k, at:at + 512].bitcast(F32), ALU.subtract).then_inc(lo_pool, 1)


def project(nc, io, cst, hT_hi, hT_lo, group, g, xn=None):
    chunks = group
    nch = len(chunks)
    nU = 2 * nch
    ntile = sum(w for _, w, _ in chunks) // P
    half_tiles = ntile // 2
    first = g == 0
    with ExitStack() as ctx:
        sb = lambda n, s, d=F32: ctx.enter_context(nc.sbuf_tensor(f"{n}{g}", s, d))
        sem = lambda n: ctx.enter_context(nc.semaphore(f"{n}{g}"))
        wst = sb("w_stage", [P, 2, KC, P])
        w_hi, w_lo = sb("w_hi", [P, 4, KC, P], F32R), sb("w_lo", [P, 4, KC, P], F32R)
        ostg = sb("out_stage", [P, 4, P * ntile])
        vbias = sb("v_bias", [P, WA])
        ps = ctx.enter_context(nc.psum_tensor(f"psP{g}", [P, nU, 512], F32))
        if first:
            square = sb("square_b", [P, D])
            ssum, tmp, rstd, half = (sb(n, [P, 8]) for n in ("ssum_b", "tmp_b", "rstd_b", "half_b"))
        else:
            UW = PAD + LAT + PAD + CTX + PAD
            OW = LAT + PAD + CTX
            u_in = sb("conv_in", [P, 2, UW])
            acc = sb("conv_acc", [P, 2, OW])
        w_in_sem = [sem("w_in_even"), sem("w_in_odd")]
        vb_in = sem("v_bias_in")
        hi_done, lo_done = sem("w_hi_done"), sem("w_lo_done")
        mm, ev_act, ev_dve = sem("unit_mm"), sem("evac_act"), sem("evac_dve")
        out_d = [sem(f"out_dma{s}_") for s in range(4)]
        if first:
            x_in, sq_done, rms_done, half_set, xn_done = sem("xb_in"), sem("sqb"), sem("rmsb"), sem("halfb"), sem("xnb")
        else:
            u_sem, pad_set, tap_done, conv_out = [sem("u_in0_"), sem("u_in1_")], sem("pad_set"), sem("tap_done"), [sem("cv0_"), sem("cv1_")]

        at = []
        n_mm = 0
        n_act = n_dve = CREDIT
        n_out = [0, 0, 0, 0]
        turn = 0
        for kind, *_, turns in SECTIONS:
            at.append((turn, n_mm, n_act, n_dve, list(n_out)))
            turn += turns
            if kind == "value":
                n_mm += ntile * turns
                n_dve += ntile * turns
            else:
                n_mm += nU * turns
            if kind == "glu":
                n_act += nch * turns
                n_dve += nch * turns
            elif kind != "value":
                n_act += nU * turns
            for s in range(4):
                if kind == "value":
                    n_out[s] += 16 * (3 if first and s % 2 else 1) * turns // 2
                elif kind != "glu" or s % 2 == 0:
                    n_out[s] += 16 * (2 if first else 1) * turns // 2
        end_out = n_out
        block = ctx.enter_context(nc.Block())

        def conv_load(eng, b):
            rows = io.proj[GA0 + P * b:GA0 + P * b + P]
            eng.dma_start(u_in[:, b % 2, PAD:PAD + LAT], rows[:, 0:LAT]).then_inc(u_sem[b % 2], 16)
            eng.dma_start(u_in[:, b % 2, 2 * PAD + LAT:2 * PAD + TOK], rows[:, LAT:TOK]).then_inc(u_sem[b % 2], 16)

        @block.sync
        def _(sp):
            def conv_store(b):
                rows = io.conv[P * b:P * b + P]
                sp.dma_start(rows[:, 0:LAT], acc[:, b % 2, 0:LAT]).then_inc(conv_out[b % 2], 16)
                sp.dma_start(rows[:, LAT:TOK], acc[:, b % 2, LAT + PAD:OW]).then_inc(conv_out[b % 2], 16)

            def conv_turn_over(b):
                sp.wait_ge(tap_done, TAPS * (b + 1))
                conv_store(b)
                if b < 2:
                    conv_load(sp, b + 2)

            sp.dma_start(vbias[:], io.b_in[V0:V0 + WA].partition_broadcast(P)).then_inc(vb_in, 16)
            for (kind, c0, c1, step, turns), (t0, *_) in zip(SECTIONS, at):
                def load(i, guarded):
                    for b, col in ((0, c0), (1, c1)):
                        if guarded:
                            sp.wait_ge(lo_done, 2 * (t0 + i - 1) + b + 1)
                        sp.dma_start(wst[:, b], io.w_in[:, ds(col + step * i, P)].rearrange("(c p) n -> p c n", p=P)
                                     ).then_inc(w_in_sem[b], 16)
                start = 0
                if t0 == 0:
                    load(0, False)
                    start = 1
                if not first and kind == "gates":
                    with sp.Fori(start, 2) as i:
                        load(i, True)
                    conv_turn_over(1)
                    start = 2
                with sp.Fori(start, turns) as i:
                    load(i, True)
                if first:
                    if kind == "qk":
                        sp.dma_start(xn[:], io.x_sample[LAT // 2:LAT].rearrange("(t p) d -> p t d", p=P)
                                     ).then_inc(x_in, 16)
                    continue
                for b in {"z": (0,), "gates": (2, 3)}.get(kind, ()):
                    conv_turn_over(b)
            if not first:
                for s in conv_out:
                    sp.wait_ge(s, 64)

        @block.gpsimd
        def _(pool):
            def split(turn_no, h, units_done):
                for b in range(2):
                    s = 2 * h + b
                    wait_reg(pool, w_in_sem[b], 16 * (turn_no + 1))
                    if units_done is not None and b == 0:
                        wait_reg(pool, mm, units_done)
                    pool.tensor_copy(w_hi[:, s], wst[:, b]).then_inc(hi_done, 1)
                    wait_reg(pool, hi_done, 2 * turn_no + b + 1)
                    pool.tensor_tensor(w_lo[:, s], wst[:, b], w_hi[:, s].bitcast(F32), ALU.subtract).then_inc(lo_done, 1)
            if first:
                pool.memset(half[:], -0.5).then_inc(half_set, 1)
            for (kind, *_, turns), (t0, m0, *_) in zip(SECTIONS, at):
                start = 0
                if t0 == 0:
                    pool.wait_ge(lo_done, 2)
                    split(1, 1, None)
                    start = 1
                if kind == "value":
                    split(t0, 0, m0 - nU)
                    split(t0 + 1, 1, m0)
                    continue
                if kind == "qk":
                    split(t0, 0, m0 - ntile)
                    split(t0 + 1, 1, m0)
                    start = 1
                if first and kind == "gates":
                    pool.wait_ge(half_set, 1)
                    pool.wait_ge(sq_done, 8)
                    rms_scale(pool, ssum[:], rstd[:], tmp[:], half[:], rms_done, 0)
                if turns // 2 > start:
                    with pool.Fori(start, turns // 2) as j:
                        split(t0 + 2 * j, 0, m0 + nU * (2 * j - 1))
                        split(t0 + 2 * j + 1, 1, m0 + nU * 2 * j)

        @block.tensor
        def _(pe):
            def triple(out, w_hi_c, w_lo_c, h_hi_c, h_lo_c, k):
                pe.matmul(out, w_hi_c, h_hi_c, start=(k == 0), stop=False)
                pe.matmul(out, w_hi_c, h_lo_c, start=False, stop=False)
                return pe.matmul(out, w_lo_c, h_hi_c, start=False, stop=(k == KC - 1))

            for (kind, *_, turns), (t0, m0, a0, d0, _) in zip(SECTIONS, at):
                pe.wait_ge(ev_act, a0)
                pe.wait_ge(ev_dve, d0)

                def turn(i, h):
                    if kind == "value":
                        pe.wait_ge(lo_done, 2 * (t0 + i + 1))
                        for t in range(ntile):
                            n = ntile * i + t
                            if n >= nU:
                                pe.wait_ge(ev_dve, d0 + n - nU + 1)
                            for k in range(KC):
                                tok = slice(P * t, P * t + P)
                                wv = [w[:, 2 * h:2 * h + 2, k, :] for w in (w_hi, w_lo)]
                                pe.matmul(ps[:, n % nU, 0:256], hT_hi[:, k, tok], wv[0], start=(k == 0), stop=False)
                                pe.matmul(ps[:, n % nU, 0:256], hT_hi[:, k, tok], wv[1], start=False, stop=False)
                                last = pe.matmul(ps[:, n % nU, 0:256], hT_lo[:, k, tok], wv[0], start=False,
                                                 stop=(k == KC - 1))
                            last.then_inc(mm, 1)
                        return
                    for b in range(2):
                        s = 2 * h + b
                        pe.wait_ge(lo_done, 2 * (t0 + i) + b + 1)
                        for c, (col, w, _) in enumerate(chunks):
                            u = nch * b + c
                            if kind == "glu":
                                pe.wait_ge(ev_dve if b == 0 else ev_act, (d0 if b == 0 else a0) + nch * i + c + 1 - nch)
                            else:
                                pe.wait_ge(ev_act, a0 + nU * i + u + 1 - nU)
                            for k in range(KC):
                                last = triple(ps[:, u, 0:w], w_hi[:, s, k], w_lo[:, s, k],
                                              hT_hi[:, k, col:col + w], hT_lo[:, k, col:col + w], k)
                            last.then_inc(mm, 1)

                if kind == "value":
                    turn(0, 0)
                    turn(1, 1)
                else:
                    with pe.Fori(0, turns // 2) as j:
                        turn(2 * j, 0)
                        turn(2 * j + 1, 1)

        @block.scalar
        def _(act):
            for counter in out_d:
                act.sem_inc(counter, DMA_START)

            def store_rows(s, row):
                w = chunks[0][1] + chunks[1][1]
                act.dma_start(io.proj[ds(row, P), chunks[0][2]:chunks[0][2] + w], ostg[:, s, 0:w]).then_inc(out_d[s], 16)
                if first:
                    act.dma_start(io.proj[ds(row, P), LAT:TOK], ostg[:, s, w:w + CTX]).then_inc(out_d[s], 16)

            per = 16 * (2 if first else 1)
            act.sem_inc(ev_act, CREDIT)
            for (kind, c0, c1, step, turns), (t0, m0, a0, d0, o0) in zip(SECTIONS, at):
                if kind == "value":
                    for i in range(turns):
                        for b in range(2):
                            s, last = 2 * i + b, ntile * i + half_tiles * (b + 1)
                            act.wait_ge(ev_dve, d0 + last)
                            vcol = slice(256 * i, 256 * i + 256)
                            src = ostg[:, s].rearrange("p (t n) -> p t n", n=256)
                            tok0 = chunks[0][2] + P * half_tiles * b
                            n = 3 if first and b else half_tiles
                            act.dma_start(io.v[tok0:tok0 + P * n, vcol].rearrange("(t p) n -> p t n", p=P),
                                          src[:, 0:n]).then_inc(out_d[s], 16)
                            if first and b:
                                act.dma_start(io.v[LAT:TOK, vcol].rearrange("(t p) n -> p t n", p=P),
                                              src[:, 3:5]).then_inc(out_d[s], 16)
                                act.dma_start(io.state_v[:, vcol].rearrange("(t p) n -> p t n", p=P),
                                              src[:, 3:5]).then_inc(out_d[s], 16)
                        if not first and i == 0:
                            act.wait_ge(pad_set, 2)
                            act.wait_ge(out_d[0], DMA_START + at[1][4][0] + 16)
                            act.wait_ge(out_d[2], DMA_START + at[1][4][2])
                            conv_load(act, 0)
                            conv_load(act, 1)
                    continue
                with act.Fori(0, turns // 2) as j:
                    for h in range(2):
                        i = 2 * j + h
                        if kind == "glu":
                            s = 2 * h + 1
                            act.wait_ge(ev_dve, d0 + nch * i - nch)
                            for c, (col, w, _) in enumerate(chunks):
                                wait_reg(act, mm, m0 + nU * i + nch + c + 1)
                                act.activation(ostg[:, s, col:col + w], ps[:, nch + c, 0:w], ACT.Sigmoid,
                                               bias=cst.cols[:, ds(GB0 // P + i, 1)]).then_inc(ev_act, 1)
                            act.wait_ge(ev_dve, d0 + nch * (i + 1))
                            store_rows(2 * h, GA0 + P * i)
                            continue
                        for b in range(2):
                            s = 2 * h + b
                            act.wait_ge(out_d[s], DMA_START + o0[s] + per * j)
                            for c, (col, w, _) in enumerate(chunks):
                                u = nch * b + c
                                wait_reg(act, mm, m0 + nU * i + u + 1)
                                func, scale = ACT.Identity, 1.0
                                bias = cst.cols[:, ds((c0, c1)[b] // P + i, 1)]
                                if kind == "z":
                                    func = ACT.Silu
                                elif kind == "gates":
                                    func = ACT.Sigmoid
                                elif b == 0:
                                    scale, bias = DH ** -0.5, cst.qbias[:, ds(i, 1)]
                                act.activation(ostg[:, s, col:col + w], ps[:, u, 0:w], func, bias=bias,
                                               scale=scale).then_inc(ev_act, 1)
                            act.wait_ge(ev_act, a0 + nU * i + nch * (b + 1))
                            store_rows(s, (c0, c1)[b] + P * i)
            for s in range(4):
                act.wait_ge(out_d[s], DMA_START + end_out[s])

        @block.vector
        def _(dve):
            dve.sem_inc(ev_dve, CREDIT)
            for b in range(2):
                dve.wait_ge(w_in_sem[b], 16)
                dve.tensor_copy(w_hi[:, b], wst[:, b]).then_inc(hi_done, 1)
                dve.wait_ge(hi_done, b + 1)
                dve.tensor_tensor(w_lo[:, b], wst[:, b], w_hi[:, b].bitcast(F32), ALU.subtract).then_inc(lo_done, 1)
            if not first:
                dve.memset(u_in[:, 0], 0.0).then_inc(pad_set, 1)
                dve.memset(u_in[:, 1], 0.0).then_inc(pad_set, 1)
            for (kind, c0, c1, step, turns), (t0, m0, a0, d0, o0) in zip(SECTIONS, at):
                if kind == "glu":
                    with dve.Fori(0, turns // 2) as j:
                        for h in range(2):
                            i = 2 * j + h
                            s = 2 * h
                            dve.wait_ge(out_d[s], DMA_START + (32 if first else 16) * j)
                            for c, (col, w, _) in enumerate(chunks):
                                dve.wait_ge(mm, m0 + nU * i + c + 1)
                                dve.wait_ge(ev_act, a0 + nch * i + c + 1)
                                dve.scalar_tensor_tensor(ostg[:, s, col:col + w], ps[:, c, 0:w],
                                                         cst.cols[:, ds(GA0 // P + i, 1)], ostg[:, s + 1, col:col + w],
                                                         ALU.add, ALU.mult).then_inc(ev_dve, 1)
                if kind == "value":
                    dve.wait_ge(vb_in, 16)
                    for i in range(turns):
                        for t in range(ntile):
                            s = 2 * i + t // half_tiles
                            if t % half_tiles == 0:
                                dve.wait_ge(out_d[s], DMA_START + o0[s])
                            n = ntile * i + t
                            dve.wait_ge(mm, m0 + n + 1)
                            dst = ostg[:, s].rearrange("p (t n) -> p t n", n=256)[:, t % half_tiles]
                            dve.tensor_tensor(dst, ps[:, n % nU, 0:256], vbias[:, 256 * i:256 * i + 256],
                                              ALU.add).then_inc(ev_dve, 1)
            if first:
                for t in range(8):
                    dve.wait_ge(x_in, 16)
                    dve.tensor_tensor_reduce(square[:], xn[:, t], xn[:, t], 1.0, 0.0, ALU.mult, ALU.add,
                                             ssum[:, t:t + 1]).then_inc(sq_done, 1)
                    dve.wait_ge(sq_done, t + 1)
                dve.wait_ge(rms_done, 2)
                for t in range(8):
                    dve.tensor_scalar(xn[:, t], xn[:, t], rstd[:, t:t + 1], None, ALU.mult).then_inc(xn_done, 1)
                return
            for b in range(4):
                dve.wait_ge(u_sem[b % 2], 32 * (b // 2 + 1))
                if b >= 2:
                    dve.wait_ge(conv_out[b % 2], 32)
                for k in range(TAPS):
                    src, dst = u_in[:, b % 2, k:k + OW], acc[:, b % 2]
                    tap = cst.taps[:, 4 * k + b:4 * k + b + 1]
                    n = TAPS * b + k
                    if k == 0:
                        op = dve.tensor_scalar(dst, src, tap, cst.cols[:, R_DWB + b:R_DWB + b + 1], ALU.mult, ALU.add)
                    else:
                        dve.wait_ge(tap_done, n)
                        op = dve.scalar_tensor_tensor(dst, src, tap, dst, ALU.mult, ALU.add)
                    op.then_inc(tap_done, 1)



QR, QC = 8, 16
BANDS = [(0, 12, 0), (4, 16, 1), (12, 16, 1), (20, 12, 2)]
SETS = [(0, 24, 0), (8, 32, 1), (24, 32, 1), (40, 24, 2)]
ROW_TYPES = [(4, 12), (0, 16), (0, 12)]
COL_TYPES = [(8, 24), (0, 32), (0, 24)]
BW_R, BW_C = 16, 47
BT = 24 * BW_C
ST = (QR - 1) * BW_C + BW_R * BW_C
MASKED = -1e30
LT = 16
TPH = LT + CTX // P
TPP = 2 * TPH
RED = 2 * LT + CTX // P
NG = 3
KW = TOK + CTX
T_OFF, _o = {}, 0
for _r in range(3):
    for _c in range(3):
        T_OFF[_r, _c] = _o
        _o += ROW_TYPES[_r][1] * COL_TYPES[_c][1]
T_W = _o


def window_masks():
    q = np.arange(P)
    rm, cm = np.zeros((3, P, 16), np.float32), np.zeros((3, P, 32), np.float32)
    for (kr0, nr, rt), a in zip(BANDS, range(4)):
        r = QR * a + q // QC
        lo = np.clip(r - WIN_R // 2, 0, ROWS - WIN_R)[:, None]
        kr = kr0 + np.arange(nr)[None]
        rm[rt, :, :nr] = np.where((kr >= lo) & (kr < lo + WIN_R), 0, MASKED)
    for (kc0, w, ct), b in zip(SETS, range(4)):
        c = QC * b + q % QC
        lo = np.clip(c - WIN_C // 2, 0, GRID - WIN_C)[:, None]
        kc = kc0 + np.arange(w)[None]
        cm[ct, :, :w] = np.where((kc >= lo) & (kc < lo + WIN_C), 0, MASKED)
    return rm, cm


def attend(nc, io, cst):
    with ExitStack() as ctx:
        sb = lambda n, s, d=F32: ctx.enter_context(nc.sbuf_tensor(n, s, d))
        ps = lambda n, s: ctx.enter_context(nc.psum_tensor(n, s, F32))
        sem = lambda n: ctx.enter_context(nc.semaphore(n))
        q_raw, k_raw, ck_raw = sb("q_raw", [P, TOK]), sb("k_raw", [P, KW]), sb("ck_raw", [P, 2, P])
        q_sp, k_hi, k_lo = sb("q_split", [P, 2, TOK], F32R), sb("k_hi", [P, 2, KW], F32R), sb("k_lo", [P, 2, KW], F32R)
        v_win, v_ctx = sb("v_win", [P, 2, 4, 8, DH + 1]), sb("v_ctx", [P, 2, 4, DH + 1])
        window, win_c, tables = sb("bias_window", [P, BW_R * BW_C]), sb("bias_cols", [P, 3, 512]), sb("bias", [P, 2, T_W])
        rmask, cmask = sb("row_mask", [P, 3, 16]), sb("col_mask", [P, 3, 32])
        s_sb, p_sb, pT = sb("scores", [P, 2, 512]), sb("probs", [P, 2, 768]), sb("probs_t", [P, 2, 6, P])
        stat = sb("stat", [P, 4, 8])
        o_sb, inv = sb("o_pair", [P, TPH, 2, DH + 1]), sb("inv_sums", [P, NG, 2])
        o_norm = sb("o_normed", [P, 2, NG, P])
        z_sb, y_sb, sk_sb = sb("z_pair", [P, TOK]), sb("y_pair", [P, TOK]), sb("sk", [P, 2, DH])
        ps_win, ps_ctx = [ps("ps_win0", [P, 512]), ps("ps_win1", [P, 512])], [ps("ps_ctx0", [P, 512]), ps("ps_ctx1", [P, 512])]
        ps_tw, ps_tc, ps_o, ps_y = ps("ps_tw", [P, 4, P]), ps("ps_tc", [P, 4, P]), ps("ps_o", [P, 512]), ps("ps_y", [P, 512])
        qk_in, v_in, win_in, mask_in, z_in = sem("qk_in"), [sem("v_in0"), sem("v_in1")], sem("win_in"), sem("mask_in"), sem("z_in")
        ck_turned, ck_done, sk_done, sk_out = sem("ck_turned"), sem("ck_done"), sem("sk_done"), sem("sk_out")
        hi_done, lo_done, col_done, tab_done = sem("qk_hi"), sem("qk_lo"), sem("cols_done"), sem("tables_done")
        s_mm, red, negmax, exp_done = sem("scores_mm"), sem("maxima"), sem("negmax"), sem("exp_done")
        tr_done, pt_win, pt_ctx, pv_done = sem("probs_turned"), sem("pt_win"), sem("pt_ctx"), sem("pv_done")
        ones_set, inv_done, normed, o_done, y_turned, y_done, y_out = sem("ones_set_v"), sem("inv_done"), sem("o_normed"), sem("o_done"), sem("y_turned"), sem("y_done"), sem("y_out")

        TILES = [(u, i) for u in range(2) for i in range(TPH)]
        red_before = [min(i, LT) * 2 + max(i - LT, 0) for i in range(TPH + 1)]
        GROUPS = TPH // NG
        PREP_AT = 4
        SPLIT_AT = 5

        def keys_of(buf, u, i):
            if i >= LT:
                return None, buf[:, u, LAT:TOK]
            kr0, nr, _ = BANDS[i // 4]
            kc0, w, _ = SETS[i % 4]
            grid = buf[:, u, 0:LAT].rearrange("p (r c) -> p r c", c=GRID)
            return grid[:, kr0:kr0 + nr, kc0:kc0 + w], buf[:, u, TOK:KW]

        def n_keys(i):
            return 0 if i >= LT else BANDS[i // 4][1] * SETS[i % 4][1]

        block = ctx.enter_context(nc.Block())

        @block.sync
        def _(sp):
            sp.sem_inc(y_out, DMA_START)
            sp.dma_start(rmask[:], io.row_mask.rearrange("t p r -> p t r")).then_inc(mask_in, 16)
            sp.dma_start(cmask[:], io.col_mask.rearrange("t p r -> p t r")).then_inc(mask_in, 16)

            def load_qk(n, free):
                if free:
                    sp.wait_ge(lo_done, 2 * n)
                    sp.wait_ge(sk_done, n)
                for half in range(2):
                    part = slice(DH * half, DH * half + DH)
                    sp.dma_start(q_raw[part], io.proj[ds(Q0 + n * DH, DH)]).then_inc(qk_in, 16)
                    sp.dma_start(k_raw[part, 0:TOK], io.proj[ds(K0 + n * DH, DH)]).then_inc(qk_in, 16)
                    sp.dma_start(ck_raw[:, :, part], io.cache_k[:, ds(n * DH, DH)].rearrange("(t p) d -> p t d", p=P)
                                 ).then_inc(qk_in, 16)

            def load_v(n, u, pv_before):
                if pv_before is not None:
                    sp.wait_ge(pv_done, START + pv_before)
                for b, (kc0, w, _) in enumerate(SETS):
                    for r in range(4):
                        src = io.v[0:LAT].rearrange("(rb r c) d -> r c rb d", r=4, c=GRID)[r, kc0:kc0 + w, :, ds(n * DH, DH)]
                        sp.dma_start(v_win[w * r:w * r + w, u, b, :, 0:DH], src).then_inc(v_in[u], 16)
                sp.dma_start(v_ctx[:, u, 0:2, 0:DH], io.cache_v[:, ds(n * DH, DH)].rearrange("(t p) d -> p t d", p=P)
                             ).then_inc(v_in[u], 16)
                sp.dma_start(v_ctx[:, u, 2:4, 0:DH], io.v[LAT:TOK, ds(n * DH, DH)].rearrange("(t p) d -> p t d", p=P)
                             ).then_inc(v_in[u], 16)

            def load_window(n, free):
                if free:
                    sp.wait_ge(col_done, 3 * n)
                for r in range(QR):
                    at = (QR - 1 - r) * BW_C
                    sp.dma_start(window[QC * r:QC * r + QC], io.table[ds(n, 1), :, at:at + BW_R * BW_C]
                                 .rearrange("h q x -> (h q) x")).then_inc(win_in, 16)

            load_window(0, False)
            load_qk(0, False)
            load_v(0, 0, None)

            load_qk(1, True)

            def body(hp, last):
                load_window(2 * hp + 1, True)
                load_v(2 * hp + 1, 1, hp * TPP)
                sp.wait_ge(sk_done, 2 * hp + 1)
                sp.dma_start(io.state_k[:, ds(2 * hp * DH, DH)].rearrange("(t p) d -> p t d", p=P), sk_sb[:]).then_inc(sk_out, 16)
                sp.wait_ge(y_done, START + hp * TPH)
                sp.dma_start(z_sb[:], io.proj[ds(ZA0 + hp * P, P)]).then_inc(z_in, 16)
                if not last:
                    load_window(2 * hp + 2, True)
                    load_qk(2 * hp + 2, True)
                    load_v(2 * hp + 2, 0, hp * TPP + TPH)
                sp.wait_ge(sk_done, 2 * hp + 2)
                sp.dma_start(io.state_k[:, ds((2 * hp + 1) * DH, DH)].rearrange("(t p) d -> p t d", p=P), sk_sb[:]).then_inc(sk_out, 16)
                if not last:
                    load_qk(2 * hp + 3, True)
                sp.wait_ge(y_done, START + hp * TPH + TPH)
                sp.dma_start(io.ya[ds(hp * P, P)], y_sb[:]).then_inc(y_out, 16)

            with sp.Fori(0, HEADS // 2 - 1) as hp:
                body(hp, False)
            body(HEADS // 2 - 1, True)
            sp.wait_ge(y_out, DMA_START + 16 * HEADS // 2)
            sp.wait_ge(sk_out, 16 * HEADS)

        @block.tensor
        def _(pe):
            for counter in (pv_done, y_turned):
                pe.sem_inc(counter, START)

            def turn_keys(n, y_before):
                pe.wait_ge(qk_in, 96 * n + 96)
                pe.wait_ge(y_done, START + y_before)
                pe.wait_ge(ck_done, n)
                pe.wait_ge(sk_done, n)
                for t in range(2):
                    pe.transpose(ps_y[:, P * t:P * t + P], ck_raw[:, t], cst.ident[:])
                for t in range(2):
                    tr = pe.transpose(ps_y[:, 256 + DH * t:256 + DH * t + DH], k_raw[0:DH, LAT + P * t:LAT + P * t + P],
                                      cst.ident[0:DH, 0:DH])
                tr.then_inc(ck_turned, 1)

            def scores(u, i, base, m, parts_before):
                if i == 0:
                    pe.wait_ge(lo_done, parts_before + 2 * u + 2)
                q = q_sp[:, u, P * i:P * i + P]
                (w_hi, c_hi), (w_lo, c_lo) = keys_of(k_hi, u, i), keys_of(k_lo, u, i)
                nk = n_keys(i)
                if nk:
                    pe.matmul(ps_win[m % 2][:, 0:nk], q, w_hi, start=True, stop=False)
                    pe.matmul(ps_win[m % 2][:, 0:nk], q, w_lo, start=False, stop=True)
                pe.matmul(ps_ctx[m % 2][:, 0:CTX], q, c_hi, start=True, stop=False)
                pe.matmul(ps_ctx[m % 2][:, 0:CTX], q, c_lo, start=False, stop=True).then_inc(s_mm, 1)

            def turn_probs(u, i, base, m):
                pe.wait_ge(exp_done, base + m + 1)
                pe.wait_ge(pt_win, START + base + m)
                pe.wait_ge(pt_ctx, START + base + m)
                if i < LT:
                    w4, nb = 4 * SETS[i % 4][1], BANDS[i // 4][1] // 4
                    for j in range(nb):
                        pe.transpose(ps_tw[0:w4, j], p_sb[:, m % 2, w4 * j:w4 * j + w4], cst.ident[:])
                for j in range(2):
                    tr = pe.transpose(ps_tc[:, j], p_sb[:, m % 2, 512 + P * j:512 + P * j + P], cst.ident[:])
                tr.then_inc(tr_done, 1)

            def weigh_values(u, i, base, m, v_count):
                if i == 0:
                    pe.wait_ge(v_in[u], v_count)
                if m == TPP - 1:
                    pe.wait_ge(pt_win, START + base + m + 1)
                    pe.wait_ge(pt_ctx, START + base + m + 1)
                pe.wait_ge(o_done, START + base + m)
                nb = 0
                if i < LT:
                    w4, nb, rb0 = 4 * SETS[i % 4][1], BANDS[i // 4][1] // 4, BANDS[i // 4][0] // 4
                    for j in range(nb):
                        pe.matmul(ps_o[:, 0:DH + 1], pT[0:w4, m % 2, j], v_win[0:w4, u, i % 4, rb0 + j],
                                  start=(j == 0), stop=False)
                for j in range(2):
                    mm = pe.matmul(ps_o[:, 0:DH + 1], pT[:, m % 2, 4 + j], v_ctx[:, u, (2 if i >= LT else 0) + j],
                                   start=(nb == 0 and j == 0), stop=(j == 1))
                mm.then_inc(pv_done, 1)

            def turn_out(g, g_base, y_base, keys):
                pe.wait_ge(sk_done, keys)
                pe.wait_ge(normed, g_base + g + 1)
                pe.wait_ge(y_done, START + y_base + NG * g)
                for t in range(NG):
                    tr = pe.transpose(ps_y[:, P * t:P * t + P], o_norm[:, g % 2, t], cst.ident[:])
                tr.then_inc(y_turned, 1)

            pe.wait_ge(ones_set, 2)
            turn_keys(0, 0)

            def body(hp, last):
                base = hp * TPP
                for m in (0, 1):
                    scores(*TILES[m], base, m, hp * 4)
                for m, (u, i) in enumerate(TILES):
                    turn_probs(u, i, base, m)
                    if m + 2 < TPP:
                        scores(*TILES[m + 2], base, m + 2, hp * 4)
                    if m >= 1:
                        weigh_values(*TILES[m - 1], base, m - 1, 288 * (hp + 1))
                    if i == PREP_AT and not (last and u == 1):
                        turn_keys(2 * hp + u + 1, hp * TPH)
                    if u == 1 and i >= 5 and i % NG == 2:
                        turn_out(i // NG - 1, hp * GROUPS, hp * TPH, 2 * hp + (2 if last else 3))
                weigh_values(*TILES[-1], base, TPP - 1, 288 * (hp + 1))
                turn_out(GROUPS - 1, hp * GROUPS, hp * TPH, 2 * hp + (2 if last else 3))

            with pe.Fori(0, HEADS // 2 - 1) as hp:
                body(hp, False)
            body(HEADS // 2 - 1, True)

        def split_low(eng, n, u):
            wait_reg(eng, hi_done, n + 1)
            low = slice(DH, P)
            for a in range(4):
                src = q_raw[low, 512 * a:512 * a + 512].rearrange("p (r b c) -> p b r c", r=QR, b=4)
                dst = q_sp[low, u, 512 * a:512 * a + 512].rearrange("p (b r c) -> p b r c", b=4, r=QR)
                for b in range(4):
                    eng.tensor_tensor(dst[:, b], src[:, b], dst[:, b].bitcast(F32), ALU.subtract)
            eng.tensor_tensor(q_sp[low, u, LAT:TOK], q_raw[low, LAT:TOK], q_sp[low, u, LAT:TOK].bitcast(F32),
                              ALU.subtract).then_inc(lo_done, 1)
            wait_reg(eng, lo_done, 2 * n + 1)
            eng.tensor_tensor(k_lo[:, u], k_raw[:], k_hi[:, u].bitcast(F32), ALU.subtract).then_inc(lo_done, 1)

        @block.vector
        def _(dve):
            for counter in (y_done, pt_win, negmax):
                dve.sem_inc(counter, START)

            def split_high(n, u, part):
                if part == 0:
                    wait_reg(dve, qk_in, 96 * n + 96)
                if part < 4:
                    src = q_raw[:, 512 * part:512 * part + 512].rearrange("p (r b c) -> p b r c", r=QR, b=4)
                    dst = q_sp[:, u, 512 * part:512 * part + 512].rearrange("p (b r c) -> p b r c", b=4, r=QR)
                    dve.tensor_copy(dst, src)
                    at = slice(512 * part, 512 * part + 512)
                    dve.tensor_copy(k_hi[:, u, at], k_raw[:, at])
                else:
                    wait_reg(dve, ck_done, n + 1)
                    dve.tensor_copy(q_sp[:, u, LAT:TOK], q_raw[:, LAT:TOK])
                    dve.tensor_copy(k_hi[:, u, LAT:KW], k_raw[:, LAT:KW]).then_inc(hi_done, 1)

            def soften(u, i, base, m, rbase, ready):
                nk, st = n_keys(i), stat[:, m % 4]
                if i == 0:
                    wait_reg(dve, tab_done, ready)
                wait_reg(dve, s_mm, base + m + 1)
                if nk:
                    off = T_OFF[BANDS[i // 4][2], SETS[i % 4][2]]
                    dve.tensor_tensor_reduce(s_sb[:, m % 2, 0:nk], ps_win[m % 2][:, 0:nk], tables[:, u, off:off + nk],
                                             1.0, -3e38, ALU.add, ALU.max, st[:, 0:1]).then_inc(red, 1)
                dve.reduce_max(st[:, 1:2], ps_ctx[m % 2][:, 0:CTX], AX_X).then_inc(red, 1)

            def negate_max(u, i, base, m, rbase):
                nk, st = n_keys(i), stat[:, m % 4]
                wait_reg(dve, red, rbase + u * RED + red_before[i + 1])
                if nk:
                    dve.tensor_scalar(st[:, 2:3], st[:, 0:1], st[:, 1:2], -1.0, ALU.max, ALU.mult).then_inc(negmax, 1)
                else:
                    dve.tensor_scalar(st[:, 2:3], st[:, 1:2], -1.0, None, ALU.mult).then_inc(negmax, 1)

            def copy_window(u, i, base, m):
                if m >= 2:
                    wait_reg(dve, pv_done, START + base + m - 1)
                wait_reg(dve, tr_done, base + m + 1)
                w4, nb = (4 * SETS[i % 4][1], BANDS[i // 4][1] // 4) if i < LT else (P, 0)
                if nb:
                    dve.tensor_copy(pT[0:w4, m % 2, 0:nb], ps_tw[0:w4, 0:nb]).then_inc(pt_win, 1)
                else:
                    dve.sem_inc(pt_win, 1)

            def invert(g, o_ready):
                wait_reg(dve, o_done, START + o_ready)
                dve.reciprocal(inv[:], o_sb[:, NG * g:NG * g + NG, :, DH]).then_inc(inv_done, 1)

            def norm_out(g, g_base):
                o, out = o_sb[:, NG * g:NG * g + NG, :, 0:DH], o_norm[:, g % 2].rearrange("p t (u d) -> p t u d", u=2)
                wait_reg(dve, inv_done, g_base + g + 1)
                dve.tensor_tensor(out, o, inv[:].unsqueeze(3).to_broadcast([P, NG, 2, DH]), ALU.mult).then_inc(normed, 1)

            def gate_out(i, g_base, z_ready):
                if i % NG == 0:
                    wait_reg(dve, y_turned, START + g_base + i // NG + 1)
                o_t = ps_y[:, P * (i % NG):P * (i % NG) + P]
                if i == 0:
                    wait_reg(dve, z_in, z_ready)
                    wait_reg(dve, y_out, DMA_START + z_ready - 16)
                if i >= LT:
                    at = slice(LAT + P * (i - LT), LAT + P * (i - LT) + P)
                    dve.tensor_tensor(y_sb[:, at], o_t, z_sb[:, at], ALU.mult).then_inc(y_done, 1)
                    return
                a, b = i // 4, i % 4
                y, z = (x[:, 512 * a:512 * a + 512].rearrange("p (r b c) -> p b r c", r=QR, b=4)[:, b] for x in (y_sb, z_sb))
                dve.tensor_tensor(y, o_t.rearrange("p (r c) -> p r c", c=QC), z, ALU.mult).then_inc(y_done, 1)

            for part in range(5):
                split_high(0, 0, part)
            split_low(dve, 0, 0)

            def body(hp, last):
                base, rbase = hp * TPP, hp * 2 * RED
                for m in (0, 1):
                    soften(*TILES[m], base, m, rbase, 2 * hp + 1)
                    negate_max(*TILES[m], base, m, rbase)
                for m, (u, i) in enumerate(TILES):
                    copy_window(u, i, base, m)
                    if m + 2 < TPP:
                        u2, i2 = TILES[m + 2]
                        soften(u2, i2, base, m + 2, rbase, 2 * hp + u2 + 1)
                    if u == 1 and i >= 6:
                        gate_out(i - 6, hp * GROUPS, 16 * (hp + 1))
                    g, last_of_group = i // NG - 1, i % NG == 1
                    if u == 1 and g >= 0 and last_of_group:
                        invert(g, base + m - 1)
                    if m + 2 < TPP:
                        negate_max(u2, i2, base, m + 2, rbase)
                    if u == 1 and g >= 0 and last_of_group:
                        norm_out(g, hp * GROUPS)
                    if SPLIT_AT <= i < SPLIT_AT + 5 and not (last and u == 1):
                        split_high(2 * hp + u + 1, 1 - u, i - SPLIT_AT)
                invert(GROUPS - 1, base + TPP)
                norm_out(GROUPS - 1, hp * GROUPS)
                for i in range(TPH - 6, TPH):
                    gate_out(i, hp * GROUPS, 16 * (hp + 1))

            with dve.Fori(0, HEADS // 2 - 1) as hp:
                body(hp, False)
            body(HEADS // 2 - 1, True)

        @block.scalar
        def _(act):
            for counter in (pt_ctx, o_done):
                act.sem_inc(counter, START)

            def copy_keys(n):
                wait_reg(act, ck_turned, n + 1)
                act.activation(k_raw[:, TOK:KW], ps_y[:, 0:CTX], ACT.Copy).then_inc(ck_done, 1)
                wait_reg(act, sk_out, 16 * n)
                act.activation(sk_sb[:], ps_y[:, 256:256 + P].rearrange("p (t d) -> p t d", t=2), ACT.Copy).then_inc(sk_done, 1)

            def exponents(u, i, base, m):
                nk, st = n_keys(i), stat[:, m % 4]
                wait_reg(act, negmax, START + base + m + 1)
                if nk:
                    act.activation(p_sb[:, m % 2, 0:nk], s_sb[:, m % 2, 0:nk], ACT.Exp, bias=st[:, 2:3])
                act.activation(p_sb[:, m % 2, 512:768], ps_ctx[m % 2][:, 0:CTX], ACT.Exp, bias=st[:, 2:3]).then_inc(exp_done, 1)

            def copy_context(u, i, base, m):
                wait_reg(act, tr_done, base + m + 1)
                act.activation(pT[:, m % 2, 4:6], ps_tc[:, 0:2], ACT.Copy).then_inc(pt_ctx, 1)

            def copy_out(u, i, base, m):
                wait_reg(act, pv_done, START + base + m + 1)
                act.activation(o_sb[:, i, u], ps_o[:, 0:DH + 1], ACT.Copy).then_inc(o_done, 1)

            copy_keys(0)

            def body(hp, last):
                base = hp * TPP
                wait_reg(act, y_turned, START + hp * GROUPS)
                exponents(*TILES[0], base, 0)
                for m, (u, i) in enumerate(TILES):
                    if m + 1 < TPP:
                        exponents(*TILES[m + 1], base, m + 1)
                    copy_context(u, i, base, m)
                    if m >= 1:
                        copy_out(*TILES[m - 1], base, m - 1)
                    if i == PREP_AT and not (last and u == 1):
                        copy_keys(2 * hp + u + 1)
                copy_out(*TILES[-1], base, TPP - 1)

            with act.Fori(0, HEADS // 2 - 1) as hp:
                body(hp, False)
            body(HEADS // 2 - 1, True)

        @block.gpsimd
        def _(pool):
            def bias_tables(n, u, s_before):
                wait_reg(pool, win_in, 128 * n + 128)
                wait_reg(pool, negmax, START + s_before)
                wait_reg(pool, tab_done, n)
                win = window[:].rearrange("p (r c) -> p r c", c=BW_C)
                for ct, (c0, w) in enumerate(COL_TYPES):
                    pool.tensor_tensor(win_c[:, ct, 0:16 * w].rearrange("p (r c) -> p r c", c=w), win[:, :, c0:c0 + w],
                                       cmask[:, ct, 0:w].unsqueeze(1).to_broadcast([P, 16, w]), ALU.add).then_inc(col_done, 1)
                wait_reg(pool, col_done, 3 * n + 3)
                for (rt, ct), off in T_OFF.items():
                    (r0, nr), w = ROW_TYPES[rt], COL_TYPES[ct][1]
                    op = pool.tensor_tensor(tables[:, u, off:off + nr * w].rearrange("p (r c) -> p r c", c=w),
                                            win_c[:, ct, w * r0:w * (r0 + nr)].rearrange("p (r c) -> p r c", c=w),
                                            rmask[:, rt, 0:nr].unsqueeze(2).to_broadcast([P, nr, w]), ALU.add)
                op.then_inc(tab_done, 1)

            def prepare(n, u, s_before):
                bias_tables(n, u, s_before)
                wait_reg(pool, tab_done, n + 1)
                split_low(pool, n, u)

            pool.memset(v_win[:, :, :, :, DH:DH + 1], 1.0).then_inc(ones_set, 1)
            pool.memset(v_ctx[:, :, :, DH:DH + 1], 1.0).then_inc(ones_set, 1)
            pool.wait_ge(mask_in, 32)
            bias_tables(0, 0, 0)
            with pool.Fori(0, HEADS // 2 - 1) as hp:
                prepare(2 * hp + 1, 1, hp * TPP)
                prepare(2 * hp + 2, 0, hp * TPP + TPH)
            prepare(HEADS - 1, 1, (HEADS // 2 - 1) * TPP)


CH = 256
NCH = TOK // CH


WG = 256


def split_weights(nc, srcs, stage, w_hi, w_lo, w_in, w_hi_done, w_lo_done):
    def load(sp, c):
        if c >= 2:
            sp.wait_ge(w_lo_done, c - 1)
        at = 0
        for src in srcs:
            n = src.shape[0] // P
            sp.dma_start(stage[:, c % 2, at:at + n], src[:, WG * c:WG * c + WG].rearrange("(k p) n -> p k n", p=P)
                         ).then_inc(w_in[c % 2], 16)
            at += n

    def high(act, c):
        act.wait_ge(w_in[c % 2], 16 * len(srcs) * (c // 2 + 1))
        act.activation(w_hi[:, :, WG * c:WG * c + WG], stage[:, c % 2], ACT.Copy).then_inc(w_hi_done, 1)

    def low(dve, c):
        dve.wait_ge(w_hi_done, c + 1)
        cols = slice(WG * c, WG * c + WG)
        dve.tensor_tensor(w_lo[:, :, cols], stage[:, c % 2], w_hi[:, :, cols].bitcast(F32), ALU.subtract).then_inc(w_lo_done, 1)
    return load, high, low


def merge(nc, io, cst):
    with ExitStack() as ctx:
        sb = lambda n, s, d=F32: ctx.enter_context(nc.sbuf_tensor(n, s, d))
        sem = lambda n: ctx.enter_context(nc.semaphore(n))
        stage, w_hi, w_lo = sb("wp_stage", [P, 2, 8, WG]), sb("wp_hi", [P, 8, D], F32R), sb("wp_lo", [P, 8, D], F32R)
        ya, cv, zb = (sb(n, [P, 2, 4, CH]) for n in ("ya_in", "cv_in", "zb_in"))
        gates = sb("gates_in", [P, 2, 2 * KC, CH])
        y_hi, y_lo = sb("y_hi", [P, 2, 8, CH], F32R), sb("y_lo", [P, 2, 8, CH], F32R)
        act_sb, yb = sb("ln_silu", [P, 4, CH]), sb("yb", [P, 4, CH])
        normed = sb("normed", [P, 2, WB])
        bn, mv, var_eps, rstd, shift, half = (sb(n, [P, 2, w]) for n, w in (
            ("bn", 6), ("mv", 2), ("var_eps", 1), ("ln_rstd", 1), ("ln_shift", 1), ("ln_half", 1)))
        gated, m_sb = sb("gated", [P, 2, 2, CH]), sb("m_out", [P, 2, KC, CH])
        ps_o = ctx.enter_context(nc.psum_tensor("ps_proj", [P, 4, 2, CH], F32))
        ps_n = ctx.enter_context(nc.psum_tensor("ps_norm", [P, 2, WB], F32))
        ps_b = ctx.enter_context(nc.psum_tensor("ps_back", [P, 4, CH], F32))
        w_in, w_hid, w_lod = [sem("wp_in0"), sem("wp_in1")], sem("wp_hid"), sem("wp_lod")
        s_in, g_in = [sem("s_in0"), sem("s_in1")], [sem("g_in0"), sem("g_in1")]
        t_in, bn_done, mv_done, rs_done, sh_done, n_done = (sem(n) for n in ("t_in", "bn_done", "mv_done", "rs_done", "sh_done", "n_done"))
        t_back, silu_done, yb_done, hi_done, lo_done, half_set = (sem(n) for n in ("t_back", "silu_m", "yb_done", "y_hid", "y_lod", "half_m"))
        mm, gated_done, m_done, m_out = sem("proj_mm"), sem("gated_done"), sem("m_done"), [sem("m_out0"), sem("m_out1")]
        load_w, high_w, low_w = split_weights(nc, (io.w_proj_a, io.w_proj_b), stage, w_hi, w_lo, w_in, w_hid, w_lod)
        GD0 = 4
        block = ctx.enter_context(nc.Block())

        def chunks(eng, body):
            with eng.Fori(0, NCH // 2) as t:
                body(2 * t, t, 0, False)
                body(2 * t + 1, t, 1, False)
            body(NCH - 1, NCH // 2, 0, True)

        @block.sync
        def _(sp):
            def small(j, par):
                for src, dst in ((io.conv, cv), (io.ya, ya), (io.proj[ZB0:ZB0 + WB], zb)):
                    sp.dma_start(dst[:, par], src[:, ds(CH * j, CH)].rearrange("(b p) t -> p b t", p=P)).then_inc(s_in[par], 16)

            def big(j, par):
                sp.dma_start(gates[:, par], io.proj[G0:D_IN, ds(CH * j, CH)].rearrange("(b p) t -> p b t", p=P)
                             ).then_inc(g_in[par], 16)

            small(0, 0)
            load_w(sp, 0)
            load_w(sp, 1)
            big(0, 0)
            load_w(sp, 2)
            load_w(sp, 3)
            small(1, 1)

            def body(j, par):
                wait_reg(sp, gated_done, GD0 + 8 * j)
                big(j + 1, 1 - par)
                wait_reg(sp, lo_done, 2 * j + 2)
                small(j + 2, par)

            with sp.Fori(0, NCH // 2 - 1) as t:
                body(2 * t, 0)
                body(2 * t + 1, 1)
            body(NCH - 3, 0)
            sp.wait_ge(gated_done, GD0 + 8 * (NCH - 2))
            big(NCH - 1, 0)

        @block.gpsimd
        def _(pool):
            pool.memset(half[:], -0.5).then_inc(half_set, 1)
            pool.wait_ge(half_set, 1)

            def norm_and_split(j, jh, par):
                wait_reg(pool, mv_done, 2 * j + 2)
                pool.tensor_scalar(var_eps[:], mv[:, :, 1:2], EPS, None, ALU.add).then_inc(rs_done, 1)
                wait_reg(pool, rs_done, 2 * j + 1)
                pool.tensor_tensor(rstd[:], var_eps[:], half[:], ALU.pow).then_inc(rs_done, 1)
                wait_reg(pool, hi_done, 2 * j + 1)
                pool.tensor_tensor(y_lo[:, par, 0:4], ya[:, par], y_hi[:, par, 0:4].bitcast(F32), ALU.subtract).then_inc(lo_done, 1)
                wait_reg(pool, hi_done, 2 * j + 2)
                pool.tensor_tensor(y_lo[:, par, 4:8], yb[:], y_hi[:, par, 4:8].bitcast(F32), ALU.subtract).then_inc(lo_done, 1)

            norm_and_split(0, 0, 0)
            chunks(pool, lambda j, jh, par, last: None if last else norm_and_split(j + 1, jh, 1 - par))

        @block.tensor
        def _(pe):
            def turn_in(j, jh, par):
                pe.wait_ge(s_in[par], 48 * (jh + 1))
                pe.wait_ge(n_done, 2 * j)
                for t in range(2):
                    for b in range(4):
                        tr = pe.transpose(ps_n[:, t, P * b:P * b + P], cv[:, par, b, P * t:P * t + P], cst.ident[:])
                tr.then_inc(t_in, 1)

            def turn_back(j):
                pe.wait_ge(n_done, 2 * j + 2)
                pe.wait_ge(silu_done, 4 * j)
                for b in range(4):
                    for t in range(2):
                        tr = pe.transpose(ps_b[:, b, P * t:P * t + P], normed[:, t, P * b:P * b + P], cst.ident[:])
                tr.then_inc(t_back, 1)

            def next_half(jh, par):
                return jh + par

            turn_in(0, 0, 0)
            turn_back(0)

            def body(j, jh, par, last):
                for n in range(16):
                    half_no, o = n // 4 % 2, 4 * (n // 8) + n % 4
                    if n % 4 == 0 and n < 8:
                        pe.wait_ge(lo_done, 2 * j + 1 + half_no)
                    if half_no == 0:
                        pe.wait_ge(w_lod, P * o // WG + 1)
                        pe.wait_ge(gated_done, GD0 + 8 * j + o + 1 - 4)
                    out = ps_o[:, o % 4, half_no]
                    for k in range(4):
                        kk, col = 4 * half_no + k, slice(P * o, P * o + P)
                        pe.matmul(out, w_hi[:, kk, col], y_hi[:, par, kk], start=(k == 0), stop=False)
                        pe.matmul(out, w_hi[:, kk, col], y_lo[:, par, kk], start=False, stop=False)
                        last_mm = pe.matmul(out, w_lo[:, kk, col], y_hi[:, par, kk], start=False, stop=(k == 3))
                    if half_no:
                        last_mm.then_inc(mm, 1)
                    if not last and n == 4:
                        turn_in(j + 1, next_half(jh, par), 1 - par)
                    if not last and n == 10:
                        turn_back(j + 1)

            chunks(pe, body)

        @block.scalar
        def _(act):
            for counter in m_out:
                act.sem_inc(counter, DMA_START)

            def norm(j):
                wait_reg(act, sh_done, j + 1)
                wait_reg(act, t_back, j)
                for t in range(2):
                    act.activation(normed[:, t], ps_n[:, t], ACT.Identity, bias=shift[:, t], scale=rstd[:, t]).then_inc(n_done, 1)

            def silu(j):
                wait_reg(act, t_back, j + 1)
                wait_reg(act, yb_done, j)
                for b in range(4):
                    act.activation(act_sb[:, b], ps_b[:, b], ACT.Silu, bias=cst.cols[:, R_LNB + b:R_LNB + b + 1],
                                   scale=cst.cols[:, R_LNG + b:R_LNG + b + 1]).then_inc(silu_done, 1)

            high_w(act, 0)
            norm(0)
            silu(0)
            high_w(act, 1)
            high_w(act, 2)
            high_w(act, 3)

            def body(j, jh, par, last):
                if not last:
                    norm(j + 1)
                    silu(j + 1)
                wait_reg(act, m_done, 8 * j + 8)
                act.dma_start(io.m[:, ds(CH * j, CH)].rearrange("(b p) t -> p b t", p=P), m_sb[:, par]).then_inc(m_out[par], 16)

            chunks(act, body)
            act.wait_ge(m_out[0], DMA_START + 16 * (NCH // 2 + 1))
            act.wait_ge(m_out[1], DMA_START + 16 * (NCH // 2))

        @block.vector
        def _(dve):
            def stats(j):
                wait_reg(dve, t_in, j + 1)
                for t in range(2):
                    dve.bn_stats(bn[:, t], ps_n[:, t]).then_inc(bn_done, 1)
                wait_reg(dve, bn_done, 2 * j + 2)
                for t in range(2):
                    dve.bn_aggr(mv[:, t], bn[:, t]).then_inc(mv_done, 1)
                wait_reg(dve, rs_done, 2 * j + 2)
                dve.scalar_tensor_tensor(shift[:], mv[:, :, 0:1], -1.0, rstd[:], ALU.mult, ALU.mult).then_inc(sh_done, 1)

            def high(j, jh, par, part):
                if part == 0:
                    wait_reg(dve, s_in[par], 48 * (jh + 1))
                    dve.tensor_copy(y_hi[:, par, 0:4], ya[:, par]).then_inc(hi_done, 1)
                else:
                    wait_reg(dve, silu_done, 4 * j + 4)
                    wait_reg(dve, lo_done, 2 * j)
                    dve.tensor_tensor(yb[:], act_sb[:], zb[:, par], ALU.mult).then_inc(yb_done, 1)
                    wait_reg(dve, yb_done, j + 1)
                    dve.tensor_copy(y_hi[:, par, 4:8], yb[:]).then_inc(hi_done, 1)

            dve.sem_inc(gated_done, GD0)
            stats(0)
            high(0, 0, 0, 0)
            low_w(dve, 0)
            high(0, 0, 0, 1)
            for c in range(1, 4):
                low_w(dve, c)

            def body(j, jh, par, last):
                wait_reg(dve, g_in[par], 16 * (jh + 1))
                wait_reg(dve, m_out[par], DMA_START + 16 * jh)
                for o in range(8):
                    n = 8 * j + o
                    wait_reg(dve, mm, n + 1)
                    dve.tensor_tensor(gated[:, o % 2], ps_o[:, o % 4], gates[:, par, o:o + KC + 1:KC], ALU.mult).then_inc(gated_done, 1)
                    wait_reg(dve, gated_done, GD0 + n + 1)
                    dve.tensor_tensor(m_sb[:, par, o], gated[:, o % 2, 0], gated[:, o % 2, 1], ALU.add).then_inc(m_done, 1)
                    if not last and o == 1:
                        stats(j + 1)
                    if not last and o == 2:
                        high(j + 1, jh + par, 1 - par, 0)
                    if not last and o == 5:
                        high(j + 1, jh + par, 1 - par, 1)

            chunks(dve, body)


def finish(nc, io, cst):
    with ExitStack() as ctx:
        sb = lambda n, s, d=F32: ctx.enter_context(nc.sbuf_tensor(n, s, d))
        sem = lambda n: ctx.enter_context(nc.semaphore(n))
        stage, w_hi, w_lo = sb("wo_stage", [P, 2, KC, WG]), sb("wo_hi", [P, KC, D], F32R), sb("wo_lo", [P, KC, D], F32R)
        m_in, x_in = sb("m_in", [P, 2, KC, CH]), sb("x_in", [P, 2, 2, D])
        m_hi, m_lo = sb("m_hi", [P, 2, KC, CH], F32R), sb("m_lo", [P, 2, KC, CH], F32R)
        gate_bc, fg = sb("gate_rows", [P, 2, D]), sb("final_g", [P, D])
        z, square = sb("z_res", [P, 2, D]), sb("z_square", [P, D])
        ssum, tmp, rstd, half = (sb(n, [P, 2, 1]) for n in ("z_ssum", "z_tmp", "z_rstd", "z_half"))
        psF = ctx.enter_context(nc.psum_tensor("psF", [P, 2, 2, 2, 512], F32))
        w_in, w_hid, w_lod = [sem("wo_in0"), sem("wo_in1")], sem("wo_hid"), sem("wo_lod")
        m_ins, x_ins, fg_in = [sem("m_in0"), sem("m_in1")], [sem("x_in0_"), sem("x_in1_")], sem("fg_in")
        gate_mm, gate_out, half_set = sem("gate_mm"), sem("gate_out"), sem("half_f")
        hi_done, lo_done, mm, scaled, z_done, sq_done, rs_done, y_done = (
            sem(n) for n in ("m_hid", "m_lod", "out_mm", "gated_f", "z_done", "z_sq", "z_rs", "y_fin"))
        y_out = [sem("y_out0"), sem("y_out1")]
        load_w, high_w, low_w = split_weights(nc, (io.w_out,), stage, w_hi, w_lo, w_in, w_hid, w_lod)
        SC0 = 8
        block = ctx.enter_context(nc.Block())

        def chunks(eng, body):
            with eng.Fori(0, NCH // 2) as t:
                body(2 * t, t, 0, False)
                body(2 * t + 1, t, 1, False)
            body(NCH - 1, NCH // 2, 0, True)

        @block.sync
        def _(sp):
            def load_m(j, par):
                sp.dma_start(m_in[:, par], io.m[:, ds(CH * j, CH)].rearrange("(b p) t -> p b t", p=P)).then_inc(m_ins[par], 16)

            def load_x(j, par, last):
                x = io.x_prompt if last else io.x_sample[ds(CH * j, CH)]
                sp.dma_start(x_in[:, par], x.rearrange("(t p) d -> p t d", p=P)).then_inc(x_ins[par], 16)

            def load(j, par, last):
                load_m(j, par)
                load_x(j, par, last)

            load_w(sp, 0)
            load_m(0, 0)
            for c in range(1, 4):
                load_w(sp, c)
            load_x(0, 0, False)
            sp.dma_start(fg[:], io.final_g.partition_broadcast(P)).then_inc(fg_in, 16)
            load(1, 1, False)

            def again(j, last):
                wait_reg(sp, lo_done, j - 1)
                wait_reg(sp, z_done, 4 * (j - 1))
            with sp.Fori(1, NCH // 2) as t:
                again(2 * t, False)
                load(2 * t, 0, False)
                again(2 * t + 1, False)
                load(2 * t + 1, 1, False)
            again(NCH - 1, True)
            load(NCH - 1, 0, True)

        @block.gpsimd
        def _(pool):
            pool.memset(half[:], -0.5).then_inc(half_set, 1)
            pool.wait_ge(half_set, 1)

            def low(j, par):
                wait_reg(pool, hi_done, j + 1)
                pool.tensor_tensor(m_lo[:, par], m_in[:, par], m_hi[:, par].bitcast(F32), ALU.subtract).then_inc(lo_done, 1)
            low(0, 0)

            def body(j, jh, par, last):
                if not last:
                    low(j + 1, 1 - par)
                for t in range(2):
                    n = 2 * j + t
                    wait_reg(pool, sq_done, n + 1)
                    pool.tensor_scalar(tmp[:, t], ssum[:, t], 1.0 / D, EPS, ALU.mult, ALU.add).then_inc(rs_done, 1)
                    wait_reg(pool, rs_done, 2 * n + 1)
                    pool.tensor_tensor(rstd[:, t], tmp[:, t], half[:, t], ALU.pow).then_inc(rs_done, 1)
            chunks(pool, body)

        @block.tensor
        def _(pe):
            pe.sem_inc(mm, START)
            for g in range(2):
                for h in range(2):
                    mmi = pe.matmul(psF[:, 0, g, h], cst.ident[0:2, g:g + 1].to_broadcast([2, P]),
                                    cst.gate[:, 512 * h:512 * h + 512], start=True, stop=True)
                mmi.then_inc(gate_mm, 1)
            pe.wait_ge(gate_out, 2)

            def body(j, jh, par, last):
                pe.wait_ge(lo_done, j + 1)
                for t in range(2):
                    for h in range(2):
                        out = psF[:, par, t, h]
                        pe.wait_ge(w_lod, 2 * h + 2)
                        pe.wait_ge(scaled, SC0 + 4 * j + 2 * t + h + 1 - 8)
                        for k in range(KC):
                            tok, col = slice(P * t, P * t + P), slice(512 * h, 512 * h + 512)
                            pe.matmul(out, m_hi[:, par, k, tok], w_hi[:, k, col], start=(k == 0), stop=False)
                            pe.matmul(out, m_hi[:, par, k, tok], w_lo[:, k, col], start=False, stop=False)
                            mmi = pe.matmul(out, m_lo[:, par, k, tok], w_hi[:, k, col], start=False, stop=(k == KC - 1))
                        mmi.then_inc(mm, 1)
            chunks(pe, body)

        @block.scalar
        def _(act):
            for counter in y_out:
                act.sem_inc(counter, DMA_START)

            for c in range(4):
                high_w(act, c)

            def body(j, jh, par, last):
                for t in range(2):
                    n = 2 * j + t
                    wait_reg(act, z_done, 2 * n + 2)
                    act.activation(square[:], z[:, t], ACT.Square, accum_out=ssum[:, t]).then_inc(sq_done, 1)
                    wait_reg(act, sq_done, n + 1)
                for t in range(2):
                    wait_reg(act, y_done, 2 * j + t + 1)
                    y = (io.y_prompt if last else io.y_sample[ds(CH * j, CH)])[P * t:P * t + P]
                    act.dma_start(y, z[:, t]).then_inc(y_out[t], 16)
            chunks(act, body)
            for s in y_out:
                act.wait_ge(s, DMA_START + 16 * NCH)

        @block.vector
        def _(dve):
            dve.sem_inc(scaled, SC0)
            def high(j, jh, par, first=False):
                wait_reg(dve, m_ins[par], 16 * (jh + 1))
                if not first:
                    wait_reg(dve, mm, START + 4 * (j - 1))
                dve.tensor_copy(m_hi[:, par], m_in[:, par]).then_inc(hi_done, 1)

            dve.wait_ge(gate_mm, 2)
            for g in range(2):
                dve.tensor_copy(gate_bc[:, g], psF[:, 0, g].rearrange("p h n -> p (h n)")).then_inc(gate_out, 1)
            low_w(dve, 0)
            high(0, 0, 0, True)
            for c in range(1, 4):
                low_w(dve, c)
            dve.wait_ge(fg_in, 16)
            dve.wait_ge(gate_out, 2)

            def body(j, jh, par, last):
                if not last:
                    high(j + 1, jh + par, 1 - par)
                g = 0 if last else 1
                wait_reg(dve, x_ins[par], 16 * (jh + 1))
                for t in range(2):
                    wait_reg(dve, y_out[t], DMA_START + 16 * j)
                    for h in range(2):
                        n = 4 * j + 2 * t + h
                        col = slice(512 * h, 512 * h + 512)
                        wait_reg(dve, mm, START + n + 1)
                        dve.tensor_tensor(z[:, t, col], psF[:, par, t, h], gate_bc[:, g, col], ALU.mult).then_inc(scaled, 1)
                        wait_reg(dve, scaled, SC0 + n + 1)
                        dve.tensor_tensor(z[:, t, col], z[:, t, col], x_in[:, par, t, col], ALU.add).then_inc(z_done, 1)
                    wait_reg(dve, rs_done, 4 * j + 2 * t + 2)
                    dve.scalar_tensor_tensor(z[:, t], z[:, t], rstd[:, t], fg[:], ALU.mult, ALU.mult).then_inc(y_done, 1)
            chunks(dve, body)


IN_NAMES = ["x_prompt", "x_sample", "cache_k", "cache_v", "c", "c_ctx", "rms_g", "w_ada", "b_ada", "w_in", "b_in",
            "rel_bias", "dw_w", "dw_b", "ln_g", "ln_b", "w_proj_a", "w_proj_b", "w_out", "final_g"]
OUTS = [("y_prompt", (CTX, D)), ("y_sample", (LAT, D)), ("state_k", (CTX, WA)), ("state_v", (CTX, WA))]


class Arrays:
    pass


def build(nc, io):
    io.proj = nc.dram_tensor("proj", (D_IN, TOK), F32, kind="Internal").ap()
    io.v = nc.dram_tensor("v_tokens", (TOK, WA), F32, kind="Internal").ap()
    io.conv = nc.dram_tensor("conv", (WB, TOK), F32, kind="Internal").ap()
    io.ya = nc.dram_tensor("ya", (WA, TOK), F32, kind="Internal").ap()
    io.m = nc.dram_tensor("merged", (D, TOK), F32, kind="Internal").ap()
    io.table = nc.dram_tensor("shifted_bias", (HEADS, QC, ST), F32, kind="Internal").ap()
    cst = Arrays()
    with ExitStack() as ctx:
        sb = lambda n, s, d=F32: ctx.enter_context(nc.sbuf_tensor(n, s, d))
        cst.ident = sb("ident", [P, P])
        cst.cols = sb("param_cols", [P, R_C])
        cst.taps = sb("taps", [P, 4 * TAPS])
        cst.qbias = sb("q_bias", [P, 4])
        cst.shift, cst.scale = sb("shift", [P, KC, 2]), sb("scale", [P, KC, 2])
        cst.gate = sb("gate_rows_2", [2, D])
        with ExitStack() as c2:
            hT_hi = c2.enter_context(nc.sbuf_tensor("hT_hi", [P, KC, HT_W], F32R))
            hT_lo = c2.enter_context(nc.sbuf_tensor("hT_lo", [P, KC, HT_W], F32R))
            modulation(nc, io, cst, hT_hi, hT_lo)
            with nc.sbuf_tensor("xn_b", [P, 8, D], F32) as xn:
                project(nc, io, cst, hT_hi, hT_lo, GROUP_A, 0, xn)
                turn_group_b(nc, cst, xn, hT_hi, hT_lo)
            project(nc, io, cst, hT_hi, hT_lo, GROUP_B, 1)
        attend(nc, io, cst)
        merge(nc, io, cst)
        finish(nc, io, cst)


def kernel(**inputs):
    import concourse.bacc as bacc
    from concourse.bass_utils import run_bass_kernel_spmd

    nc = bacc.Bacc("TRN2", target_bir_lowering=False, num_devices=1)
    arrays, io = {}, Arrays()
    flat = {"x_prompt": (CTX, D), "x_sample": (LAT, D), "cache_k": (CTX, WA), "cache_v": (CTX, WA), "c": (D,),
            "rms_g": (D,), "w_ada": (D, 3 * D), "b_ada": (3 * D,), "w_in": (D, D_IN), "b_in": (D_IN,),
            "rel_bias": (HEADS, 2 * WIN_R - 1, 2 * WIN_C - 1), "dw_w": (TAPS, WB), "dw_b": (WB,), "ln_g": (WB,),
            "ln_b": (WB,), "w_proj_a": (WA, D), "w_proj_b": (WB, D), "w_out": (D, D)}
    row_mask, col_mask = window_masks()
    consts = {"ident": np.eye(P, dtype=np.float32), "row_mask": row_mask, "col_mask": col_mask}
    given = {n: inputs[n] for n in IN_NAMES}
    given.update(consts)

    aps = {}
    for name, a in given.items():
        a = np.ascontiguousarray(a).reshape(flat.get(name, np.shape(a)))
        arrays[f"in_{name}"] = a
        aps[name] = nc.dram_tensor(f"in_{name}", a.shape, mybir.dt.from_np(a.dtype), kind="ExternalInput").ap()
    for name, shape in OUTS:
        aps[name] = nc.dram_tensor(f"out_{name}", shape, F32, kind="ExternalOutput").ap()
    io.__dict__.update(aps)
    build(nc, io)
    r = run_bass_kernel_spmd(nc, [arrays], core_ids=[0]).results[0]
    y_p, y_s, sk, sv = (r[f"out_{name}"] for name, _ in OUTS)
    return (y_p.reshape(1, CTX, D), y_s.reshape(1, LAT, D), sk.reshape(1, 1, CTX, HEADS, DH),
            sv.reshape(1, 1, CTX, HEADS, DH))
```

```python
from contextlib import ExitStack

import numpy as np

import concourse.bass as bass
from concourse import mybir

F32 = mybir.dt.float32
F32R = mybir.dt.float32r
ALU = mybir.AluOpType
ACT = mybir.ActivationFunctionType
AX_X = mybir.AxisListType.X
ds = bass.ds

P = 128
D = 1024
KC = D // P
LAT, CTX = 2048, 256
TOK = LAT + CTX
HEADS, DH = 8, 64
WA = WB = 512
TAPS, PAD = 31, 15
GRID, ROWS = 64, 32
WIN_R, WIN_C = 8, 16
EPS = 1e-6
Q0, K0, V0, ZA0 = 0, WA, 2 * WA, 3 * WA
GA0 = 4 * WA
GB0 = GA0 + WB
ZB0 = 4 * WA + 2 * WB
G0 = 4 * WA + 3 * WB
D_IN = G0 + 2 * D

GROUP_A = [(0, 512, 0), (512, 512, 512), (1024, CTX, LAT)]
GROUP_B = [(0, 512, 1024), (512, 512, 1536)]
HT_W = 1280

R_BIN, R_DWB, R_LNG, R_LNB, R_RMS, R_BADA, R_C = 0, 44, 48, 52, 56, 64, 88
R_END = R_C + 2 * KC

SECTIONS = [
    ("glu", GA0, GB0, P, 4),
    ("value", V0, V0 + P, 2 * P, 2),
    ("qk", Q0, K0, P, 4),
    ("z", ZA0, ZB0, P, 4),
    ("gates", G0, G0 + D, P, 8),
]
TURNS = sum(s[4] for s in SECTIONS)
CREDIT = 16


START, DMA_START = 1, 16


def rms_scale(pool, src, out, eps_tmp, minus_half, done, n):
    pool.tensor_scalar(eps_tmp, src, 1.0 / D, EPS, ALU.mult, ALU.add).then_inc(done, 1)
    pool.wait_ge(done, n + 1)
    pool.tensor_tensor(out, eps_tmp, minus_half, ALU.pow).then_inc(done, 1)


def wait_reg(eng, sem, value):
    eng.wait_ge(sem, value)
    eng.nop(nofuse=True)


GATE_OUT_AT = [12, 20]


def modulation(nc, io, cst, hT_hi, hT_lo):
    with ExitStack() as ctx:
        sb = lambda n, s, d=F32: ctx.enter_context(nc.sbuf_tensor(n, s, d))
        sem = lambda n: ctx.enter_context(nc.semaphore(n))
        rows = sb("param_rows", [P, P])
        taps = sb("tap_rows", [P, P])
        silu_c = sb("silu_c", [P, 2 * KC])
        wada = sb("wada", [P, 3, KC, 512])
        ada_row = sb("ada_row", [2, 4 * 512])
        gate_bias = sb("gate_bias", [2, D])
        table_pad = sb("table_pad", [HEADS, BT])
        xn = sb("xn_a", [P, 10, D])
        square = sb("square", [P, D])
        ssum = sb("ssum", [P, 10])
        tmp = sb("rms_tmp", [P, 10])
        rstd = sb("rstd", [P, 10])
        half = sb("minus_half", [P, 10])
        scale1 = sb("scale1", [P, KC, 2])
        hf = sb("h_f32", [P, 3, 512])
        psT = ctx.enter_context(nc.psum_tensor("psT", [P, 2, 512], F32))
        psM = ctx.enter_context(nc.psum_tensor("psM", [P, 2, 512], F32))
        psX = ctx.enter_context(nc.psum_tensor("psX", [P, 3, 512], F32))
        psC = ctx.enter_context(nc.psum_tensor("psC", [P, 2 * KC, 2], F32))
        ada_turned, gb_in, gate_done = sem("ada_turned"), sem("gate_bias_in"), sem("gate_done")
        tab_zero, tab_in, tab_out = sem("tab_zero"), sem("tab_in"), sem("tab_out")
        ident_in = sem("ident_in")
        rows_in, x_in, ada_in = sem("rows_in"), [sem(f"x_in{i}") for i in range(5)], [sem(f"ada_in{i}") for i in range(3)]
        turned, cols_out, silu_done = sem("turned"), sem("cols_out"), sem("silu_done")
        ada_mm, ada_out, sq_done, rms_done, xn_done = sem("ada_mm"), sem("ada_out"), sem("sq_done"), sem("rms_done"), sem("xn_done")
        half_set, mod_done, tr_done, hf_done, hi_done, lo_dve, lo_pool = (
            sem("half_set"), sem("mod_done"), sem("tr_done"), sem("hf_done"), sem("hi_done"), sem("lo_dve"), sem("lo_pool"))
        units = [(c, k) for c in range(3) for k in range(KC)]
        block = ctx.enter_context(nc.Block())

        @block.sync
        def _(sp):
            sp.dma_start(cst.ident[:], io.ident).then_inc(ident_in, 16)
            def load_x(tiles):
                for t in tiles:
                    src = io.x_sample[P * t:P * t + P] if t < 8 else io.x_prompt[P * (t - 8):P * (t - 7)]
                    sp.dma_start(xn[:, t], src).then_inc(x_in[t // 2], 16)

            for j in range(6):
                if j >= 3:
                    sp.wait_ge(ada_mm, j - 2)
                sp.dma_start(wada[:, j % 3], io.w_ada[:, 512 * j:512 * j + 512]
                             .rearrange("(c p) n -> p c n", p=P)).then_inc(ada_in[j % 3], 16)
                if j == 0:
                    load_x(range(3))
                    sp.wait_ge(rows_in, 16 * 9)
                if j == 1:
                    load_x(range(3, 6))
                if j == 2:
                    load_x(range(6, 10))
                if j == 2:
                    sp.dma_start(gate_bias[:], io.b_ada[2 * D:3 * D].partition_broadcast(2)).then_inc(gb_in, 16)
                    sp.wait_ge(tab_zero, 1)
                    pad3 = table_pad[:].rearrange("h (r c) -> h r c", c=BW_C)
                    sp.dma_start(pad3[:, 4:19, 8:39], io.rel_bias).then_inc(tab_in, 16)
            sp.wait_ge(tab_in, 16)
            for c in range(QC):
                sp.dma_start(io.table[:, c], table_pad[:, QC - 1 - c:QC - 1 - c + ST]).then_inc(tab_out, 16)
            sp.wait_ge(tab_out, 16 * QC)

        @block.gpsimd
        def _(pool):
            pool.memset(half[:], -0.5).then_inc(half_set, 1)
            pool.wait_ge(half_set, 1)
            pool.wait_ge(sq_done, 10)
            rms_scale(pool, ssum[:], rstd[:], tmp[:], half[:], rms_done, 0)
            for n, (c, k) in enumerate(units):
                if n % 2:
                    pool.wait_ge(hi_done, n + 1)
                    w, at = GROUP_A[c][1], GROUP_A[c][0]
                    pool.tensor_tensor(hT_lo[:, k, at:at + w], hf[:, n % 3, 0:w],
                                       hT_hi[:, k, at:at + w].bitcast(F32), ALU.subtract).then_inc(lo_pool, 1)

        @block.scalar
        def _(act):
            for r, a, n in ((R_BIN, io.b_in, 44), (R_DWB, io.dw_b, 4), (R_LNG, io.ln_g, 4), (R_LNB, io.ln_b, 4),
                            (R_RMS, io.rms_g, 8), (R_BADA, io.b_ada, 24), (R_C, io.c_ctx, 8), (R_C + KC, io.c, 8)):
                act.dma_start(rows[r:r + n, :], a.rearrange("(r p) -> r p", p=P)).then_inc(rows_in, 16)
            act.dma_start(taps[0:4 * TAPS, :], io.dw_w.rearrange("k (b p) -> (k b) p", p=P)).then_inc(rows_in, 16)
            act.wait_ge(turned, 1)
            act.activation(silu_c[:], psT[:, 0, R_C:R_END], ACT.Silu).then_inc(silu_done, 1)
            for t in range(10):
                act.wait_ge(x_in[t // 2], 32)
                if t:
                    act.wait_ge(sq_done, t)
                act.activation(square[:], xn[:, t], ACT.Square, accum_out=ssum[:, t:t + 1]).then_inc(sq_done, 1)
            for n, (c, k) in enumerate(units):
                w, g = GROUP_A[c][1], 0 if c == 2 else 1
                if n == 0:
                    act.wait_ge(mod_done, 4)
                act.wait_ge(tr_done, n + 1)
                if n >= 3:
                    act.wait_ge(lo_pool if n % 2 == 0 else lo_dve, (n - 3) // 2 + 1)
                act.activation(hf[:, n % 3, 0:w], psX[:, n % 3, 0:w], ACT.Identity,
                               bias=cst.shift[:, k, g:g + 1], scale=cst.scale[:, k, g:g + 1]).then_inc(hf_done, 1)

        @block.vector
        def _(dve):
            dve.memset(table_pad[:], 0.0).then_inc(tab_zero, 1)
            dve.wait_ge(turned, 1)
            dve.wait_ge(silu_done, 1)
            dve.tensor_copy(cst.cols[:, 0:R_C], psT[:, 0, 0:R_C]).then_inc(cols_out, 1)
            dve.wait_ge(turned, 2)
            dve.tensor_copy(cst.taps[:], psT[:, 1, 0:4 * TAPS]).then_inc(cols_out, 1)
            dve.wait_ge(cols_out, 2)
            dve.tensor_scalar(cst.qbias[:], cst.cols[:, 0:4], DH ** -0.5, None, ALU.mult)

            def ada_out_of(j):
                dve.wait_ge(ada_mm, j + 1)
                dve.tensor_copy(ada_row[:, 512 * j:512 * j + 512], psM[0:2, j % 2]).then_inc(ada_out, 1)

            ada_out_of(0)
            ada_out_of(1)
            dve.wait_ge(rms_done, 2)
            for t in range(10):
                dve.tensor_scalar(xn[:, t], xn[:, t], rstd[:, t:t + 1], None, ALU.mult).then_inc(xn_done, 1)
            ada_out_of(2)
            ada_out_of(3)
            dve.wait_ge(ada_turned, 1)
            for dst, b in ((cst.shift, 0), (scale1, KC)):
                bias = cst.cols[:, R_BADA + b:R_BADA + b + KC].unsqueeze(2).to_broadcast([P, KC, 2])
                dve.tensor_tensor(dst[:], psC[:, b:b + KC], bias, ALU.add).then_inc(mod_done, 1)
            dve.wait_ge(mod_done, 2)
            for g in range(2):
                dve.scalar_tensor_tensor(cst.scale[:, :, g], scale1[:, :, g], 1.0,
                                         cst.cols[:, R_RMS:R_RMS + KC], ALU.add, ALU.mult).then_inc(mod_done, 1)
            for n, (c, k) in enumerate(units):
                if n in GATE_OUT_AT:
                    h = GATE_OUT_AT.index(n)
                    at = slice(512 * h, 512 * h + 512)
                    dve.wait_ge(gb_in, 16)
                    dve.wait_ge(ada_mm, 5 + h)
                    dve.tensor_tensor(cst.gate[:, at], psM[0:2, h], gate_bias[:, at], ALU.add).then_inc(gate_done, 1)
                w, at = GROUP_A[c][1], GROUP_A[c][0]
                dve.wait_ge(hf_done, n + 1)
                dve.tensor_copy(hT_hi[:, k, at:at + w], hf[:, n % 3, 0:w]).then_inc(hi_done, 1)
                if n % 2 == 0:
                    dve.wait_ge(hi_done, n + 1)
                    dve.tensor_tensor(hT_lo[:, k, at:at + w], hf[:, n % 3, 0:w],
                                      hT_hi[:, k, at:at + w].bitcast(F32), ALU.subtract).then_inc(lo_dve, 1)

        @block.tensor
        def _(pe):
            pe.wait_ge(ident_in, 16)
            pe.wait_ge(rows_in, 16 * 9)
            pe.transpose(psT[:, 0, 0:R_END], rows[0:R_END, :], cst.ident[0:R_END, 0:R_END]).then_inc(turned, 1)
            pe.transpose(psT[:, 1, 0:4 * TAPS], taps[0:4 * TAPS, :], cst.ident[0:4 * TAPS, 0:4 * TAPS]).then_inc(turned, 1)
            pe.wait_ge(silu_done, 1)
            sc = silu_c[:].rearrange("p (g k) -> p k g", g=2)

            def ada_product(j, k):
                if k == 0:
                    pe.wait_ge(ada_in[j % 3], 16 * (j // 3 + 1))
                    if j >= 2:
                        pe.wait_ge(ada_out, j - 1)
                mm = pe.matmul(psM[0:2, j % 2], sc[:, k, :], wada[:, j % 3, k], start=(k == 0), stop=(k == KC - 1))
                if k == KC - 1:
                    mm.then_inc(ada_mm, 1)

            for j in range(5):
                if j < 4:
                    for k in range(KC):
                        ada_product(j, k)
                if j >= 1:
                    pe.wait_ge(ada_out, j)
                    for m in range(4 * j - 4, 4 * j):
                        tr = pe.transpose(psC[:, m], ada_row[:, P * m:P * m + P], cst.ident[0:2, 0:2])
            tr.then_inc(ada_turned, 1)
            pe.wait_ge(xn_done, 10)
            for n, (c, k) in enumerate(units):
                if n >= 3:
                    pe.wait_ge(hf_done, n - 2)
                if 2 <= n < 2 + 2 * KC:
                    ada_product(4 + (n - 2) // KC, (n - 2) % KC)
                tiles = range(4 * c, 4 * c + GROUP_A[c][1] // P)
                for m, t in enumerate(tiles):
                    tr = pe.transpose(psX[:, n % 3, P * m:P * m + P], xn[:, t, P * k:P * k + P], cst.ident[:])
                tr.then_inc(tr_done, 1)


def turn_group_b(ctx, nc, cst, xn, hT_hi, hT_lo):
    slots = 4
    sem = lambda n: ctx.enter_context(nc.semaphore(n))
    hf = ctx.enter_context(nc.sbuf_tensor("hb_f32", [P, slots, 512], F32))
    psX = ctx.enter_context(nc.psum_tensor("psXb", [P, slots, 512], F32))
    tr_done, hf_done, hi_done, lo_dve, lo_pool = (
        sem("b_tr_done"), sem("b_hf_done"), sem("b_hi_done"), sem("b_lo_dve"), sem("b_lo_pool"))
    units = [(c, k) for c in range(2) for k in range(KC)]

    def turn(pe):
        for n, (c, k) in enumerate(units):
            if n >= slots:
                pe.wait_ge(hf_done, n - slots + 1)
            for m in range(4):
                tr = pe.transpose(psX[:, n % slots, P * m:P * m + P], xn[:, 4 * c + m, P * k:P * k + P], cst.ident[:])
            tr.then_inc(tr_done, 1)

    def wait_turned(eng):
        eng.wait_ge(tr_done, len(units))

    def wait_split(pe):
        pe.wait_ge(hi_done, len(units))
        pe.wait_ge(lo_dve, len(units) // 2)
        pe.wait_ge(lo_pool, len(units) // 2)

    def modulate(act):
        for n, (c, k) in enumerate(units):
            act.wait_ge(tr_done, n + 1)
            if n >= slots:
                act.wait_ge(lo_pool if n % 2 else lo_dve, (n - slots) // 2 + 1)
            act.activation(hf[:, n % slots], psX[:, n % slots], ACT.Identity, bias=cst.shift[:, k, 1:2],
                           scale=cst.scale[:, k, 1:2]).then_inc(hf_done, 1)

    def low(eng, n, done):
        c, k = units[n]
        eng.wait_ge(hi_done, n + 1)
        at = slice(512 * c, 512 * c + 512)
        eng.tensor_tensor(hT_lo[:, k, at], hf[:, n % slots], hT_hi[:, k, at].bitcast(F32), ALU.subtract).then_inc(done, 1)

    def high_and_low(dve, between):
        for n, (c, k) in enumerate(units):
            dve.wait_ge(hf_done, n + 1)
            dve.tensor_copy(hT_hi[:, k, 512 * c:512 * c + 512], hf[:, n % slots]).then_inc(hi_done, 1)
            if n % 2 == 0:
                low(dve, n, lo_dve)
            between(n)

    def low_odd(pool):
        for n in range(1, len(units), 2):
            low(pool, n, lo_pool)
    return turn, wait_turned, wait_split, modulate, high_and_low, low_odd


def project(nc, io, cst, hT_hi, hT_lo, group, g, xn):
    chunks = group
    nch = len(chunks)
    nU = 2 * nch
    ntile = sum(w for _, w, _ in chunks) // P
    half_tiles = ntile // 2
    first = g == 0
    with ExitStack() as ctx:
        sb = lambda n, s, d=F32: ctx.enter_context(nc.sbuf_tensor(f"{n}{g}", s, d))
        sem = lambda n: ctx.enter_context(nc.semaphore(f"{n}{g}"))
        wst = sb("w_stage", [P, 2, KC, P])
        w_hi, w_lo = sb("w_hi", [P, 4, KC, P], F32R), sb("w_lo", [P, 4, KC, P], F32R)
        ostg = sb("out_stage", [P, 4, P * ntile])
        vbias = sb("v_bias", [P, WA])
        ps = ctx.enter_context(nc.psum_tensor(f"psP{g}", [P, nU, 512], F32))
        if first:
            square = sb("square_b", [P, D])
            ssum, tmp, rstd, half = (sb(n, [P, 8]) for n in ("ssum_b", "tmp_b", "rstd_b", "half_b"))
        else:
            UW = PAD + LAT + PAD + CTX + PAD
            OW = LAT + PAD + CTX
            u_in = xn[:].rearrange("p t d -> p (t d)")[:, 0:2 * UW].rearrange("p (b w) -> p b w", b=2)
            acc = sb("conv_acc", [P, 2, OW])
        w_in_sem = [sem("w_in_even"), sem("w_in_odd")]
        vb_in = sem("v_bias_in")
        hi_done, lo_done = sem("w_hi_done"), sem("w_lo_done")
        mm, ev_act, ev_dve = sem("unit_mm"), sem("evac_act"), sem("evac_dve")
        out_d = [sem(f"out_dma{s}_") for s in range(4)]
        if first:
            x_in, sq_done, rms_done, half_set, xn_done = sem("xb_in"), sem("sqb"), sem("rmsb"), sem("halfb"), sem("xnb")
        else:
            u_sem, pad_set, tap_done, conv_out = [sem("u_in0_"), sem("u_in1_")], sem("pad_set"), sem("tap_done"), [sem("cv0_"), sem("cv1_")]

            turn_xn, wait_turned, wait_split, modulate, high_and_low, low_odd = turn_group_b(ctx, nc, cst, xn, hT_hi, hT_lo)

        at = []
        n_mm = 0
        n_act = n_dve = CREDIT
        n_out = [0, 0, 0, 0]
        turn = 0
        for kind, *_, turns in SECTIONS:
            at.append((turn, n_mm, n_act, n_dve, list(n_out)))
            turn += turns
            if kind == "value":
                n_mm += ntile * turns
                n_dve += ntile * turns
            else:
                n_mm += nU * turns
            if kind == "glu":
                n_act += nch * turns
                n_dve += nch * turns
            elif kind != "value":
                n_act += nU * turns
            for s in range(4):
                if kind == "value":
                    n_out[s] += 16 * (3 if first and s % 2 else 1) * turns // 2
                elif kind != "glu" or s % 2 == 0:
                    n_out[s] += 16 * (2 if first else 1) * turns // 2
        end_out = n_out
        block = ctx.enter_context(nc.Block())

        def conv_load(eng, b):
            rows = io.proj[GA0 + P * b:GA0 + P * b + P]
            eng.dma_start(u_in[:, b % 2, PAD:PAD + LAT], rows[:, 0:LAT]).then_inc(u_sem[b % 2], 16)
            eng.dma_start(u_in[:, b % 2, 2 * PAD + LAT:2 * PAD + TOK], rows[:, LAT:TOK]).then_inc(u_sem[b % 2], 16)

        @block.sync
        def _(sp):
            def conv_store(b):
                rows = io.conv[P * b:P * b + P]
                sp.dma_start(rows[:, 0:LAT], acc[:, b % 2, 0:LAT]).then_inc(conv_out[b % 2], 16)
                sp.dma_start(rows[:, LAT:TOK], acc[:, b % 2, LAT + PAD:OW]).then_inc(conv_out[b % 2], 16)

            def conv_turn_over(b):
                sp.wait_ge(tap_done, TAPS * (b + 1))
                conv_store(b)
                if b < 2:
                    conv_load(sp, b + 2)

            sp.dma_start(vbias[:], io.b_in[V0:V0 + WA].partition_broadcast(P)).then_inc(vb_in, 16)
            for (kind, c0, c1, step, turns), (t0, *_) in zip(SECTIONS, at):
                def load(i, guarded):
                    for b, col in ((0, c0), (1, c1)):
                        if guarded:
                            sp.wait_ge(lo_done, 2 * (t0 + i - 1) + b + 1)
                        sp.dma_start(wst[:, b], io.w_in[:, ds(col + step * i, P)].rearrange("(c p) n -> p c n", p=P)
                                     ).then_inc(w_in_sem[b], 16)
                start = 0
                if t0 == 0:
                    load(0, False)
                    start = 1
                if not first and kind == "gates":
                    with sp.Fori(start, 2) as i:
                        load(i, True)
                    conv_turn_over(1)
                    start = 2
                with sp.Fori(start, turns) as i:
                    load(i, True)
                if first:
                    if kind == "qk":
                        sp.dma_start(xn[:], io.x_sample[LAT // 2:LAT].rearrange("(t p) d -> p t d", p=P)
                                     ).then_inc(x_in, 16)
                    continue
                for b in {"z": (0,), "gates": (2, 3)}.get(kind, ()):
                    conv_turn_over(b)
            if not first:
                for s in conv_out:
                    sp.wait_ge(s, 64)

        @block.gpsimd
        def _(pool):
            def split(turn_no, h, units_done):
                for b in range(2):
                    s = 2 * h + b
                    wait_reg(pool, w_in_sem[b], 16 * (turn_no + 1))
                    if units_done is not None and b == 0:
                        wait_reg(pool, mm, units_done)
                    pool.tensor_copy(w_hi[:, s], wst[:, b]).then_inc(hi_done, 1)
                    wait_reg(pool, hi_done, 2 * turn_no + b + 1)
                    pool.tensor_tensor(w_lo[:, s], wst[:, b], w_hi[:, s].bitcast(F32), ALU.subtract).then_inc(lo_done, 1)
            if first:
                pool.memset(half[:], -0.5).then_inc(half_set, 1)
            else:
                low_odd(pool)
            for (kind, *_, turns), (t0, m0, *_) in zip(SECTIONS, at):
                start = 0
                if t0 == 0:
                    pool.wait_ge(lo_done, 2)
                    split(1, 1, None)
                    start = 1
                if kind == "value":
                    split(t0, 0, m0 - nU)
                    split(t0 + 1, 1, m0)
                    continue
                if kind == "qk":
                    split(t0, 0, m0 - ntile)
                    split(t0 + 1, 1, m0)
                    start = 1
                if first and kind == "gates":
                    pool.wait_ge(half_set, 1)
                    pool.wait_ge(sq_done, 8)
                    rms_scale(pool, ssum[:], rstd[:], tmp[:], half[:], rms_done, 0)
                if turns // 2 > start:
                    with pool.Fori(start, turns // 2) as j:
                        split(t0 + 2 * j, 0, m0 + nU * (2 * j - 1))
                        split(t0 + 2 * j + 1, 1, m0 + nU * 2 * j)

        @block.tensor
        def _(pe):
            def triple(out, w_hi_c, w_lo_c, h_hi_c, h_lo_c, k):
                pe.matmul(out, w_hi_c, h_hi_c, start=(k == 0), stop=False)
                pe.matmul(out, w_hi_c, h_lo_c, start=False, stop=False)
                return pe.matmul(out, w_lo_c, h_hi_c, start=False, stop=(k == KC - 1))

            if not first:
                turn_xn(pe)
                wait_split(pe)
            for (kind, *_, turns), (t0, m0, a0, d0, _) in zip(SECTIONS, at):
                pe.wait_ge(ev_act, a0)
                pe.wait_ge(ev_dve, d0)

                def products(i, h):
                    if kind == "value":
                        pe.wait_ge(lo_done, 2 * (t0 + i + 1))
                        for t in range(ntile):
                            n = ntile * i + t
                            if n >= nU:
                                pe.wait_ge(ev_dve, d0 + n - nU + 1)
                            for k in range(KC):
                                tok = slice(P * t, P * t + P)
                                wv = [w[:, 2 * h:2 * h + 2, k, :] for w in (w_hi, w_lo)]
                                pe.matmul(ps[:, n % nU, 0:256], hT_hi[:, k, tok], wv[0], start=(k == 0), stop=False)
                                pe.matmul(ps[:, n % nU, 0:256], hT_hi[:, k, tok], wv[1], start=False, stop=False)
                                last = pe.matmul(ps[:, n % nU, 0:256], hT_lo[:, k, tok], wv[0], start=False,
                                                 stop=(k == KC - 1))
                            last.then_inc(mm, 1)
                        return
                    for b in range(2):
                        s = 2 * h + b
                        pe.wait_ge(lo_done, 2 * (t0 + i) + b + 1)
                        for c, (col, w, _) in enumerate(chunks):
                            u = nch * b + c
                            if kind == "glu":
                                pe.wait_ge(ev_dve if b == 0 else ev_act, (d0 if b == 0 else a0) + nch * i + c + 1 - nch)
                            else:
                                pe.wait_ge(ev_act, a0 + nU * i + u + 1 - nU)
                            for k in range(KC):
                                last = triple(ps[:, u, 0:w], w_hi[:, s, k], w_lo[:, s, k],
                                              hT_hi[:, k, col:col + w], hT_lo[:, k, col:col + w], k)
                            last.then_inc(mm, 1)

                if kind == "value":
                    products(0, 0)
                    products(1, 1)
                else:
                    with pe.Fori(0, turns // 2) as j:
                        products(2 * j, 0)
                        products(2 * j + 1, 1)

        @block.scalar
        def _(act):
            for counter in out_d:
                act.sem_inc(counter, DMA_START)

            def store_rows(s, row):
                w = chunks[0][1] + chunks[1][1]
                act.dma_start(io.proj[ds(row, P), chunks[0][2]:chunks[0][2] + w], ostg[:, s, 0:w]).then_inc(out_d[s], 16)
                if first:
                    act.dma_start(io.proj[ds(row, P), LAT:TOK], ostg[:, s, w:w + CTX]).then_inc(out_d[s], 16)

            if not first:
                modulate(act)
            per = 16 * (2 if first else 1)
            act.sem_inc(ev_act, CREDIT)
            for (kind, c0, c1, step, turns), (t0, m0, a0, d0, o0) in zip(SECTIONS, at):
                if kind == "value":
                    for i in range(turns):
                        for b in range(2):
                            s, last = 2 * i + b, ntile * i + half_tiles * (b + 1)
                            act.wait_ge(ev_dve, d0 + last)
                            vcol = slice(256 * i, 256 * i + 256)
                            src = ostg[:, s].rearrange("p (t n) -> p t n", n=256)
                            tok0 = chunks[0][2] + P * half_tiles * b
                            n = 3 if first and b else half_tiles
                            act.dma_start(io.v[tok0:tok0 + P * n, vcol].rearrange("(t p) n -> p t n", p=P),
                                          src[:, 0:n]).then_inc(out_d[s], 16)
                            if first and b:
                                act.dma_start(io.v[LAT:TOK, vcol].rearrange("(t p) n -> p t n", p=P),
                                              src[:, 3:5]).then_inc(out_d[s], 16)
                                act.dma_start(io.state_v[:, vcol].rearrange("(t p) n -> p t n", p=P),
                                              src[:, 3:5]).then_inc(out_d[s], 16)
                        if not first and i == 0:
                            act.wait_ge(pad_set, 2)
                            act.wait_ge(out_d[0], DMA_START + at[1][4][0] + 16)
                            act.wait_ge(out_d[2], DMA_START + at[1][4][2])
                            conv_load(act, 0)
                            conv_load(act, 1)
                    continue
                with act.Fori(0, turns // 2) as j:
                    for h in range(2):
                        i = 2 * j + h
                        if kind == "glu":
                            s = 2 * h + 1
                            act.wait_ge(ev_dve, d0 + nch * i - nch)
                            for c, (col, w, _) in enumerate(chunks):
                                wait_reg(act, mm, m0 + nU * i + nch + c + 1)
                                act.activation(ostg[:, s, col:col + w], ps[:, nch + c, 0:w], ACT.Sigmoid,
                                               bias=cst.cols[:, ds(GB0 // P + i, 1)]).then_inc(ev_act, 1)
                            act.wait_ge(ev_dve, d0 + nch * (i + 1))
                            store_rows(2 * h, GA0 + P * i)
                            continue
                        for b in range(2):
                            s = 2 * h + b
                            act.wait_ge(out_d[s], DMA_START + o0[s] + per * j)
                            for c, (col, w, _) in enumerate(chunks):
                                u = nch * b + c
                                wait_reg(act, mm, m0 + nU * i + u + 1)
                                func, scale = ACT.Identity, 1.0
                                bias = cst.cols[:, ds((c0, c1)[b] // P + i, 1)]
                                if kind == "z":
                                    func = ACT.Silu
                                elif kind == "gates":
                                    func = ACT.Sigmoid
                                elif b == 0:
                                    scale, bias = DH ** -0.5, cst.qbias[:, ds(i, 1)]
                                act.activation(ostg[:, s, col:col + w], ps[:, u, 0:w], func, bias=bias,
                                               scale=scale).then_inc(ev_act, 1)
                            act.wait_ge(ev_act, a0 + nU * i + nch * (b + 1))
                            store_rows(s, (c0, c1)[b] + P * i)
            for s in range(4):
                act.wait_ge(out_d[s], DMA_START + end_out[s])

        @block.vector
        def _(dve):
            dve.sem_inc(ev_dve, CREDIT)

            def split_first(b):
                dve.wait_ge(w_in_sem[b], 16)
                dve.tensor_copy(w_hi[:, b], wst[:, b]).then_inc(hi_done, 1)
                dve.wait_ge(hi_done, b + 1)
                dve.tensor_tensor(w_lo[:, b], wst[:, b], w_hi[:, b].bitcast(F32), ALU.subtract).then_inc(lo_done, 1)

            if first:
                split_first(0)
                split_first(1)
            else:
                high_and_low(dve, lambda n: split_first((8, 12).index(n)) if n in (8, 12) else None)
                wait_turned(dve)
                dve.memset(u_in[:, 0], 0.0).then_inc(pad_set, 1)
                dve.memset(u_in[:, 1], 0.0).then_inc(pad_set, 1)
            for (kind, c0, c1, step, turns), (t0, m0, a0, d0, o0) in zip(SECTIONS, at):
                if kind == "glu":
                    with dve.Fori(0, turns // 2) as j:
                        for h in range(2):
                            i = 2 * j + h
                            s = 2 * h
                            dve.wait_ge(out_d[s], DMA_START + (32 if first else 16) * j)
                            for c, (col, w, _) in enumerate(chunks):
                                dve.wait_ge(mm, m0 + nU * i + c + 1)
                                dve.wait_ge(ev_act, a0 + nch * i + c + 1)
                                dve.scalar_tensor_tensor(ostg[:, s, col:col + w], ps[:, c, 0:w],
                                                         cst.cols[:, ds(GA0 // P + i, 1)], ostg[:, s + 1, col:col + w],
                                                         ALU.add, ALU.mult).then_inc(ev_dve, 1)
                if kind == "value":
                    dve.wait_ge(vb_in, 16)
                    for i in range(turns):
                        for t in range(ntile):
                            s = 2 * i + t // half_tiles
                            if t % half_tiles == 0:
                                dve.wait_ge(out_d[s], DMA_START + o0[s])
                            n = ntile * i + t
                            dve.wait_ge(mm, m0 + n + 1)
                            dst = ostg[:, s].rearrange("p (t n) -> p t n", n=256)[:, t % half_tiles]
                            dve.tensor_tensor(dst, ps[:, n % nU, 0:256], vbias[:, 256 * i:256 * i + 256],
                                              ALU.add).then_inc(ev_dve, 1)
            if first:
                for t in range(8):
                    dve.wait_ge(x_in, 16)
                    dve.tensor_tensor_reduce(square[:], xn[:, t], xn[:, t], 1.0, 0.0, ALU.mult, ALU.add,
                                             ssum[:, t:t + 1]).then_inc(sq_done, 1)
                    dve.wait_ge(sq_done, t + 1)
                dve.wait_ge(rms_done, 2)
                for t in range(8):
                    dve.tensor_scalar(xn[:, t], xn[:, t], rstd[:, t:t + 1], None, ALU.mult).then_inc(xn_done, 1)
                return
            for b in range(4):
                dve.wait_ge(u_sem[b % 2], 32 * (b // 2 + 1))
                if b >= 2:
                    dve.wait_ge(conv_out[b % 2], 32)
                for k in range(TAPS):
                    src, dst = u_in[:, b % 2, k:k + OW], acc[:, b % 2]
                    tap = cst.taps[:, 4 * k + b:4 * k + b + 1]
                    n = TAPS * b + k
                    if k == 0:
                        op = dve.tensor_scalar(dst, src, tap, cst.cols[:, R_DWB + b:R_DWB + b + 1], ALU.mult, ALU.add)
                    else:
                        dve.wait_ge(tap_done, n)
                        op = dve.scalar_tensor_tensor(dst, src, tap, dst, ALU.mult, ALU.add)
                    op.then_inc(tap_done, 1)



QR, QC = 8, 16
BANDS = [(0, 12, 0), (4, 16, 1), (12, 16, 1), (20, 12, 2)]
SETS = [(0, 24, 0), (8, 32, 1), (24, 32, 1), (40, 24, 2)]
ROW_TYPES = [(4, 12), (0, 16), (0, 12)]
COL_TYPES = [(8, 24), (0, 32), (0, 24)]
BW_R, BW_C = 16, 47
BT = 24 * BW_C
ST = (QR - 1) * BW_C + BW_R * BW_C
MASKED = -1e30
LT = 16
TPH = LT + CTX // P
TPP = 2 * TPH
RED = 2 * LT + CTX // P
NG = 3
KW = TOK + CTX
T_OFF, _o = {}, 0
for _r in range(3):
    for _c in range(3):
        T_OFF[_r, _c] = _o
        _o += ROW_TYPES[_r][1] * COL_TYPES[_c][1]
T_W = _o


def window_masks():
    q = np.arange(P)
    rm, cm = np.zeros((3, P, 16), np.float32), np.zeros((3, P, 32), np.float32)
    for (kr0, nr, rt), a in zip(BANDS, range(4)):
        r = QR * a + q // QC
        lo = np.clip(r - WIN_R // 2, 0, ROWS - WIN_R)[:, None]
        kr = kr0 + np.arange(nr)[None]
        rm[rt, :, :nr] = np.where((kr >= lo) & (kr < lo + WIN_R), 0, MASKED)
    for (kc0, w, ct), b in zip(SETS, range(4)):
        c = QC * b + q % QC
        lo = np.clip(c - WIN_C // 2, 0, GRID - WIN_C)[:, None]
        kc = kc0 + np.arange(w)[None]
        cm[ct, :, :w] = np.where((kc >= lo) & (kc < lo + WIN_C), 0, MASKED)
    return rm, cm


def attend(nc, io, cst):
    with ExitStack() as ctx:
        sb = lambda n, s, d=F32: ctx.enter_context(nc.sbuf_tensor(n, s, d))
        ps = lambda n, s: ctx.enter_context(nc.psum_tensor(n, s, F32))
        sem = lambda n: ctx.enter_context(nc.semaphore(n))
        q_raw, k_raw, ck_raw = sb("q_raw", [P, TOK]), sb("k_raw", [P, KW]), sb("ck_raw", [P, 2, P])
        q_sp, k_hi, k_lo = sb("q_split", [P, 2, TOK], F32R), sb("k_hi", [P, 2, KW], F32R), sb("k_lo", [P, 2, KW], F32R)
        v_win, v_ctx = sb("v_win", [P, 2, 4, 8, DH + 1]), sb("v_ctx", [P, 2, 4, DH + 1])
        window, win_c, tables = sb("bias_window", [P, BW_R * BW_C]), sb("bias_cols", [P, 3, 512]), sb("bias", [P, 2, T_W])
        rmask, cmask = sb("row_mask", [P, 3, 16]), sb("col_mask", [P, 3, 32])
        s_sb, p_sb, pT = sb("scores", [P, 2, 512]), sb("probs", [P, 2, 768]), sb("probs_t", [P, 2, 6, P])
        stat = sb("stat", [P, 4, 8])
        o_sb, inv = sb("o_pair", [P, TPH, 2, DH + 1]), sb("inv_sums", [P, NG, 2])
        o_norm = sb("o_normed", [P, 2, NG, P])
        z_sb, y_sb, sk_sb = sb("z_pair", [P, TOK]), sb("y_pair", [P, TOK]), sb("sk", [P, 2, DH])
        ps_win, ps_ctx = [ps("ps_win0", [P, 512]), ps("ps_win1", [P, 512])], [ps("ps_ctx0", [P, 512]), ps("ps_ctx1", [P, 512])]
        ps_tw, ps_tc, ps_o, ps_y = ps("ps_tw", [P, 4, P]), ps("ps_tc", [P, 4, P]), ps("ps_o", [P, 512]), ps("ps_y", [P, 512])
        qk_in, v_in, win_in, mask_in, z_in = sem("qk_in"), [sem("v_in0"), sem("v_in1")], sem("win_in"), sem("mask_in"), sem("z_in")
        ck_turned, ck_done, sk_done, sk_out = sem("ck_turned"), sem("ck_done"), sem("sk_done"), sem("sk_out")
        hi_done, lo_done, col_done, tab_done = sem("qk_hi"), sem("qk_lo"), sem("cols_done"), sem("tables_done")
        s_mm, red, negmax, exp_done = sem("scores_mm"), sem("maxima"), sem("negmax"), sem("exp_done")
        tr_done, pt_win, pt_ctx, pv_done = sem("probs_turned"), sem("pt_win"), sem("pt_ctx"), sem("pv_done")
        ones_set, inv_done, normed, o_done, y_turned, y_done, y_out = sem("ones_set_v"), sem("inv_done"), sem("o_normed"), sem("o_done"), sem("y_turned"), sem("y_done"), sem("y_out")

        TILES = [(u, i) for u in range(2) for i in range(TPH)]
        red_before = [min(i, LT) * 2 + max(i - LT, 0) for i in range(TPH + 1)]
        GROUPS = TPH // NG
        PREP_AT = (6, 4)
        SPLIT_AT = (7, 5)

        def keys_of(buf, u, i):
            if i >= LT:
                return None, buf[:, u, LAT:TOK]
            kr0, nr, _ = BANDS[i // 4]
            kc0, w, _ = SETS[i % 4]
            grid = buf[:, u, 0:LAT].rearrange("p (r c) -> p r c", c=GRID)
            return grid[:, kr0:kr0 + nr, kc0:kc0 + w], buf[:, u, TOK:KW]

        def n_keys(i):
            return 0 if i >= LT else BANDS[i // 4][1] * SETS[i % 4][1]

        block = ctx.enter_context(nc.Block())

        def load_window(q, n, free):
            if free:
                q.wait_ge(col_done, 3 * n)
            for r in range(QR):
                at = (QR - 1 - r) * BW_C
                q.dma_start(window[QC * r:QC * r + QC], io.table[ds(n, 1), :, at:at + BW_R * BW_C]
                             .rearrange("h q x -> (h q) x")).then_inc(win_in, 16)

        def pairs(eng, body):
            body(0, True, False)
            with eng.Fori(1, HEADS // 2 - 1) as hp:
                body(hp, False, False)
            body(HEADS // 2 - 1, False, True)

        @block.sync
        def _(sp):
            sp.sem_inc(y_out, DMA_START)

            def load_qk(n, free):
                if free:
                    sp.wait_ge(lo_done, 10 * n)
                    sp.wait_ge(sk_done, n)
                for half in range(2):
                    part = slice(DH * half, DH * half + DH)
                    sp.dma_start(q_raw[part], io.proj[ds(Q0 + n * DH, DH)]).then_inc(qk_in, 16)
                    sp.dma_start(k_raw[part, 0:TOK], io.proj[ds(K0 + n * DH, DH)]).then_inc(qk_in, 16)
                    sp.dma_start(ck_raw[:, :, part], io.cache_k[:, ds(n * DH, DH)].rearrange("(t p) d -> p t d", p=P)
                                 ).then_inc(qk_in, 16)

            def load_v(n, u, pv_before):
                if pv_before is not None:
                    sp.wait_ge(pv_done, START + pv_before)
                for b, (kc0, w, _) in enumerate(SETS):
                    for r in range(4):
                        src = io.v[0:LAT].rearrange("(rb r c) d -> r c rb d", r=4, c=GRID)[r, kc0:kc0 + w, :, ds(n * DH, DH)]
                        sp.dma_start(v_win[w * r:w * r + w, u, b, :, 0:DH], src).then_inc(v_in[u], 16)
                sp.dma_start(v_ctx[:, u, 0:2, 0:DH], io.cache_v[:, ds(n * DH, DH)].rearrange("(t p) d -> p t d", p=P)
                             ).then_inc(v_in[u], 16)
                sp.dma_start(v_ctx[:, u, 2:4, 0:DH], io.v[LAT:TOK, ds(n * DH, DH)].rearrange("(t p) d -> p t d", p=P)
                             ).then_inc(v_in[u], 16)

            load_qk(0, False)
            load_v(0, 0, None)
            load_window(sp, 1, True)
            load_qk(1, True)

            def body(hp, last):
                load_v(2 * hp + 1, 1, hp * TPP)
                sp.wait_ge(y_done, START + hp * TPH)
                sp.dma_start(z_sb[:], io.proj[ds(ZA0 + hp * P, P)]).then_inc(z_in, 16)
                if not last:
                    load_window(sp, 2 * hp + 2, True)
                    load_qk(2 * hp + 2, True)
                    load_v(2 * hp + 2, 0, hp * TPP + TPH)
                    load_qk(2 * hp + 3, True)
                    load_window(sp, 2 * hp + 3, True)
                sp.wait_ge(y_done, START + hp * TPH + TPH)
                sp.dma_start(io.ya[ds(hp * P, P)], y_sb[:]).then_inc(y_out, 16)

            with sp.Fori(0, HEADS // 2 - 1) as hp:
                body(hp, False)
            body(HEADS // 2 - 1, True)
            sp.wait_ge(y_out, DMA_START + 16 * HEADS // 2)

        @block.tensor
        def _(pe):
            for counter in (pv_done, y_turned):
                pe.sem_inc(counter, START)

            def turn_keys(n, y_before):
                pe.wait_ge(qk_in, 96 * n + 96)
                pe.wait_ge(y_done, START + y_before)
                pe.wait_ge(ck_done, n)
                pe.wait_ge(sk_done, n)
                for t in range(2):
                    pe.transpose(ps_y[:, P * t:P * t + P], ck_raw[:, t], cst.ident[:])
                for t in range(2):
                    tr = pe.transpose(ps_y[:, 256 + DH * t:256 + DH * t + DH], k_raw[0:DH, LAT + P * t:LAT + P * t + P],
                                      cst.ident[0:DH, 0:DH])
                tr.then_inc(ck_turned, 1)

            def scores(u, i, m, parts_before):
                if i == 0:
                    pe.wait_ge(lo_done, parts_before + 10 * u + 10)
                q = q_sp[:, u, P * i:P * i + P]
                (w_hi, c_hi), (w_lo, c_lo) = keys_of(k_hi, u, i), keys_of(k_lo, u, i)
                nk = n_keys(i)
                if nk:
                    pe.matmul(ps_win[m % 2][:, 0:nk], q, w_hi, start=True, stop=False)
                    pe.matmul(ps_win[m % 2][:, 0:nk], q, w_lo, start=False, stop=True)
                pe.matmul(ps_ctx[m % 2][:, 0:CTX], q, c_hi, start=True, stop=False)
                pe.matmul(ps_ctx[m % 2][:, 0:CTX], q, c_lo, start=False, stop=True).then_inc(s_mm, 1)

            def turn_probs(u, i, base, m):
                pe.wait_ge(exp_done, base + m + 1)
                pe.wait_ge(pt_win, START + base + m)
                pe.wait_ge(pt_ctx, START + base + m)
                if i < LT:
                    w4, nb = 4 * SETS[i % 4][1], BANDS[i // 4][1] // 4
                    for j in range(nb):
                        pe.transpose(ps_tw[0:w4, j], p_sb[:, m % 2, w4 * j:w4 * j + w4], cst.ident[:])
                for j in range(2):
                    tr = pe.transpose(ps_tc[:, j], p_sb[:, m % 2, 512 + P * j:512 + P * j + P], cst.ident[:])
                tr.then_inc(tr_done, 1)

            def weigh_values(u, i, base, m, v_count):
                if i == 0:
                    pe.wait_ge(v_in[u], v_count)
                if m == TPP - 1 and v_count is not None:
                    pe.wait_ge(pt_win, START + base + m + 1)
                    pe.wait_ge(pt_ctx, START + base + m + 1)
                pe.wait_ge(o_done, START + base + m)
                nb = 0
                if i < LT:
                    w4, nb, rb0 = 4 * SETS[i % 4][1], BANDS[i // 4][1] // 4, BANDS[i // 4][0] // 4
                    for j in range(nb):
                        pe.matmul(ps_o[:, 0:DH + 1], pT[0:w4, m % 2, j], v_win[0:w4, u, i % 4, rb0 + j],
                                  start=(j == 0), stop=False)
                for j in range(2):
                    mm = pe.matmul(ps_o[:, 0:DH + 1], pT[:, m % 2, 4 + j], v_ctx[:, u, (2 if i >= LT else 0) + j],
                                   start=(nb == 0 and j == 0), stop=(j == 1))
                mm.then_inc(pv_done, 1)

            def turn_out(g, g_base, y_base, keys):
                pe.wait_ge(sk_done, keys)
                pe.wait_ge(normed, g_base + g + 1)
                pe.wait_ge(y_done, START + y_base + NG * g)
                for t in range(NG):
                    tr = pe.transpose(ps_y[:, P * t:P * t + P], o_norm[:, g % 2, t], cst.ident[:])
                tr.then_inc(y_turned, 1)

            pe.wait_ge(ones_set, 2)
            turn_keys(0, 0)
            for m in (0, 1):
                scores(*TILES[m], m, 0)

            def body(hp, first, last):
                base = hp * TPP
                for m, (u, i) in enumerate(TILES):
                    turn_probs(u, i, base, m)
                    if m + 2 < TPP:
                        scores(*TILES[m + 2], m + 2, hp * 20)
                    elif not last:
                        scores(*TILES[m + 2 - TPP], m + 2, hp * 20 + 20)
                    if m >= 1:
                        weigh_values(*TILES[m - 1], base, m - 1, 288 * (hp + 1))
                    elif not first:
                        weigh_values(*TILES[-1], base, -1, None)
                    if i == PREP_AT[u] and not (last and u == 1):
                        turn_keys(2 * hp + u + 1, hp * TPH)
                    if u == 1 and i >= 5 and i % NG == 2:
                        turn_out(i // NG - 1, hp * GROUPS, hp * TPH, 2 * hp + (2 if last else 3))
                    if m == 2 and not first:
                        turn_out(-1, hp * GROUPS, hp * TPH, 2 * hp + 1)
                if last:
                    weigh_values(*TILES[-1], base, TPP - 1, 288 * (hp + 1))
                    turn_out(GROUPS - 1, hp * GROUPS, hp * TPH, 2 * hp + 2)

            pairs(pe, body)

        def split_low(eng, n, u):
            low = slice(DH, P)
            for part in range(5):
                if part:
                    wait_reg(eng, lo_done, 10 * n + 2 * part)
                wait_reg(eng, hi_done, 5 * n + part + 1)
                if part < 4:
                    src = q_raw[low, 512 * part:512 * part + 512].rearrange("p (r b c) -> p b r c", r=QR, b=4)
                    dst = q_sp[low, u, 512 * part:512 * part + 512].rearrange("p (b r c) -> p b r c", b=4, r=QR)
                    for b in range(4):
                        op = eng.tensor_tensor(dst[:, b], src[:, b], dst[:, b].bitcast(F32), ALU.subtract)
                else:
                    at = slice(LAT, TOK)
                    op = eng.tensor_tensor(q_sp[low, u, at], q_raw[low, at], q_sp[low, u, at].bitcast(F32), ALU.subtract)
                op.then_inc(lo_done, 1)
                wait_reg(eng, lo_done, 10 * n + 2 * part + 1)
                at = slice(512 * part, 512 * part + 512) if part < 4 else slice(LAT, KW)
                eng.tensor_tensor(k_lo[:, u, at], k_raw[:, at], k_hi[:, u, at].bitcast(F32), ALU.subtract).then_inc(lo_done, 1)

        @block.vector
        def _(dve):
            for counter in (y_done, pt_win, negmax):
                dve.sem_inc(counter, START)

            def split_high(n, u, part):
                if part == 0:
                    wait_reg(dve, qk_in, 96 * n + 96)
                if part < 4:
                    src = q_raw[:, 512 * part:512 * part + 512].rearrange("p (r b c) -> p b r c", r=QR, b=4)
                    dst = q_sp[:, u, 512 * part:512 * part + 512].rearrange("p (b r c) -> p b r c", b=4, r=QR)
                    dve.tensor_copy(dst, src)
                    at = slice(512 * part, 512 * part + 512)
                    dve.tensor_copy(k_hi[:, u, at], k_raw[:, at]).then_inc(hi_done, 1)
                else:
                    wait_reg(dve, ck_done, n + 1)
                    dve.tensor_copy(q_sp[:, u, LAT:TOK], q_raw[:, LAT:TOK])
                    dve.tensor_copy(k_hi[:, u, LAT:KW], k_raw[:, LAT:KW]).then_inc(hi_done, 1)

            def soften(u, i, base, m, ready):
                nk, st = n_keys(i), stat[:, m % 4]
                if i == 0:
                    wait_reg(dve, tab_done, ready)
                wait_reg(dve, s_mm, base + m + 1)
                if nk:
                    off = T_OFF[BANDS[i // 4][2], SETS[i % 4][2]]
                    dve.tensor_tensor_reduce(s_sb[:, m % 2, 0:nk], ps_win[m % 2][:, 0:nk], tables[:, u, off:off + nk],
                                             1.0, -3e38, ALU.add, ALU.max, st[:, 0:1]).then_inc(red, 1)
                dve.reduce_max(st[:, 1:2], ps_ctx[m % 2][:, 0:CTX], AX_X).then_inc(red, 1)

            def negate_max(u, i, base, m, rbase):
                nk, st = n_keys(i), stat[:, m % 4]
                wait_reg(dve, red, rbase + u * RED + red_before[i + 1])
                if nk:
                    dve.tensor_scalar(st[:, 2:3], st[:, 0:1], st[:, 1:2], -1.0, ALU.max, ALU.mult).then_inc(negmax, 1)
                else:
                    dve.tensor_scalar(st[:, 2:3], st[:, 1:2], -1.0, None, ALU.mult).then_inc(negmax, 1)

            def copy_window(u, i, base, m, first):
                if m >= 2 or not first:
                    wait_reg(dve, pv_done, START + base + m - 1)
                wait_reg(dve, tr_done, base + m + 1)
                w4, nb = (4 * SETS[i % 4][1], BANDS[i // 4][1] // 4) if i < LT else (P, 0)
                if nb:
                    dve.tensor_copy(pT[0:w4, m % 2, 0:nb], ps_tw[0:w4, 0:nb]).then_inc(pt_win, 1)
                else:
                    dve.sem_inc(pt_win, 1)

            def invert(g, o_ready):
                wait_reg(dve, o_done, START + o_ready)
                dve.reciprocal(inv[:], o_sb[:, NG * g:NG * g + NG, :, DH]).then_inc(inv_done, 1)

            def norm_out(g, g_base):
                o, out = o_sb[:, NG * g:NG * g + NG, :, 0:DH], o_norm[:, g % 2].rearrange("p t (u d) -> p t u d", u=2)
                wait_reg(dve, inv_done, g_base + g + 1)
                dve.tensor_tensor(out, o, inv[:].unsqueeze(3).to_broadcast([P, NG, 2, DH]), ALU.mult).then_inc(normed, 1)

            def gate_out(i, g_base, z_ready):
                if i % NG == 0:
                    wait_reg(dve, y_turned, START + g_base + i // NG + 1)
                o_t = ps_y[:, P * (i % NG):P * (i % NG) + P]
                if i == 0:
                    wait_reg(dve, z_in, z_ready)
                    wait_reg(dve, y_out, DMA_START + z_ready - 16)
                if i >= LT:
                    at = slice(LAT + P * (i - LT), LAT + P * (i - LT) + P)
                    dve.tensor_tensor(y_sb[:, at], o_t, z_sb[:, at], ALU.mult).then_inc(y_done, 1)
                    return
                a, b = i // 4, i % 4
                y, z = (x[:, 512 * a:512 * a + 512].rearrange("p (r b c) -> p b r c", r=QR, b=4)[:, b] for x in (y_sb, z_sb))
                dve.tensor_tensor(y, o_t.rearrange("p (r c) -> p r c", c=QC), z, ALU.mult).then_inc(y_done, 1)

            for part in range(5):
                split_high(0, 0, part)
            split_low(dve, 0, 0)
            for m in (0, 1):
                soften(*TILES[m], 0, m, 1)
                negate_max(*TILES[m], 0, m, 0)

            def body(hp, first, last):
                base, rbase = hp * TPP, hp * 2 * RED
                for m, (u, i) in enumerate(TILES):
                    copy_window(u, i, base, m, first)
                    ahead = m + 2 < TPP or not last
                    (u2, i2), over = TILES[(m + 2) % TPP], (m + 2) // TPP
                    if ahead:
                        soften(u2, i2, base, m + 2, 2 * (hp + over) + u2 + 1)
                    g, end_of_group = i // NG - 1, i % NG == 1
                    if u == 1 and i >= 6:
                        gate_out(i - 6, hp * GROUPS, 16 * (hp + 1))
                    if m < 6 and not first:
                        gate_out(TPH - 6 + m, (hp - 1) * GROUPS, 16 * hp)
                    if u == 1 and g >= 0 and end_of_group:
                        invert(g, base + m - 1)
                    if m == 1 and not first:
                        invert(GROUPS - 1, base)
                    if ahead:
                        negate_max(u2, i2, base, m + 2, rbase + over * 2 * RED)
                    if u == 1 and g >= 0 and end_of_group:
                        norm_out(g, hp * GROUPS)
                    if m == 1 and not first:
                        norm_out(GROUPS - 1, (hp - 1) * GROUPS)
                    if 0 <= i - SPLIT_AT[u] < 5 and not (last and u == 1):
                        split_high(2 * hp + u + 1, 1 - u, i - SPLIT_AT[u])
                if last:
                    invert(GROUPS - 1, base + TPP)
                    norm_out(GROUPS - 1, hp * GROUPS)
                    for i in range(TPH - 6, TPH):
                        gate_out(i, hp * GROUPS, 16 * (hp + 1))

            pairs(dve, body)

        @block.scalar
        def _(act):
            act.dma_start(rmask[:], io.row_mask.rearrange("t p r -> p t r")).then_inc(mask_in, 16)
            act.dma_start(cmask[:], io.col_mask.rearrange("t p r -> p t r")).then_inc(mask_in, 16)
            load_window(act, 0, False)
            for counter in (pt_ctx, o_done):
                act.sem_inc(counter, START)

            def copy_keys(n, first=False):
                wait_reg(act, ck_turned, n + 1)
                act.activation(k_raw[:, TOK:KW], ps_y[:, 0:CTX], ACT.Copy).then_inc(ck_done, 1)
                if not first:
                    wait_reg(act, sk_out, 16 * n)
                act.activation(sk_sb[:], ps_y[:, 256:256 + P].rearrange("p (t d) -> p t d", t=2), ACT.Copy).then_inc(sk_done, 1)
                wait_reg(act, sk_done, n + 1)
                act.dma_start(io.state_k[:, ds(n * DH, DH)].rearrange("(t p) d -> p t d", p=P), sk_sb[:]).then_inc(sk_out, 16)

            def exponents(u, i, base, m):
                nk, st = n_keys(i), stat[:, m % 4]
                wait_reg(act, negmax, START + base + m + 1)
                if nk:
                    act.activation(p_sb[:, m % 2, 0:nk], s_sb[:, m % 2, 0:nk], ACT.Exp, bias=st[:, 2:3])
                act.activation(p_sb[:, m % 2, 512:768], ps_ctx[m % 2][:, 0:CTX], ACT.Exp, bias=st[:, 2:3]).then_inc(exp_done, 1)

            def copy_context(u, i, base, m):
                wait_reg(act, tr_done, base + m + 1)
                act.activation(pT[:, m % 2, 4:6], ps_tc[:, 0:2], ACT.Copy).then_inc(pt_ctx, 1)

            def copy_out(u, i, base, m):
                wait_reg(act, pv_done, START + base + m + 1)
                act.activation(o_sb[:, i, u], ps_o[:, 0:DH + 1], ACT.Copy).then_inc(o_done, 1)

            copy_keys(0, True)
            exponents(*TILES[0], 0, 0)

            def body(hp, first, last):
                base = hp * TPP
                for m, (u, i) in enumerate(TILES):
                    if m + 1 < TPP or not last:
                        exponents(*TILES[(m + 1) % TPP], base, m + 1)
                    copy_context(u, i, base, m)
                    if m == 1 and not first:
                        wait_reg(act, y_turned, START + hp * GROUPS - 1)
                    if m == PREP_AT[0] and not first:
                        wait_reg(act, y_turned, START + hp * GROUPS)
                    if m >= 1:
                        copy_out(*TILES[m - 1], base, m - 1)
                    elif not first:
                        copy_out(*TILES[-1], base, -1)
                    if i == PREP_AT[u] and not (last and u == 1):
                        copy_keys(2 * hp + u + 1)
                if last:
                    copy_out(*TILES[-1], base, TPP - 1)

            pairs(act, body)
            act.wait_ge(sk_out, 16 * HEADS)

        @block.gpsimd
        def _(pool):
            def bias_tables(n, u, s_before):
                wait_reg(pool, win_in, 128 * n + 128)
                wait_reg(pool, negmax, START + s_before)
                wait_reg(pool, tab_done, n)
                win = window[:].rearrange("p (r c) -> p r c", c=BW_C)
                for ct, (c0, w) in enumerate(COL_TYPES):
                    pool.tensor_tensor(win_c[:, ct, 0:16 * w].rearrange("p (r c) -> p r c", c=w), win[:, :, c0:c0 + w],
                                       cmask[:, ct, 0:w].unsqueeze(1).to_broadcast([P, 16, w]), ALU.add).then_inc(col_done, 1)
                wait_reg(pool, col_done, 3 * n + 3)
                for (rt, ct), off in T_OFF.items():
                    (r0, nr), w = ROW_TYPES[rt], COL_TYPES[ct][1]
                    op = pool.tensor_tensor(tables[:, u, off:off + nr * w].rearrange("p (r c) -> p r c", c=w),
                                            win_c[:, ct, w * r0:w * (r0 + nr)].rearrange("p (r c) -> p r c", c=w),
                                            rmask[:, rt, 0:nr].unsqueeze(2).to_broadcast([P, nr, w]), ALU.add)
                op.then_inc(tab_done, 1)

            def prepare(n, u, s_before):
                bias_tables(n, u, s_before)
                wait_reg(pool, tab_done, n + 1)
                split_low(pool, n, u)

            pool.memset(v_win[:, :, :, :, DH:DH + 1], 1.0).then_inc(ones_set, 1)
            pool.memset(v_ctx[:, :, :, DH:DH + 1], 1.0).then_inc(ones_set, 1)
            pool.wait_ge(mask_in, 32)
            bias_tables(0, 0, 0)
            with pool.Fori(0, HEADS // 2 - 1) as hp:
                prepare(2 * hp + 1, 1, hp * TPP)
                prepare(2 * hp + 2, 0, hp * TPP + TPH)
            prepare(HEADS - 1, 1, (HEADS // 2 - 1) * TPP)


CH = 256
NCH = TOK // CH


WG = 256


def split_weights(nc, srcs, stage, w_hi, w_lo, w_in, w_hi_done, w_lo_done):
    def load(sp, c):
        if c >= 2:
            sp.wait_ge(w_lo_done, c - 1)
        at = 0
        for src in srcs:
            n = src.shape[0] // P
            sp.dma_start(stage[:, c % 2, at:at + n], src[:, WG * c:WG * c + WG].rearrange("(k p) n -> p k n", p=P)
                         ).then_inc(w_in[c % 2], 16)
            at += n

    def high(act, c):
        act.wait_ge(w_in[c % 2], 16 * len(srcs) * (c // 2 + 1))
        act.activation(w_hi[:, :, WG * c:WG * c + WG], stage[:, c % 2], ACT.Copy).then_inc(w_hi_done, 1)

    def low(dve, c):
        dve.wait_ge(w_hi_done, c + 1)
        cols = slice(WG * c, WG * c + WG)
        dve.tensor_tensor(w_lo[:, :, cols], stage[:, c % 2], w_hi[:, :, cols].bitcast(F32), ALU.subtract).then_inc(w_lo_done, 1)
    return load, high, low


def merge(nc, io, cst):
    with ExitStack() as ctx:
        sb = lambda n, s, d=F32: ctx.enter_context(nc.sbuf_tensor(n, s, d))
        sem = lambda n: ctx.enter_context(nc.semaphore(n))
        stage, w_hi, w_lo = sb("wp_stage", [P, 2, 8, WG]), sb("wp_hi", [P, 8, D], F32R), sb("wp_lo", [P, 8, D], F32R)
        ya, cv, zb = (sb(n, [P, 2, 4, CH]) for n in ("ya_in", "cv_in", "zb_in"))
        gates = sb("gates_in", [P, 2, 2 * KC, CH])
        y_hi, y_lo = sb("y_hi", [P, 2, 8, CH], F32R), sb("y_lo", [P, 2, 8, CH], F32R)
        act_sb, yb = sb("ln_silu", [P, 4, CH]), sb("yb", [P, 4, CH])
        normed = sb("normed", [P, 2, WB])
        bn, mv, var_eps, rstd, shift, half = (sb(n, [P, 2, w]) for n, w in (
            ("bn", 6), ("mv", 2), ("var_eps", 1), ("ln_rstd", 1), ("ln_shift", 1), ("ln_half", 1)))
        gated, m_sb = sb("gated", [P, 2, 2, CH]), sb("m_out", [P, 2, KC, CH])
        ps_o = ctx.enter_context(nc.psum_tensor("ps_proj", [P, 4, 2, CH], F32))
        ps_n = ctx.enter_context(nc.psum_tensor("ps_norm", [P, 2, WB], F32))
        ps_b = ctx.enter_context(nc.psum_tensor("ps_back", [P, 4, CH], F32))
        w_in, w_hid, w_lod = [sem("wp_in0"), sem("wp_in1")], sem("wp_hid"), sem("wp_lod")
        s_in, g_in = [sem("s_in0"), sem("s_in1")], [sem("g_in0"), sem("g_in1")]
        t_in, bn_done, mv_done, rs_done, sh_done, n_done = (sem(n) for n in ("t_in", "bn_done", "mv_done", "rs_done", "sh_done", "n_done"))
        t_back, silu_done, yb_done, hi_done, lo_done, half_set = (sem(n) for n in ("t_back", "silu_m", "yb_done", "y_hid", "y_lod", "half_m"))
        mm, gated_done, m_done, m_out = sem("proj_mm"), sem("gated_done"), sem("m_done"), [sem("m_out0"), sem("m_out1")]
        load_w, high_w, low_w = split_weights(nc, (io.w_proj_a, io.w_proj_b), stage, w_hi, w_lo, w_in, w_hid, w_lod)
        GD0 = 4
        block = ctx.enter_context(nc.Block())

        def chunks(eng, body):
            with eng.Fori(0, NCH // 2) as t:
                body(2 * t, t, 0, False)
                body(2 * t + 1, t, 1, False)
            body(NCH - 1, NCH // 2, 0, True)

        @block.sync
        def _(sp):
            def small(j, par):
                for src, dst in ((io.conv, cv), (io.ya, ya), (io.proj[ZB0:ZB0 + WB], zb)):
                    sp.dma_start(dst[:, par], src[:, ds(CH * j, CH)].rearrange("(b p) t -> p b t", p=P)).then_inc(s_in[par], 16)

            def big(j, par):
                sp.dma_start(gates[:, par], io.proj[G0:D_IN, ds(CH * j, CH)].rearrange("(b p) t -> p b t", p=P)
                             ).then_inc(g_in[par], 16)

            small(0, 0)
            load_w(sp, 0)
            load_w(sp, 1)
            big(0, 0)
            load_w(sp, 2)
            load_w(sp, 3)
            small(1, 1)

            def body(j, par):
                wait_reg(sp, gated_done, GD0 + 8 * j)
                big(j + 1, 1 - par)
                wait_reg(sp, lo_done, 2 * j + 2)
                small(j + 2, par)

            with sp.Fori(0, NCH // 2 - 1) as t:
                body(2 * t, 0)
                body(2 * t + 1, 1)
            body(NCH - 3, 0)
            sp.wait_ge(gated_done, GD0 + 8 * (NCH - 2))
            big(NCH - 1, 0)

        @block.gpsimd
        def _(pool):
            pool.memset(half[:], -0.5).then_inc(half_set, 1)
            pool.wait_ge(half_set, 1)

            def norm_and_split(j, jh, par):
                wait_reg(pool, mv_done, 2 * j + 2)
                pool.tensor_scalar(var_eps[:], mv[:, :, 1:2], EPS, None, ALU.add).then_inc(rs_done, 1)
                wait_reg(pool, rs_done, 2 * j + 1)
                pool.tensor_tensor(rstd[:], var_eps[:], half[:], ALU.pow).then_inc(rs_done, 1)
                wait_reg(pool, hi_done, 2 * j + 1)
                pool.tensor_tensor(y_lo[:, par, 0:4], ya[:, par], y_hi[:, par, 0:4].bitcast(F32), ALU.subtract).then_inc(lo_done, 1)
                wait_reg(pool, hi_done, 2 * j + 2)
                pool.tensor_tensor(y_lo[:, par, 4:8], yb[:], y_hi[:, par, 4:8].bitcast(F32), ALU.subtract).then_inc(lo_done, 1)

            norm_and_split(0, 0, 0)
            chunks(pool, lambda j, jh, par, last: None if last else norm_and_split(j + 1, jh, 1 - par))

        @block.tensor
        def _(pe):
            def turn_in(j, jh, par):
                pe.wait_ge(s_in[par], 48 * (jh + 1))
                pe.wait_ge(n_done, 2 * j)
                for t in range(2):
                    for b in range(4):
                        tr = pe.transpose(ps_n[:, t, P * b:P * b + P], cv[:, par, b, P * t:P * t + P], cst.ident[:])
                tr.then_inc(t_in, 1)

            def turn_back(j):
                pe.wait_ge(n_done, 2 * j + 2)
                pe.wait_ge(silu_done, 4 * j)
                for b in range(4):
                    for t in range(2):
                        tr = pe.transpose(ps_b[:, b, P * t:P * t + P], normed[:, t, P * b:P * b + P], cst.ident[:])
                tr.then_inc(t_back, 1)

            def next_half(jh, par):
                return jh + par

            turn_in(0, 0, 0)
            turn_back(0)

            def body(j, jh, par, last):
                for n in range(16):
                    half_no, o = n // 4 % 2, 4 * (n // 8) + n % 4
                    if n % 4 == 0 and n < 8:
                        pe.wait_ge(lo_done, 2 * j + 1 + half_no)
                    if half_no == 0:
                        pe.wait_ge(w_lod, P * o // WG + 1)
                        pe.wait_ge(gated_done, GD0 + 8 * j + o + 1 - 4)
                    out = ps_o[:, o % 4, half_no]
                    for k in range(4):
                        kk, col = 4 * half_no + k, slice(P * o, P * o + P)
                        pe.matmul(out, w_hi[:, kk, col], y_hi[:, par, kk], start=(k == 0), stop=False)
                        pe.matmul(out, w_hi[:, kk, col], y_lo[:, par, kk], start=False, stop=False)
                        last_mm = pe.matmul(out, w_lo[:, kk, col], y_hi[:, par, kk], start=False, stop=(k == 3))
                    if half_no:
                        last_mm.then_inc(mm, 1)
                    if not last and n == 4:
                        turn_in(j + 1, next_half(jh, par), 1 - par)
                    if not last and n == 10:
                        turn_back(j + 1)

            chunks(pe, body)

        @block.scalar
        def _(act):
            for counter in m_out:
                act.sem_inc(counter, DMA_START)

            def norm(j):
                wait_reg(act, sh_done, j + 1)
                wait_reg(act, t_back, j)
                for t in range(2):
                    act.activation(normed[:, t], ps_n[:, t], ACT.Identity, bias=shift[:, t], scale=rstd[:, t]).then_inc(n_done, 1)

            def silu(j):
                wait_reg(act, t_back, j + 1)
                wait_reg(act, yb_done, j)
                for b in range(4):
                    act.activation(act_sb[:, b], ps_b[:, b], ACT.Silu, bias=cst.cols[:, R_LNB + b:R_LNB + b + 1],
                                   scale=cst.cols[:, R_LNG + b:R_LNG + b + 1]).then_inc(silu_done, 1)

            high_w(act, 0)
            norm(0)
            high_w(act, 1)
            silu(0)
            high_w(act, 2)
            high_w(act, 3)

            def body(j, jh, par, last):
                if not last:
                    norm(j + 1)
                    silu(j + 1)
                wait_reg(act, m_done, 8 * j + 8)
                act.dma_start(io.m[:, ds(CH * j, CH)].rearrange("(b p) t -> p b t", p=P), m_sb[:, par]).then_inc(m_out[par], 16)

            chunks(act, body)
            act.wait_ge(m_out[0], DMA_START + 16 * (NCH // 2 + 1))
            act.wait_ge(m_out[1], DMA_START + 16 * (NCH // 2))

        @block.vector
        def _(dve):
            def stats(j):
                wait_reg(dve, t_in, j + 1)
                for t in range(2):
                    dve.bn_stats(bn[:, t], ps_n[:, t]).then_inc(bn_done, 1)
                wait_reg(dve, bn_done, 2 * j + 2)
                for t in range(2):
                    dve.bn_aggr(mv[:, t], bn[:, t]).then_inc(mv_done, 1)
                wait_reg(dve, rs_done, 2 * j + 2)
                dve.scalar_tensor_tensor(shift[:], mv[:, :, 0:1], -1.0, rstd[:], ALU.mult, ALU.mult).then_inc(sh_done, 1)

            def high(j, jh, par, part):
                if part == 0:
                    wait_reg(dve, s_in[par], 48 * (jh + 1))
                    dve.tensor_copy(y_hi[:, par, 0:4], ya[:, par]).then_inc(hi_done, 1)
                else:
                    wait_reg(dve, silu_done, 4 * j + 4)
                    wait_reg(dve, lo_done, 2 * j)
                    dve.tensor_tensor(yb[:], act_sb[:], zb[:, par], ALU.mult).then_inc(yb_done, 1)
                    wait_reg(dve, yb_done, j + 1)
                    dve.tensor_copy(y_hi[:, par, 4:8], yb[:]).then_inc(hi_done, 1)

            dve.sem_inc(gated_done, GD0)
            stats(0)
            high(0, 0, 0, 0)
            low_w(dve, 0)
            low_w(dve, 1)
            high(0, 0, 0, 1)
            low_w(dve, 2)
            low_w(dve, 3)

            def body(j, jh, par, last):
                wait_reg(dve, g_in[par], 16 * (jh + 1))
                wait_reg(dve, m_out[par], DMA_START + 16 * jh)
                for o in range(8):
                    n = 8 * j + o
                    wait_reg(dve, mm, n + 1)
                    dve.tensor_tensor(gated[:, o % 2], ps_o[:, o % 4], gates[:, par, o:o + KC + 1:KC], ALU.mult).then_inc(gated_done, 1)
                    wait_reg(dve, gated_done, GD0 + n + 1)
                    dve.tensor_tensor(m_sb[:, par, o], gated[:, o % 2, 0], gated[:, o % 2, 1], ALU.add).then_inc(m_done, 1)
                    if not last and o == 1:
                        stats(j + 1)
                    if not last and o == 2:
                        high(j + 1, jh + par, 1 - par, 0)
                    if not last and o == 5:
                        high(j + 1, jh + par, 1 - par, 1)

            chunks(dve, body)


def finish(nc, io, cst):
    with ExitStack() as ctx:
        sb = lambda n, s, d=F32: ctx.enter_context(nc.sbuf_tensor(n, s, d))
        sem = lambda n: ctx.enter_context(nc.semaphore(n))
        stage, w_hi, w_lo = sb("wo_stage", [P, 2, KC, WG]), sb("wo_hi", [P, KC, D], F32R), sb("wo_lo", [P, KC, D], F32R)
        m_in, x_in = sb("m_in", [P, 2, KC, CH]), sb("x_in", [P, 2, 2, D])
        m_hi, m_lo = sb("m_hi", [P, 2, KC, CH], F32R), sb("m_lo", [P, 2, KC, CH], F32R)
        gate_bc, fg = sb("gate_rows", [P, 2, D]), sb("final_g", [P, D])
        z, square = sb("z_res", [P, 2, D]), sb("z_square", [P, D])
        ssum, tmp, rstd, half = (sb(n, [P, 2, 1]) for n in ("z_ssum", "z_tmp", "z_rstd", "z_half"))
        psF = ctx.enter_context(nc.psum_tensor("psF", [P, 2, 2, 2, 512], F32))
        w_in, w_hid, w_lod = [sem("wo_in0"), sem("wo_in1")], sem("wo_hid"), sem("wo_lod")
        m_ins, x_ins, fg_in = [sem("m_in0"), sem("m_in1")], [sem("x_in0_"), sem("x_in1_")], sem("fg_in")
        gate_mm, gate_out, half_set = sem("gate_mm"), sem("gate_out"), sem("half_f")
        hi_done, lo_done, mm, scaled, z_done, sq_done, rs_done, y_done = (
            sem(n) for n in ("m_hid", "m_lod", "out_mm", "gated_f", "z_done", "z_sq", "z_rs", "y_fin"))
        y_out = [sem("y_out0"), sem("y_out1")]
        load_w, high_w, low_w = split_weights(nc, (io.w_out,), stage, w_hi, w_lo, w_in, w_hid, w_lod)
        SC0 = 8
        block = ctx.enter_context(nc.Block())

        def chunks(eng, body):
            with eng.Fori(0, NCH // 2) as t:
                body(2 * t, t, 0, False)
                body(2 * t + 1, t, 1, False)
            body(NCH - 1, NCH // 2, 0, True)

        @block.sync
        def _(sp):
            def load_m(j, par):
                sp.dma_start(m_in[:, par], io.m[:, ds(CH * j, CH)].rearrange("(b p) t -> p b t", p=P)).then_inc(m_ins[par], 16)

            def load_x(j, par, last):
                x = io.x_prompt if last else io.x_sample[ds(CH * j, CH)]
                sp.dma_start(x_in[:, par], x.rearrange("(t p) d -> p t d", p=P)).then_inc(x_ins[par], 16)

            def load(j, par, last):
                load_m(j, par)
                load_x(j, par, last)

            load_m(0, 0)
            load_w(sp, 0)
            for c in range(1, 4):
                load_w(sp, c)
            load_x(0, 0, False)
            sp.dma_start(fg[:], io.final_g.partition_broadcast(P)).then_inc(fg_in, 16)
            load(1, 1, False)

            def again(j, last):
                wait_reg(sp, lo_done, j - 1)
                wait_reg(sp, z_done, 4 * (j - 1))
            with sp.Fori(1, NCH // 2) as t:
                again(2 * t, False)
                load(2 * t, 0, False)
                again(2 * t + 1, False)
                load(2 * t + 1, 1, False)
            again(NCH - 1, True)
            load(NCH - 1, 0, True)

        @block.gpsimd
        def _(pool):
            pool.memset(half[:], -0.5).then_inc(half_set, 1)
            pool.wait_ge(half_set, 1)

            def low(j, par):
                wait_reg(pool, hi_done, j + 1)
                pool.tensor_tensor(m_lo[:, par], m_in[:, par], m_hi[:, par].bitcast(F32), ALU.subtract).then_inc(lo_done, 1)
            low(0, 0)

            def body(j, jh, par, last):
                if not last:
                    low(j + 1, 1 - par)
                for t in range(2):
                    n = 2 * j + t
                    wait_reg(pool, sq_done, n + 1)
                    pool.tensor_scalar(tmp[:, t], ssum[:, t], 1.0 / D, EPS, ALU.mult, ALU.add).then_inc(rs_done, 1)
                    wait_reg(pool, rs_done, 2 * n + 1)
                    pool.tensor_tensor(rstd[:, t], tmp[:, t], half[:, t], ALU.pow).then_inc(rs_done, 1)
            chunks(pool, body)

        @block.tensor
        def _(pe):
            pe.sem_inc(mm, START)
            for g in range(2):
                for h in range(2):
                    mmi = pe.matmul(psF[:, 1, g, h], cst.ident[0:2, g:g + 1].to_broadcast([2, P]),
                                    cst.gate[:, 512 * h:512 * h + 512], start=True, stop=True)
                mmi.then_inc(gate_mm, 1)

            def body(j, jh, par, last):
                pe.wait_ge(lo_done, j + 1)
                if par:
                    pe.wait_ge(gate_out, 2)
                for t in range(2):
                    for h in range(2):
                        out = psF[:, par, t, h]
                        pe.wait_ge(w_lod, 2 * h + 2)
                        pe.wait_ge(scaled, SC0 + 4 * j + 2 * t + h + 1 - 8)
                        for k in range(KC):
                            tok, col = slice(P * t, P * t + P), slice(512 * h, 512 * h + 512)
                            pe.matmul(out, m_hi[:, par, k, tok], w_hi[:, k, col], start=(k == 0), stop=False)
                            pe.matmul(out, m_hi[:, par, k, tok], w_lo[:, k, col], start=False, stop=False)
                            mmi = pe.matmul(out, m_lo[:, par, k, tok], w_hi[:, k, col], start=False, stop=(k == KC - 1))
                        mmi.then_inc(mm, 1)
            chunks(pe, body)

        @block.scalar
        def _(act):
            for counter in y_out:
                act.sem_inc(counter, DMA_START)

            for c in range(4):
                high_w(act, c)

            def body(j, jh, par, last):
                for t in range(2):
                    n = 2 * j + t
                    wait_reg(act, z_done, 2 * n + 2)
                    act.activation(square[:], z[:, t], ACT.Square, accum_out=ssum[:, t]).then_inc(sq_done, 1)
                    wait_reg(act, sq_done, n + 1)
                for t in range(2):
                    wait_reg(act, y_done, 2 * j + t + 1)
                    y = (io.y_prompt if last else io.y_sample[ds(CH * j, CH)])[P * t:P * t + P]
                    act.dma_start(y, z[:, t]).then_inc(y_out[t], 16)
            chunks(act, body)
            for s in y_out:
                act.wait_ge(s, DMA_START + 16 * NCH)

        @block.vector
        def _(dve):
            dve.sem_inc(scaled, SC0)
            def high(j, jh, par, first=False):
                wait_reg(dve, m_ins[par], 16 * (jh + 1))
                if not first:
                    wait_reg(dve, mm, START + 4 * (j - 1))
                dve.tensor_copy(m_hi[:, par], m_in[:, par]).then_inc(hi_done, 1)

            high(0, 0, 0, True)
            low_w(dve, 0)
            low_w(dve, 1)
            dve.wait_ge(gate_mm, 2)
            for g in range(2):
                dve.tensor_copy(gate_bc[:, g], psF[:, 1, g].rearrange("p h n -> p (h n)")).then_inc(gate_out, 1)
            low_w(dve, 2)
            low_w(dve, 3)
            dve.wait_ge(fg_in, 16)
            dve.wait_ge(gate_out, 2)

            def body(j, jh, par, last):
                if not last:
                    high(j + 1, jh + par, 1 - par)
                g = 0 if last else 1
                wait_reg(dve, x_ins[par], 16 * (jh + 1))
                for t in range(2):
                    wait_reg(dve, y_out[t], DMA_START + 16 * j)
                    for h in range(2):
                        n = 4 * j + 2 * t + h
                        col = slice(512 * h, 512 * h + 512)
                        wait_reg(dve, mm, START + n + 1)
                        dve.tensor_tensor(z[:, t, col], psF[:, par, t, h], gate_bc[:, g, col], ALU.mult).then_inc(scaled, 1)
                        wait_reg(dve, scaled, SC0 + n + 1)
                        dve.tensor_tensor(z[:, t, col], z[:, t, col], x_in[:, par, t, col], ALU.add).then_inc(z_done, 1)
                    wait_reg(dve, rs_done, 4 * j + 2 * t + 2)
                    dve.scalar_tensor_tensor(z[:, t], z[:, t], rstd[:, t], fg[:], ALU.mult, ALU.mult).then_inc(y_done, 1)
            chunks(dve, body)


IN_NAMES = ["x_prompt", "x_sample", "cache_k", "cache_v", "c", "c_ctx", "rms_g", "w_ada", "b_ada", "w_in", "b_in",
            "rel_bias", "dw_w", "dw_b", "ln_g", "ln_b", "w_proj_a", "w_proj_b", "w_out", "final_g"]
OUTS = [("y_prompt", (CTX, D)), ("y_sample", (LAT, D)), ("state_k", (CTX, WA)), ("state_v", (CTX, WA))]


class Arrays:
    pass


def build(nc, io):
    io.proj = nc.dram_tensor("proj", (D_IN, TOK), F32, kind="Internal").ap()
    io.v = nc.dram_tensor("v_tokens", (TOK, WA), F32, kind="Internal").ap()
    io.conv = nc.dram_tensor("conv", (WB, TOK), F32, kind="Internal").ap()
    io.ya = nc.dram_tensor("ya", (WA, TOK), F32, kind="Internal").ap()
    io.m = nc.dram_tensor("merged", (D, TOK), F32, kind="Internal").ap()
    io.table = nc.dram_tensor("shifted_bias", (HEADS, QC, ST), F32, kind="Internal").ap()
    cst = Arrays()
    with ExitStack() as ctx:
        sb = lambda n, s, d=F32: ctx.enter_context(nc.sbuf_tensor(n, s, d))
        cst.ident = sb("ident", [P, P])
        cst.cols = sb("param_cols", [P, R_C])
        cst.taps = sb("taps", [P, 4 * TAPS])
        cst.qbias = sb("q_bias", [P, 4])
        cst.shift, cst.scale = sb("shift", [P, KC, 2]), sb("scale", [P, KC, 2])
        cst.gate = sb("gate_rows_2", [2, D])
        with ExitStack() as c2:
            hT_hi = c2.enter_context(nc.sbuf_tensor("hT_hi", [P, KC, HT_W], F32R))
            hT_lo = c2.enter_context(nc.sbuf_tensor("hT_lo", [P, KC, HT_W], F32R))
            modulation(nc, io, cst, hT_hi, hT_lo)
            with nc.sbuf_tensor("xn_b", [P, 8, D], F32) as xn:
                project(nc, io, cst, hT_hi, hT_lo, GROUP_A, 0, xn)
                project(nc, io, cst, hT_hi, hT_lo, GROUP_B, 1, xn)
        attend(nc, io, cst)
        merge(nc, io, cst)
        finish(nc, io, cst)


def kernel(**inputs):
    import concourse.bacc as bacc
    from concourse.bass_utils import run_bass_kernel_spmd

    nc = bacc.Bacc("TRN2", target_bir_lowering=False, num_devices=1)
    arrays, io = {}, Arrays()
    flat = {"x_prompt": (CTX, D), "x_sample": (LAT, D), "cache_k": (CTX, WA), "cache_v": (CTX, WA), "c": (D,),
            "rms_g": (D,), "w_ada": (D, 3 * D), "b_ada": (3 * D,), "w_in": (D, D_IN), "b_in": (D_IN,),
            "rel_bias": (HEADS, 2 * WIN_R - 1, 2 * WIN_C - 1), "dw_w": (TAPS, WB), "dw_b": (WB,), "ln_g": (WB,),
            "ln_b": (WB,), "w_proj_a": (WA, D), "w_proj_b": (WB, D), "w_out": (D, D)}
    row_mask, col_mask = window_masks()
    consts = {"ident": np.eye(P, dtype=np.float32), "row_mask": row_mask, "col_mask": col_mask}
    given = {n: inputs[n] for n in IN_NAMES}
    given.update(consts)

    aps = {}
    for name, a in given.items():
        a = np.ascontiguousarray(a).reshape(flat.get(name, np.shape(a)))
        arrays[f"in_{name}"] = a
        aps[name] = nc.dram_tensor(f"in_{name}", a.shape, mybir.dt.from_np(a.dtype), kind="ExternalInput").ap()
    for name, shape in OUTS:
        aps[name] = nc.dram_tensor(f"out_{name}", shape, F32, kind="ExternalOutput").ap()
    io.__dict__.update(aps)
    build(nc, io)
    r = run_bass_kernel_spmd(nc, [arrays], core_ids=[0]).results[0]
    y_p, y_s, sk, sv = (r[f"out_{name}"] for name, _ in OUTS)
    return (y_p.reshape(1, CTX, D), y_s.reshape(1, LAT, D), sk.reshape(1, 1, CTX, HEADS, DH),
            sv.reshape(1, 1, CTX, HEADS, DH))
```
